# Optimizing a Trainium2 kernel written in Bass

```python
import math
import jax, jax.numpy as jnp
from jax import lax
import numpy as np

D_MODEL = 1024
BATCH = 1
SEQ = 512
DEPTH = 2
DEC_BATCH = 8
DEC_SEQ = 4
PAST_LEN = 1024
PAGE_SIZE = 128

M_HEADS = 4
M_HEAD_DIM = D_MODEL // 8
M_WIDTH = M_HEADS * M_HEAD_DIM
CONV_WIDTH = 4
M_CHUNK = 64
A_HEAD_DIM = 64
A_HEADS = (D_MODEL // 2) // A_HEAD_DIM
A_KV_HEADS = A_HEADS // 2
A_GROUP = A_HEADS // A_KV_HEADS
A_WIDTH = A_HEADS * A_HEAD_DIM
A_KV_WIDTH = A_KV_HEADS * A_HEAD_DIM
IDX_HEADS = 8
IDX_DIM = 64
TOPK_MAX = 256
Q_BLOCK = 128
ROPE_THETA = 10000.0
D_FF = ((8 * D_MODEL // 3 + 255) // 256) * 256
NORM_EPS = 1e-6
PROJ_SPLITS = (M_WIDTH, M_WIDTH, M_WIDTH, M_WIDTH, M_HEADS, M_HEADS,
               A_WIDTH, A_KV_WIDTH, A_KV_WIDTH, IDX_HEADS * IDX_DIM, IDX_DIM, IDX_HEADS)
D_IN = sum(PROJ_SPLITS)
MIX_WIDTH = M_WIDTH + A_WIDTH

kernel_name = "hybrid_mlstm_dsa_decoder_step"

def rmsnorm(x, g):
    xf = x.astype(jnp.float32)
    y = xf * lax.rsqrt(jnp.mean(xf * xf, axis=-1, keepdims=True) + NORM_EPS)
    return (y * g.astype(jnp.float32)).astype(x.dtype)

def rope(x, pos):
    half = x.shape[-1] // 2
    inv = ROPE_THETA ** (-jnp.arange(half, dtype=jnp.float32) / half)
    ang = pos.astype(jnp.float32)[:, None] * inv[None, :]
    cos = jnp.cos(ang)[None, :, None, :]
    sin = jnp.sin(ang)[None, :, None, :]
    xf = x.astype(jnp.float32)
    x1, x2 = xf[..., :half], xf[..., half:]
    return jnp.concatenate([x1 * cos - x2 * sin, x2 * cos + x1 * sin], axis=-1).astype(x.dtype)

def gather_rows(rows, idx):
    return jax.vmap(lambda r, i: r[i])(rows, idx)

def project(x, g_mix_l, w_in_l):
    p = rmsnorm(x, g_mix_l) @ w_in_l
    parts, start = [], 0
    for width in PROJ_SPLITS:
        parts.append(p[..., start:start + width])
        start += width
    return parts

def causal_conv(u, buf, w):
    T = u.shape[1]
    full = jnp.concatenate([buf, u], axis=1)
    out = full[:, 0:T] * w[0]
    for j in range(1, CONV_WIDTH):
        out = out + full[:, j:j + T] * w[j]
    return out, full[:, -(CONV_WIDTH - 1):]

def mlstm_chunkwise(q, k, v, ig, lf, C0, n0, m0):
    B, T, H, d = q.shape
    L = math.gcd(T, M_CHUNK)
    NC = T // L

    def to_chunks(a):
        a = a.reshape((B, NC, L, H) + a.shape[3:])
        return jnp.moveaxis(a, (1, 3), (0, 2))

    f32 = jnp.float32
    xs = (to_chunks(q.astype(f32)), to_chunks(k.astype(f32)), to_chunks(v.astype(f32)),
          to_chunks(ig.astype(f32)), to_chunks(lf.astype(f32)))
    causal = jnp.tril(jnp.ones((L, L), dtype=bool))

    def step(carry, xc):
        C, n, m = carry
        qb, kb, vb, ib, fb = xc
        b = jnp.cumsum(fb, axis=-1)
        logD = b[..., :, None] - b[..., None, :] + ib[..., None, :]
        logD = jnp.where(causal, logD, -jnp.inf)
        inter = b + m[..., None]
        m_t = jnp.maximum(jnp.max(logD, axis=-1), inter)
        w_inter = jnp.exp(inter - m_t)
        s = jnp.einsum('bhtd,bhsd->bhts', qb, kb) * jnp.exp(logD - m_t[..., None])
        num = (w_inter[..., None] * jnp.einsum('bhvd,bhtd->bhtv', C, qb)
               + jnp.einsum('bhts,bhsv->bhtv', s, vb))
        nq = w_inter * jnp.einsum('bhd,bhtd->bht', n, qb) + jnp.sum(s, axis=-1)
        h = num / jnp.maximum(jnp.abs(nq), jnp.exp(-m_t))[..., None]
        bL = b[..., -1]
        log_w = bL[..., None] - b + ib
        m_new = jnp.maximum(bL + m, jnp.max(log_w, axis=-1))
        decay = jnp.exp(bL + m - m_new)
        wk = jnp.exp(log_w - m_new[..., None])
        C_new = decay[..., None, None] * C + jnp.einsum('bhs,bhsv,bhsd->bhvd', wk, vb, kb)
        n_new = decay[..., None] * n + jnp.einsum('bhs,bhsd->bhd', wk, kb)
        return (C_new, n_new, m_new), h

    (C, n, m), hs = lax.scan(step, (C0.astype(f32), n0.astype(f32), m0.astype(f32)), xs)
    h = jnp.moveaxis(hs, (0, 2), (1, 3)).reshape(B, T, H, d)
    return h, C, n, m

def mlstm_mixer(mq, mk, mv, mo, mi, mf, conv_buf, C0, n0, m0, conv_w_l, b_gate_l, g_mout_l):
    B, T, _ = mq.shape
    qk, new_buf = causal_conv(jnp.concatenate([mq, mk], axis=-1), conv_buf.astype(mq.dtype), conv_w_l)
    qk = jax.nn.silu(qk)
    shp = (B, T, M_HEADS, M_HEAD_DIM)
    q = qk[..., :M_WIDTH].reshape(shp)
    k = qk[..., M_WIDTH:].reshape(shp) * (M_HEAD_DIM ** -0.5)
    v = mv.reshape(shp)
    bg = b_gate_l.astype(jnp.float32)
    ig = mi.astype(jnp.float32) + bg[:M_HEADS]
    lf = jax.nn.log_sigmoid(mf.astype(jnp.float32) + bg[M_HEADS:])
    h, C, n, m = mlstm_chunkwise(q, k, v, ig, lf, C0, n0, m0)
    h = rmsnorm(h, g_mout_l.reshape(M_HEADS, M_HEAD_DIM)).reshape(B, T, M_WIDTH)
    return jax.nn.sigmoid(mo.astype(jnp.float32)) * h, (C, n, m, new_buf)

def attn_inputs(aq, ak, av, iq, ik, pos, g_q_l, g_k_l):
    B, T, _ = aq.shape
    q = rope(rmsnorm(aq.reshape(B, T, A_HEADS, A_HEAD_DIM), g_q_l), pos)
    k = rope(rmsnorm(ak.reshape(B, T, A_KV_HEADS, A_HEAD_DIM), g_k_l), pos)
    v = av.reshape(B, T, A_KV_HEADS, A_HEAD_DIM)
    qi = rope(iq.reshape(B, T, IDX_HEADS, IDX_DIM), pos)
    ki = rope(ik.reshape(B, T, 1, IDX_DIM), pos)[:, :, 0]
    return q, k, v, qi, ki

def indexer_scores(qi, w, ki):
    dots = jnp.einsum('bthd,bsd->bths', qi.astype(jnp.float32), ki.astype(jnp.float32)) * (IDX_DIM ** -0.5)
    return jnp.einsum('bth,bths->bts', w.astype(jnp.float32) * (IDX_HEADS ** -0.5), jax.nn.relu(dots))

def select_keys(qi, w, ki, qpos, key_pos, topk):
    scores = indexer_scores(qi, w, ki)
    visible = key_pos[None, :] <= qpos[:, None]
    scores = jnp.where(visible[None], scores, -jnp.inf)
    _, idx = lax.top_k(scores, topk)
    valid = idx <= qpos[None, :, None]
    return idx, valid

def attend_selected(q, kg, vg, valid):
    B, T = q.shape[:2]
    qg = q.reshape(B, T, A_KV_HEADS, A_GROUP, A_HEAD_DIM).astype(jnp.float32)
    s = jnp.einsum('btkgd,btnkd->btkgn', qg, kg.astype(jnp.float32)) * (A_HEAD_DIM ** -0.5)
    s = jnp.where(valid[:, :, None, None, :], s, -jnp.inf)
    p = jax.nn.softmax(s, axis=-1)
    o = jnp.einsum('btkgn,btnkd->btkgd', p, vg.astype(jnp.float32))
    return o.reshape(B, T, A_WIDTH)

def dsa_prompt(q, k, v, qi, ki, w):
    B, S = q.shape[:2]
    topk = min(TOPK_MAX, S // 4)
    nb = S // Q_BLOCK
    key_pos = jnp.arange(S, dtype=jnp.int32)

    def blocks(a):
        return jnp.moveaxis(a.reshape((B, nb, Q_BLOCK) + a.shape[2:]), 1, 0)

    def one_block(args):
        qb, qib, wb, start = args
        qpos = start + jnp.arange(Q_BLOCK, dtype=jnp.int32)
        idx, valid = select_keys(qib, wb, ki, qpos, key_pos, topk)
        return attend_selected(qb, gather_rows(k, idx), gather_rows(v, idx), valid)

    starts = jnp.arange(nb, dtype=jnp.int32) * Q_BLOCK
    out = lax.map(one_block, (blocks(q), blocks(qi), blocks(w), starts))
    return jnp.moveaxis(out, 0, 1).reshape(B, S, A_WIDTH)

def dsa_sample(q, k, v, qi, ki, w, pos, l, cache_k, cache_v, cache_kidx, page_table):
    B, T = q.shape[:2]
    past = page_table.shape[1] * PAGE_SIZE
    L = past + T
    topk = min(TOPK_MAX, L // 4)
    ki_past = cache_kidx[l, page_table].reshape(B, past, IDX_DIM)
    ki_all = jnp.concatenate([ki_past.astype(ki.dtype), ki], axis=1)
    idx, valid = select_keys(qi, w, ki_all, pos, jnp.arange(L, dtype=jnp.int32), topk)
    in_past = (idx < past)[..., None, None]
    pidx = jnp.minimum(idx, past - 1)
    phys = gather_rows(page_table, pidx // PAGE_SIZE)
    off = pidx % PAGE_SIZE
    nidx = jnp.clip(idx - past, 0, T - 1)
    kg = jnp.where(in_past, cache_k[l, phys, off].astype(k.dtype), gather_rows(k, nidx))
    vg = jnp.where(in_past, cache_v[l, phys, off].astype(v.dtype), gather_rows(v, nidx))
    return attend_selected(q, kg, vg, valid)

def finish_layer(x, m_out, a_out, w_out_l, g_ffn_l, w_gu_l, w_down_l):
    mix = jnp.concatenate([m_out.astype(x.dtype), a_out.astype(x.dtype)], axis=-1)
    x = x + mix @ w_out_l
    g, u = jnp.split(rmsnorm(x, g_ffn_l) @ w_gu_l, 2, axis=-1)
    return x + (jax.nn.silu(g) * u) @ w_down_l

def setup_inputs(seed: int = 0) -> dict:
    key = jax.random.key(seed)
    ks = jax.random.split(key, 24)
    n_pages = PAST_LEN // PAGE_SIZE
    n_used = DEC_BATCH * n_pages
    n_pool = n_used + n_used // 4

    def nrm(k, shape, scale=1.0):
        return scale * jax.random.normal(k, shape, jnp.float32)

    page_table = jax.random.permutation(ks[5], n_pool)[:n_used].reshape(DEC_BATCH, n_pages).astype(jnp.int32)
    b_gate = jnp.concatenate([nrm(ks[13], (DEPTH, M_HEADS), 0.1),
                              3.0 + nrm(ks[14], (DEPTH, M_HEADS), 0.5)], axis=-1)
    return {
        "x_prompt": nrm(ks[0], (BATCH, SEQ, D_MODEL)),
        "x_sample": nrm(ks[1], (DEC_BATCH, DEC_SEQ, D_MODEL)),
        "cache_k": nrm(ks[2], (DEPTH, n_pool, PAGE_SIZE, A_KV_HEADS, A_HEAD_DIM)),
        "cache_v": nrm(ks[3], (DEPTH, n_pool, PAGE_SIZE, A_KV_HEADS, A_HEAD_DIM)),
        "cache_kidx": nrm(ks[4], (DEPTH, n_pool, PAGE_SIZE, IDX_DIM)),
        "page_table": page_table,
        "state_C": nrm(ks[6], (DEPTH, DEC_BATCH, M_HEADS, M_HEAD_DIM, M_HEAD_DIM), 0.1),
        "state_n": nrm(ks[7], (DEPTH, DEC_BATCH, M_HEADS, M_HEAD_DIM), 0.1),
        "state_m": nrm(ks[8], (DEPTH, DEC_BATCH, M_HEADS)),
        "state_conv": nrm(ks[9], (DEPTH, DEC_BATCH, CONV_WIDTH - 1, 2 * M_WIDTH)),
        "g_mix": 1.0 + nrm(ks[10], (DEPTH, D_MODEL), 0.1),
        "w_in": nrm(ks[11], (DEPTH, D_MODEL, D_IN), D_MODEL ** -0.5),
        "conv_w": nrm(ks[12], (DEPTH, CONV_WIDTH, 2 * M_WIDTH), CONV_WIDTH ** -0.5),
        "b_gate": b_gate,
        "g_mout": 1.0 + nrm(ks[15], (DEPTH, M_WIDTH), 0.1),
        "g_q": 1.0 + nrm(ks[16], (DEPTH, A_HEAD_DIM), 0.1),
        "g_k": 1.0 + nrm(ks[17], (DEPTH, A_HEAD_DIM), 0.1),
        "w_out": nrm(ks[18], (DEPTH, MIX_WIDTH, D_MODEL), MIX_WIDTH ** -0.5),
        "g_ffn": 1.0 + nrm(ks[19], (DEPTH, D_MODEL), 0.1),
        "w_gate_up": nrm(ks[20], (DEPTH, D_MODEL, 2 * D_FF), D_MODEL ** -0.5),
        "w_down": nrm(ks[21], (DEPTH, D_FF, D_MODEL), D_FF ** -0.5),
    }

def reference(x_prompt, x_sample, cache_k, cache_v, cache_kidx, page_table, state_C, state_n, state_m,
              state_conv, g_mix, w_in, conv_w, b_gate, g_mout, g_q, g_k, w_out, g_ffn, w_gate_up, w_down):
    B, S, _ = x_prompt.shape
    DB, T, _ = x_sample.shape
    past = page_table.shape[1] * PAGE_SIZE
    pos_p = jnp.arange(S, dtype=jnp.int32)
    pos_s = past + jnp.arange(T, dtype=jnp.int32)
    xp, xs = x_prompt, x_sample
    kp, vp, kip, Cp, Np, Mp, Bp = [], [], [], [], [], [], []
    ks_, vs_, kis, Cs, Ns, Ms, Bs = [], [], [], [], [], [], []
    for l in range(DEPTH):
        mq, mk, mv, mo, mi, mf, aq, ak, av, iq, ik, iw = project(xp, g_mix[l], w_in[l])
        m_out, (C, n, m, buf) = mlstm_mixer(
            mq, mk, mv, mo, mi, mf, jnp.zeros((B, CONV_WIDTH - 1, 2 * M_WIDTH), xp.dtype),
            jnp.zeros((B, M_HEADS, M_HEAD_DIM, M_HEAD_DIM), jnp.float32),
            jnp.zeros((B, M_HEADS, M_HEAD_DIM), jnp.float32), jnp.zeros((B, M_HEADS), jnp.float32),
            conv_w[l], b_gate[l], g_mout[l])
        q, k, v, qi, ki = attn_inputs(aq, ak, av, iq, ik, pos_p, g_q[l], g_k[l])
        a_out = dsa_prompt(q, k, v, qi, ki, iw)
        xp = finish_layer(xp, m_out, a_out, w_out[l], g_ffn[l], w_gate_up[l], w_down[l])
        kp.append(k); vp.append(v); kip.append(ki); Cp.append(C); Np.append(n); Mp.append(m); Bp.append(buf)
        mq, mk, mv, mo, mi, mf, aq, ak, av, iq, ik, iw = project(xs, g_mix[l], w_in[l])
        m_out, (C, n, m, buf) = mlstm_mixer(
            mq, mk, mv, mo, mi, mf, state_conv[l], state_C[l], state_n[l], state_m[l],
            conv_w[l], b_gate[l], g_mout[l])
        q, k, v, qi, ki = attn_inputs(aq, ak, av, iq, ik, pos_s, g_q[l], g_k[l])
        a_out = dsa_sample(q, k, v, qi, ki, iw, pos_s, l, cache_k, cache_v, cache_kidx, page_table)
        xs = finish_layer(xs, m_out, a_out, w_out[l], g_ffn[l], w_gate_up[l], w_down[l])
        ks_.append(k); vs_.append(v); kis.append(ki); Cs.append(C); Ns.append(n); Ms.append(m); Bs.append(buf)
    return (xp, xs,
            jnp.stack(kp), jnp.stack(vp), jnp.stack(kip), jnp.stack(Cp), jnp.stack(Np), jnp.stack(Mp), jnp.stack(Bp),
            jnp.stack(ks_), jnp.stack(vs_), jnp.stack(kis), jnp.stack(Cs), jnp.stack(Ns), jnp.stack(Ms), jnp.stack(Bs))


_drawn_inputs = setup_inputs


def setup_inputs(seed=0):
    import zlib

    import numpy as np

    out = dict(_drawn_inputs(seed))
    spreads = {}
    factors = {'g_q': 2.869}
    for name, (base, spread) in spreads.items():
        noise = np.random.default_rng([zlib.crc32(name.encode()), seed]).standard_normal(out[name].shape)
        drawn = base * np.exp(spread * noise) if base else spread * noise
        out[name] = __import__('jax').numpy.asarray(drawn.astype(out[name].dtype))
    for name, factor in factors.items():
        out[name] = (out[name] * factor).astype(out[name].dtype)
    return out
```

```python
from contextlib import ExitStack

import concourse.bass as bass
from concourse import mybir

F32 = mybir.dt.float32
I32 = mybir.dt.int32
ACT = mybir.ActivationFunctionType
ALU = mybir.AluOpType
AX = mybir.AxisListType

P = 128
D = 1024
KT = D // P
SEQ = 512
DB, DT = 8, 4
NS = DB * DT
T = SEQ + NS
HALF = T // 2
DEPTH = 2
PAGE = 128
PAGES = 8
PAST = PAGE * PAGES
POOL = DB * PAGES * 5 // 4
MH = 4
KVH, QH, IH, HD = 4, 8, 8, 64
DFF = 2816
FT = DFF // P
EPS = 1e-6
NEG = -1e30
GONE = -3e38
KEYS = PAST + NS
TOPK_P, TOPK_S = 128, 256
TILES = [(0, P), (P, P), (2 * P, P), (3 * P, P), (SEQ, NS)]
MQ, MK, MV, MO, MI, AQ, AK, IQ, IK = 0, 512, 1024, 1536, 2048, 2056, 2568, 3080, 3592
D_IN = 3664
SLABS = ([("small", 0, 80)]
         + [("tok", c, 512) for c in (IQ, AQ, AK, MV, MO)]
         + [("conv", MQ, 512), ("conv", MK, 512)]
         + [("out", 0, 512), ("out", 512, 512)] + [("ffn", 256 * j, 256) for j in range(FT // 2)]
         + [("down", P * j, P) for j in range(KT)])
CONV0 = 1 + 5 * 3
OUT0 = CONV0 + 8
FFN0 = OUT0 + 8
DOWN0 = FFN0 + 2 * FT
SLOTS = {"small": 1, "tok": 3, "conv": 4, "out": 4, "ffn": 4, "down": 1}


def slots_before(i):
    return sum(SLOTS[kind] for kind, _, _ in SLABS[:i])


STORES = 2 + DB + 1 + 2
CONST = [("ident", P), ("ones", P), ("cos", 160), ("sin", 160), ("bcm", NS), ("blk", DB), ("rep", 2 * P),
         ("sel", MH * P), ("newpen", NS), ("pen0", P)]
CAT = {}
NCONST = 0
for _name, _n in CONST:
    CAT[_name] = (NCONST, _n)
    NCONST += _n


def build(nc, A, O):
    ctx = ExitStack()
    with ctx:
        def sb(name, cols, rows=P, dt=F32):
            return ctx.enter_context(nc.sbuf_tensor(name, [rows, cols], dt))

        layer_semaphores = []

        def sem(name, layer=True):
            s = ctx.enter_context(nc.semaphore(name))
            if layer:
                layer_semaphores.append(s)
            return s

        s_slab_in_even = sem("slab_in_even")
        s_slab_in_odd = sem("slab_in_odd")
        s_vec_in = sem("vec_in")
        s_out_done = sem("out_done")
        s_kipage_in0 = sem("kipage_in0")
        s_kipage_in1 = sem("kipage_in1")
        s_gate_in = sem("gate_in")
        s_g_in = sem("g_in")
        s_conv_state_turned = sem("conv_state_turned")
        s_kiturn = sem("kiturn")
        s_index_used = sem("index_used")
        s_c0_in = sem("c0_in")
        s_qi_roped = sem("qi_roped")
        s_kv_stored = sem("kv_stored")
        s_out_free = sem("out_free")
        s_qk_ready = sem("qk_ready")
        s_gate_rows_ready = sem("gate_rows_ready")
        s_n0_in = sem("n0_in")
        s_tail_copied = sem("tail_copied")
        s_stored = sem("stored")
        s_c_new = sem("c_new")
        s_n_new = sem("n_new")
        s_c_copied = sem("c_copied")
        s_kt_turned = sem("kt_turned")
        s_kpage_in0 = sem("kpage_in0")
        s_kpage_in1 = sem("kpage_in1")
        s_s_pv = sem("s_pv")
        s_vpage_in0 = sem("vpage_in0")
        s_vpage_in1 = sem("vpage_in1")
        s_hn_ready = sem("hn_ready")
        s_ones_set = sem("ones_set")
        s_scored = sem("scored")
        s_masked = sem("masked")
        s_sd = sem("sd")
        s_sd_masked = sem("sd_masked")
        s_act_chain = sem("act_chain")
        s_conv_z = sem("conv_z")
        s_conv_e = sem("conv_e")
        s_sq1 = sem("sq1")
        s_sum1 = sem("sum1")
        s_rstd1 = sem("rstd1")
        s_gate_read = sem("gate_read")
        s_gate_log = sem("gate_log")
        s_gate_exps = sem("gate_exps")
        s_idx_turned = sem("idx_turned")
        s_idx_copied = sem("idx_copied")
        s_dots = sem("dots")
        s_relu_free = sem("relu_free")
        s_relu_done = sem("relu_done")
        s_sdots = sem("sdots")
        s_kicopy = sem("kicopy")
        s_srelu = sem("srelu")
        s_snew = sem("snew")
        s_qk_sums = sem("qk_sums")
        s_qk_rstd = sem("qk_rstd")
        s_conv_done = sem("conv_done")
        s_tail_turned = sem("tail_turned")
        s_c0_turned = sem("c0_turned")
        s_cq_done = sem("cq_done")
        s_c0_copied = sem("c0_copied")
        s_s_dt = sem("s_dt")
        s_s_de = sem("s_de")
        s_dtmp_ready = sem("dtmp_ready")
        s_dexp = sem("dexp")
        s_c_sum = sem("c_sum")
        s_hsq = sem("hsq")
        s_hrstd = sem("hrstd")
        s_mix_turned = sem("mix_turned")
        s_mix_copied = sem("mix_copied")
        s_qt_turned = sem("qt_turned")
        s_qt_copied = sem("qt_copied")
        s_a_max = sem("a_max")
        s_a_tok = sem("a_tok")
        s_a_p = sem("a_p")
        s_pt_turned = sem("pt_turned")
        s_pv = sem("pv")
        s_pt_copied = sem("pt_copied")
        s_s_log = sem("s_log")
        s_kt_copied = sem("kt_copied")
        s_s_neg = sem("s_neg")
        s_s_exp = sem("s_exp")
        s_s_pt = sem("s_pt")
        s_s_ptc = sem("s_ptc")
        s_sq2 = sem("sq2")
        s_sum2 = sem("sum2")
        s_rstd2 = sem("rstd2")
        s_xn2_ready = sem("xn2_ready")
        s_gate_e = sem("gate_e")
        s_xn_ready = sem("xn_ready")
        s_vec_copied = sem("vec_copied")
        s_gate_turned = sem("gate_turned")
        s_w_spread = sem("w_spread")
        s_gate_cols_turned = sem("gate_cols_turned")
        s_gate_cols_ready = sem("gate_cols_ready")
        s_sscore = sem("sscore")
        s_qk_mem_ready = sem("qk_mem_ready")
        s_ktok_copied = sem("ktok_copied")
        s_ktok_turned = sem("ktok_turned")
        s_s_small = sem("s_small")
        s_cq_copied = sem("cq_copied")
        s_cq_turned = sem("cq_turned")
        s_s_sd = sem("s_sd")
        s_s_num = sem("s_num")
        s_kmask_ready = sem("kmask_ready")
        s_u_sum = sem("u_sum")
        s_s_num_read = sem("s_num_read")
        s_n_sum = sem("n_sum")
        s_negm_bc = sem("negm_bc")
        s_mem_s = sem("mem_s")
        s_num_read = sem("num_read")
        s_num = sem("num")
        s_k_twice_ready = sem("k_twice_ready")
        s_s_turned = sem("s_turned")
        s_s_q_ready = sem("s_q_ready")
        s_a_copied = sem("a_copied")
        s_a_turned = sem("a_turned")
        s_a_s = sem("a_s")
        s_s_logits = sem("s_logits")
        s_s_norm = sem("s_norm")
        s_mix_ready = sem("mix_ready")
        s_dve_chain = sem("dve_chain")
        s_const_in = sem("const_in", layer=False)
        s_x_in = sem("x_in", layer=False)
        s_x_turned = sem("x_turned", layer=False)
        s_x_copied = sem("x_copied", layer=False)
        s_y_turned = sem("y_turned", layer=False)
        s_y_copied = sem("y_copied", layer=False)
        s_y_stored = sem("y_stored", layer=False)

        x = sb("x", KT * T)
        xn = sb("xn", KT * T)
        ring = sb("ring", 2 * 4096)
        proj = sb("proj", 13860)
        rawr = sb("rawr", 3 * 571)
        cq = sb("cq", KT * T)
        qk2 = sb("qk2", 4096)
        kiT = sb("kiT", SEQ)
        pen = sb("pen", 3 * SEQ)
        R4 = sb("R4", 4224)
        pen_s = sb("pen_s", KEYS, NS)
        con = sb("con", NCONST)
        gmout = sb("gmout", 512)
        gqk = sb("gqk", 2 * HD)
        vec = sb("vec", P, 80)
        vT = sb("vT", 80)
        convst = sb("convst", 8 * 24)
        tails = sb("tails", 8 * 27)
        negM = sb("negM", T, MH)
        gcols = sb("gcols", 64)
        small = sb("small", 400)
        tiny = sb("tiny", 64, 8)
        pages = sb("pages", DB * PAGES, 1, I32)
        psum = ctx.enter_context(nc.psum_tensor("psum", [P, 8 * 512], F32))

        def ps(bank, n=1):
            return psum[:, 512 * bank:512 * (bank + n)]

        def const(name, rows=P):
            a, n = CAT[name]
            return con[0:rows, a:a + n]

        ident, ones = const("ident"), const("ones")
        xv = x[:, :].rearrange("p (k t) -> p k t", k=KT)
        xnv = xn[:, :].rearrange("p (k t) -> p k t", k=KT)
        cqv = cq[:, :].rearrange("p (k t) -> p k t", k=KT)
        g80 = proj[:, 0:400].rearrange("p (t c) -> p t c", t=5)
        qi = proj[:, 400:3600].rearrange("p (t h d) -> p t h d", t=5, h=10)
        qk = proj[:, 3600:7440].rearrange("p (t h d) -> p t h d", t=5, h=12)
        va = proj[:, 7440:8720].rearrange("p (t c) -> p t c", t=5)
        mv = proj[:, 8720:11300].rearrange("p (t h c) -> p t h c", t=5, h=MH)
        mo = proj[:, 11300:13860].rearrange("p (t c) -> p t c", t=5)
        hid = proj[:, 0:FT * T].rearrange("p (f t) -> p f t", f=FT)
        htok = proj[:, 400:2960].rearrange("p (t h d) -> p t h d", t=5, h=MH)
        kw = xn[:, 0:2560].rearrange("p (t h d) -> p t h d", t=5, h=MH)
        raw = rawr[:, :].rearrange("p (s c) -> p s c", s=3)
        qiT = qk2[:, 0:2048].rearrange("p (g t) -> p g t", g=4)
        kiTb = qk2[0:HD, 2048:4096].rearrange("p (s c) -> p s c", s=2)
        c0 = qk2[:, :].rearrange("p (b h d) -> p b h d", b=DB, h=MH)
        qT = qk2[:, 0:2048].rearrange("p (g t) -> p g t", g=4)
        kT2 = qk2[:, 2048:4096].rearrange("p (g t) -> p g t", g=4)
        penv = pen[:, :].rearrange("p (j s) -> p j s", j=3)
        gr = cq[0:MH, 0:7 * T].rearrange("p (r t) -> p r t", r=7)
        rm, ra = pen[0:MH, 0:T], pen[0:MH, T:2 * T]
        relu_p = R4[:, 0:1024].rearrange("p (s c) -> p s c", s=2)
        relu_s = R4[:, 0:2 * KEYS].rearrange("p (g c) -> p g c", g=2)
        ki_pages = R4[:, 2400:3424].rearrange("p (s g d) -> p s g d", s=2, g=PAGES)
        wx = R4[0:NS, 3500:3756]
        sd = R4[:, 0:2048].rearrange("p (s t) -> p s t", s=4)
        dtmp = R4[:, 2048:3072].rearrange("p (s t) -> p s t", s=2)
        ct = R4[:, 3072:4096].rearrange("p (s t) -> p s t", s=2)
        kmask = R4[0:NS, 2048:3072]
        wP = small[:, 0:32].rearrange("p (t h) -> p t h", t=4)
        wS = small[:, 32:96].rearrange("p (g c) -> p g c", g=2)
        qiTs = small[0:HD, 96:352].rearrange("p (b c) -> p b c", b=DB)
        kiTs = small[0:HD, 352:384]
        eps = small[:, 392:393]
        m8 = small[:, 384:392]
        mixv = xnv
        tail_rows = xn[0:27, 2560:3584]
        nrow = xn[0:DB, 3584:4096]
        c_end, n_end = R4[:, 3072:3584], R4[0:1, 3584:4096]
        sds = small[0:NS, 0:P].rearrange("p (h t) -> p h t", h=MH)
        cqs, dec_bc = small[:, P:2 * P], small[:, 256:288]
        den = small[:, 288:308].rearrange("p (t h) -> p t h", t=5)
        hss = small[:, 308:328].rearrange("p (t h) -> p t h", t=5)
        a_score = proj[:, 400:1936].rearrange("p (s c) -> p s c", s=3)
        a_pt = proj[:, 1936:2960].rearrange("p (s c) -> p s c", s=2)
        atok = proj[:, 2960:3472]
        a_neg = small[:, 328:336]
        a_sum = small[:, 336:352].rearrange("p (s h) -> p s h", s=2)
        s_max = small[:, 352:355]
        s_q = kiT[:, :].rearrange("p (g b c) -> p g b c", g=2, b=DB)
        kTnew = small[:, 0:64].rearrange("p (g s) -> p g s", g=2)
        k_twice = proj[:, 11300:13348].rearrange("p (t h i d) -> p t h i d", t=4, h=KVH, i=2)
        kTb = proj[:, 8720:10768].rearrange("p (g s) -> p g s", g=2)
        s_prob = proj[:, 10768:11824]
        s_pt = proj[:, 11824:12976].rearrange("p (g c) -> p g c", g=9)
        k_pages = cq[:, 0:4096].rearrange("p (s g c) -> p s g c", s=2, g=PAGES)
        v_pages = R4[:, 0:4096].rearrange("p (s g c) -> p s g c", s=2, g=PAGES)
        small_ss = small[:, 96:156].rearrange("p (t h) -> p t h", t=5)
        m0T = tiny[0:MH, 0:8]
        bgate = tiny[0:MH, 8:10]
        mrow = tiny[0:MH, 46:55]
        winter = tiny[0:MH, 10:42]
        decT = tiny[0:8, 42:46]
        acol = gcols[:, 0:60].rearrange("p (t q h) -> p t q h", t=5, q=3)

        def sig(f):
            return R4[:, T * (1 + f % 2):T * (1 + f % 2) + T].rearrange("p (h t) -> p h t", h=2)

        def slab_view(i):
            kind, _, n = SLABS[i]
            base = 4096 * (i % 2)
            nk = FT if kind == "down" else KT
            cols = 512 if kind == "ffn" else n
            return ring[:, base:base + nk * cols].rearrange("p (k n) -> p k n", k=nk)

        def slab_arrived(eng, i):
            pieces = sum(2 if SLABS[j][0] in ("small", "ffn") else 1 for j in range(i % 2, i + 1, 2))
            eng.wait_ge(s_slab_in_even if i % 2 == 0 else s_slab_in_odd, 16 * pieces)

        def sync_layer(block, l):
            @block.sync
            def _(sp):
                w_in, w_out, w_gu, w_down = (A[n][bass.ds(l, 1), :, :] for n in ("w_in", "w_out", "w_gate_up", "w_down"))
                lay = bass.ds(l, 1)

                sp.dma_start(vec[0:32, :], A["conv_w"][lay, :, :].rearrange("a j (m p) -> (a j m) p", p=P)).then_inc(s_vec_in, 16)
                sp.dma_start(vec[32:40, :], A["g_mix"][lay, :].rearrange("a (k p) -> (a k) p", p=P)).then_inc(s_vec_in, 16)
                sp.dma_start(vec[40:48, :], A["g_ffn"][lay, :].rearrange("a (k p) -> (a k) p", p=P)).then_inc(s_vec_in, 16)
                sp.dma_start(vec[48:80, :], A["state_n"][lay, :, :, :].rearrange("a b h d -> (a b h) d")).then_inc(s_vec_in, 16)
                sp.dma_start(R4[0:24, 3072:4096], A["state_conv"][lay, :, :, :].rearrange("a b j c -> (a b j) c")).then_inc(s_vec_in, 16)

                def load_slab(i):
                    kind, c, n = SLABS[i]
                    sem = s_slab_in_even if i % 2 == 0 else s_slab_in_odd
                    dst = slab_view(i)
                    if i >= 2:
                        sp.wait_ge(s_out_done, slots_before(i - 1))
                    if kind == "small":
                        for a, b, c in ((0, 8, MI), (8, 80, IK)):
                            sp.dma_start(dst[:, :, a:b], w_in[:, :, c:c + b - a].rearrange("a (k p) n -> p (a k) n", p=P)).then_inc(sem, 16)
                    elif kind == "ffn":
                        for a, c in ((0, c), (256, DFF + c)):
                            sp.dma_start(dst[:, :, a:a + 256], w_gu[:, :, c:c + 256].rearrange("a (k p) n -> p (a k) n", p=P)).then_inc(sem, 16)
                    else:
                        w = {"tok": w_in, "conv": w_in, "out": w_out, "down": w_down}[kind]
                        sp.dma_start(dst, w[:, :, c:c + n].rearrange("a (k p) n -> p (a k) n", p=P)).then_inc(sem, 16)

                def page(i):
                    return bass.ds(l * POOL + sp.value_load(pages[0:1, i:i + 1], min_val=0, max_val=POOL - 1), 1)

                def load_index_keys(b):
                    for g in range(PAGES):
                        src = A["cache_kidx"][page(b * PAGES + g), :, :].rearrange("a p d -> p (a d)")
                        sp.dma_start(ki_pages[:, b % 2, g, :], src).then_inc(s_kipage_in0 if b % 2 == 0 else s_kipage_in1, 16)

                load_slab(0)
                load_slab(1)
                sp.dma_start(pen[0:MH, 0:2 * T], A["gate_rows"][:, :]).then_inc(s_gate_in, 16)
                sp.dma_start(m0T, A["state_m"][lay, :, :].rearrange("a b h -> h (a b)"), allow_slow_non_contiguous=True).then_inc(s_gate_in, 16)
                sp.dma_start(bgate[:, 0:1], A["b_gate"][lay, 0:MH].rearrange("a h -> h a"), allow_slow_non_contiguous=True).then_inc(s_gate_in, 16)
                sp.dma_start(bgate[:, 1:2], A["b_gate"][lay, MH:2 * MH].rearrange("a h -> h a"), allow_slow_non_contiguous=True).then_inc(s_gate_in, 16)
                sp.dma_start(gqk[:, 0:HD], A["g_q"][lay, :].partition_broadcast(P).rearrange("p a n -> p (a n)")).then_inc(s_g_in, 16)
                sp.dma_start(gqk[:, HD:2 * HD], A["g_k"][lay, :].partition_broadcast(P).rearrange("p a n -> p (a n)")).then_inc(s_g_in, 16)
                sp.dma_start(gmout[:, :], A["g_mout"][lay, :].partition_broadcast(P).rearrange("p a n -> p (a n)")).then_inc(s_g_in, 16)
                sp.wait_ge(s_conv_state_turned, 1)
                load_index_keys(0)
                load_index_keys(1)
                for i in range(2, 6):
                    load_slab(i)
                for b in range(2, DB):
                    sp.wait_ge(s_kiturn, 2 * b - 2)
                    load_index_keys(b)
                load_slab(6)
                load_slab(7)
                sp.wait_ge(s_index_used, 1)
                for b in range(DB):
                    sp.dma_start(c0[:, b, :, :], A["state_C"][lay, b, :, :, :].rearrange("a h v d -> v (a h) d")).then_inc(s_c0_in, 16)
                load_slab(8)
                load_slab(9)
                sp.wait_ge(s_qi_roped, 1)
                sp.dma_start(O["kidx_p"][lay, 0, :, :].rearrange("a (t p) d -> p (a t) d", p=P), qi[:, 0:4, 8, :]).then_inc(s_kv_stored, 16)
                sp.dma_start(O["kidx_s"][lay, :, :, :].rearrange("a b t d -> (a b t) d"), qi[0:NS, 4, 8, :]).then_inc(s_kv_stored, 16)
                sp.wait_ge(s_out_free, 10)
                sp.dma_start(O["v_p"][lay, 0, :, :, :].rearrange("a (t p) h d -> p (a t) (h d)", p=P), va[:, 0:4, :]).then_inc(s_kv_stored, 16)
                sp.dma_start(O["v_s"][lay, :, :, :, :].rearrange("a b t h d -> (a b t) (h d)"), va[0:NS, 4, :]).then_inc(s_kv_stored, 16)
                sp.wait_ge(s_qk_ready, 1)
                sp.dma_start(O["k_p"][lay, 0, :, :, :].rearrange("a (t p) h d -> p (a t) (h d)", p=P), qk[:, 0:4, 8:12, :].rearrange("p t h d -> p t (h d)")).then_inc(s_kv_stored, 16)
                sp.dma_start(O["k_s"][lay, :, :, :, :].rearrange("a b t h d -> (a b t) (h d)"), qk[0:NS, 4, 8:12, :].rearrange("p h d -> p (h d)")).then_inc(s_kv_stored, 16)
                sp.wait_ge(s_gate_rows_ready, 1)
                sp.dma_start(O["m_p"][lay, 0, :].rearrange("a h -> h a"), mrow[:, 0:1], allow_slow_non_contiguous=True).then_inc(s_kv_stored, 16)
                sp.dma_start(O["m_s"][lay, :, :].rearrange("a b h -> h (a b)"), mrow[:, 1:9], allow_slow_non_contiguous=True).then_inc(s_kv_stored, 16)
                sp.wait_ge(s_out_done, OUT0)
                sp.dma_start(nrow, A["state_n"][lay, :, :, :].rearrange("a b h d -> (a b) (h d)")).then_inc(s_n0_in, 16)
                sp.wait_ge(s_tail_copied, 1)
                sp.dma_start(O["conv_p"][lay, 0, :, :].rearrange("a j c -> (a j) c"), tail_rows[0:3, :]).then_inc(s_stored, 16)
                sp.dma_start(O["conv_s"][lay, :, :, :].rearrange("a b j c -> (a b j) c"), tail_rows[3:27, :]).then_inc(s_stored, 16)
                sp.wait_ge(s_c_new, MH)
                for b in range(DB):
                    sp.dma_start(O["C_s"][lay, b, :, :, :].rearrange("a h v d -> v (a h) d"), c0[:, b, :, :]).then_inc(s_stored, 16)
                sp.wait_ge(s_n_new, 1)
                sp.dma_start(O["n_s"][lay, :, :, :].rearrange("a b h d -> (a b) (h d)"), nrow).then_inc(s_stored, 16)
                sp.wait_ge(s_c_copied, 1)
                sp.dma_start(O["C_p"][lay, 0, :, :, :].rearrange("a h v d -> v (a h) d"), c_end.rearrange("p (h d) -> p h d", h=MH)).then_inc(s_stored, 16)
                sp.dma_start(O["n_p"][lay, 0, :, :].rearrange("a h d -> a (h d)"), n_end).then_inc(s_stored, 16)
                sp.wait_ge(s_stored, 16 * STORES)
                sp.wait_ge(s_kv_stored, 16 * 8)

                def load_pages(name, buf, b, sems):
                    for g in range(PAGES):
                        sp.dma_start(buf[:, b % 2, g, :], A[name][page(b * PAGES + g), :, :].rearrange("a p d -> p (a d)")).then_inc(sems[b % 2], 16)

                def load_keys(b):
                    if b >= 2:
                        sp.wait_ge(s_kt_turned, 4 * (b - 1))
                    load_pages("cache_k", k_pages, b, (s_kpage_in0, s_kpage_in1))

                def load_values(b):
                    if b >= 2:
                        sp.wait_ge(s_s_pv, b - 1)
                    load_pages("cache_v", v_pages, b, (s_vpage_in0, s_vpage_in1))

                sp.wait_ge(s_hn_ready, 1)
                for load, b in [(load_keys, 0), (load_keys, 1), (load_values, 0), (load_values, 1), (load_keys, 2), (load_keys, 3),
                                (load_keys, 4), (load_keys, 5), (load_values, 2), (load_values, 3), (load_values, 4),
                                (load_values, 5), (load_keys, 6), (load_keys, 7), (load_values, 6), (load_values, 7)]:
                    load(b)
                for i in range(10, len(SLABS)):
                    load_slab(i)
        def pool_layer(block, l):
            @block.gpsimd
            def _(pool):
                pool.memset(mv[:, 0:4, :, P:P + 1], 1.0)
                pool.memset(mv[0:NS, 4, :, P:P + 1], 1.0).then_inc(s_ones_set, 1)
                for j in range(3):
                    pool.wait_ge(s_scored, j + 1)
                    blk = penv[:, j, (j + 1) * P:(j + 2) * P]
                    pool.affine_select(out=blk, in_=blk, compare_op=ALU.is_ge, fill=NEG, base=0,
                                       pattern=[[-1, P]], channel_multiplier=1).then_inc(s_masked, 1)
                for n in range(4 * MH):
                    s = n % 4
                    pool.wait_ge(s_sd, n + 1)
                    blk = sd[:, s, P * s:P * s + P]
                    pool.affine_select(out=blk, in_=blk, compare_op=ALU.is_ge, fill=0.0, base=0,
                                       pattern=[[1, P]], channel_multiplier=-1).then_inc(s_sd_masked, 1)
        def act_layer(block, l):
            @block.scalar
            def _(act):
                chain = [0]

                def step(ins):
                    chain[0] += 1
                    ins.then_inc(s_act_chain, 1)
                    act.wait_ge(s_act_chain, chain[0])

                def norm(squares, summed, rstd_ready, out):
                    act.activation(cq[:, :], x[:, :], ACT.Square).then_inc(squares, 1)
                    act.wait_ge(summed, 1)
                    step(act.activation(out, ps(4, 2).rearrange("p (h t) -> p h t", h=2)[:, :, 0:HALF], ACT.Ln,
                                        bias=eps[:, :], scale=1.0 / D))
                    act.activation(out, out, ACT.Exp, scale=-0.5).then_inc(rstd_ready, 1)

                def slot(n):
                    act.wait_ge(s_out_done, n + 1)
                    return ps(2 * (n % 2), 2)

                def token_slab(n, parts, func=ACT.Copy, scale=1.0):
                    for i in range(3):
                        src = slot(n + i).rearrange("p (t c) -> p t c", t=2)
                        for c, m, dst in parts:
                            if i < 2:
                                ins = act.activation(dst[:, 2 * i:2 * i + 2], like(src[:, :, c:c + m], dst, 1), func, scale=scale)
                            else:
                                ins = act.activation(dst[0:NS, 4], like(src[0:NS, 0, c:c + m], dst, 0), func, scale=scale)
                        ins.then_inc(s_out_free, 1)

                def like(src, dst, free):
                    if len(dst.shape) == 3:
                        return src
                    if free:
                        return src.rearrange("p t (h d) -> p t h d", h=dst.shape[2])
                    return src.rearrange("p (h d) -> p h d", h=dst.shape[2])

                def conv_exp(m):
                    act.wait_ge(s_conv_z, m + 1)
                    act.activation(R4[:, T * (m % 2):T * (m % 2) + T], cqv[:, m, :], ACT.Exp, scale=-1.0).then_inc(s_conv_e, 1)

                rstd = R4[:, 0:T].rearrange("p (h t) -> p h t", h=2)
                norm(s_sq1, s_sum1, s_rstd1, rstd)

                src = slot(0)[:, 0:400].rearrange("p (t c) -> p t c", t=5)
                act.activation(g80[:, 0:4, :], src[:, 0:4, :], ACT.Copy)
                act.activation(g80[0:NS, 4, :], src[0:NS, 4, :], ACT.Copy).then_inc(s_out_free, 1)
                token_slab(1, [(0, 512, qi[:, :, 0:8, :])])
                token_slab(4, [(0, 512, qk[:, :, 0:8, :])])

                act.wait_ge(s_gate_read, 1)
                step(act.activation(gr[:, 2, :], gr[:, 1, :], ACT.Abs))
                step(act.activation(gr[:, 2, :], gr[:, 2, :], ACT.Exp, scale=-1.0))
                act.activation(gr[:, 2, :], gr[:, 2, :], ACT.Ln, bias=1.0).then_inc(s_gate_log, 1)
                act.wait_ge(s_gate_rows_ready, 1)
                act.activation(gr[:, 4, :], gr[:, 6, :], ACT.Exp, scale=-1.0)
                act.activation(gr[:, 5, 0:SEQ], gr[:, 0, 0:SEQ], ACT.Exp, bias=negM[:, SEQ - 1:SEQ])
                act.activation(gr[:, 5, SEQ:T], gr[:, 5, SEQ:T], ACT.Exp)
                act.activation(winter, winter, ACT.Exp).then_inc(s_gate_exps, 1)

                for i in range(5):
                    act.wait_ge(s_idx_turned, i + 1)
                    act.activation(qiT[:, i, :] if i < 4 else kiT[:, :], ps(4 + i % 2), ACT.Copy).then_inc(s_idx_copied, 1)
                act.wait_ge(s_idx_turned, 6)
                act.activation(qiTs.rearrange("p b (h t) -> p h b t", h=IH),
                               ps(6)[0:HD, 0:256].rearrange("p (h b t) -> p h b t", h=IH, b=DB), ACT.Copy)
                act.activation(kiTs, ps(6)[0:HD, 256:288], ACT.Copy)
                act.activation(wS, ps(7)[:, 0:64].rearrange("p (g c) -> p g c", g=2), ACT.Copy).then_inc(s_idx_copied, 1)

                token_slab(7, [(0, 256, qk[:, :, 8:12, :]), (256, 256, va)])

                for n in range(3 * IH):
                    j = n // IH + 1
                    act.wait_ge(s_dots, n + 1)
                    if n >= 2:
                        act.wait_ge(s_relu_free, n - 1)
                    act.activation(relu_p[:, n % 2, 0:(j + 1) * P], ps(4 + n % 2)[:, 0:(j + 1) * P], ACT.Relu,
                                   scale=HD ** -0.5).then_inc(s_relu_done, 1)
                token_slab(10, [(0, 512, mv[:, :, :, 0:P])])

                for b in range(DB):
                    for hf in range(2):
                        act.wait_ge(s_kiturn, 2 * b + hf + 1)
                        if b >= 2:
                            act.wait_ge(s_sdots, 2 * (b - 2) + hf + 1)
                        act.activation(kiTb[:, b % 2, 512 * hf:512 * hf + 512], ps(6 + hf)[0:HD, :], ACT.Copy).then_inc(s_kicopy, 1)
                    if b % 4 == 3:
                        act.wait_ge(s_sdots, 2 * b + 2)
                        if b == 3:
                            act.wait_ge(s_relu_free, 3 * IH)
                        act.activation(relu_s[:, b // 4, 0:PAST], ps(4, 2), ACT.Relu, scale=HD ** -0.5).then_inc(s_srelu, 1)
                act.wait_ge(s_snew, 1)
                act.activation(relu_s[:, :, PAST:KEYS], ps(6)[:, 0:64].rearrange("p (g c) -> p g c", g=2), ACT.Relu,
                               scale=HD ** -0.5).then_inc(s_srelu, 1)
                token_slab(13, [(0, 512, mo)], ACT.Exp, -1.0)

                act.wait_ge(s_qk_sums, 1)
                for rows, t in ((P, slice(0, 4)), (NS, slice(4, 5))):
                    step(act.activation(small_ss[0:rows, t, :], small_ss[0:rows, t, :], ACT.Ln, bias=eps[0:rows, :], scale=1.0 / HD))
                    ins = act.activation(small_ss[0:rows, t, :], small_ss[0:rows, t, :], ACT.Exp, scale=-0.5)
                ins.then_inc(s_qk_rstd, 1)

                for m in range(8):
                    src = slot(CONV0 + m).rearrange("p (h t) -> p h t", h=2)
                    if m >= 3:
                        act.wait_ge(s_conv_done, m - 2)
                    act.activation(raw[:, m % 3, 3:3 + HALF], src[:, 0, 0:HALF], ACT.Copy)
                    act.activation(raw[:, m % 3, 3 + HALF:3 + SEQ], src[:, 1, 0:SEQ - HALF], ACT.Copy)
                    act.activation(raw[:, m % 3, 3 + SEQ:571].rearrange("p (b c) -> p b c", b=DB)[:, :, 3:7],
                                   src[:, 1, SEQ - HALF:HALF].rearrange("p (b c) -> p b c", b=DB), ACT.Copy).then_inc(s_out_free, 1)
                    if m >= 1:
                        conv_exp(m - 1)
                conv_exp(7)
                act.wait_ge(s_tail_turned, 1)
                act.activation(tail_rows, ps(0, 2)[0:27, :], ACT.Copy).then_inc(s_tail_copied, 1)
                for g in range(8):
                    act.wait_ge(s_c0_turned, g + 1)
                    if g >= 2:
                        act.wait_ge(s_cq_done, g - 1)
                    act.activation(ct[:, g % 2, :], ps(g % 2), ACT.Copy).then_inc(s_c0_copied, 1)
                act.wait_ge(s_s_dt, 1)
                act.activation(sds.rearrange("p h t -> p (h t)"), sds.rearrange("p h t -> p (h t)"), ACT.Exp).then_inc(s_s_de, 1)
                for n in range(4 * MH):
                    act.wait_ge(s_dtmp_ready, n + 1)
                    d = dtmp[:, n % 2, P * (n % 4):SEQ]
                    act.activation(d, d, ACT.Exp).then_inc(s_dexp, 1)
                act.wait_ge(s_c_sum, 1)
                act.activation(c_end, ps(2), ACT.Copy)
                act.activation(n_end, ps(3)[0:1, :], ACT.Copy).then_inc(s_c_copied, 1)
                act.wait_ge(s_hsq, 1)
                for rows, t in ((P, slice(0, 4)), (NS, slice(4, 5))):
                    step(act.activation(hss[0:rows, t, :], hss[0:rows, t, :], ACT.Ln, bias=eps[0:rows, :], scale=1.0 / P))
                    ins = act.activation(hss[0:rows, t, :], hss[0:rows, t, :], ACT.Exp, scale=-0.5)
                ins.then_inc(s_hrstd, 1)
                for h in range(MH):
                    act.wait_ge(s_mix_turned, h + 1)
                    if h == 0:
                        act.wait_ge(s_c_new, MH)
                        act.wait_ge(s_stored, 16 * STORES)
                    act.activation(mixv[:, h, :], ps(2 * (h % 2), 2)[:, 0:T], ACT.Copy).then_inc(s_mix_copied, 1)

                for g in range(8):
                    act.wait_ge(s_qt_turned, g + 1)
                    act.activation(qT[:, g, :] if g < 4 else kT2[:, g - 4, :], ps(4 + g % 2), ACT.Copy).then_inc(s_qt_copied, 1)
                for n in range(4 * QH + 1):
                    if n < 4 * QH:
                        j, h = n // QH, n % QH
                        w = (j + 1) * P
                        act.wait_ge(s_a_max, n + 1)
                        if h == 0 and j >= 2:
                            act.wait_ge(s_a_tok, j - 1)
                        act.activation(a_score[:, n % 3, 0:w], a_score[:, n % 3, 0:w], ACT.Exp, bias=a_neg[:, n % 4:n % 4 + 1],
                                       scale=HD ** -0.5, accum_out=a_sum[:, j % 2, h:h + 1]).then_inc(s_a_p, 1)
                    if n >= 1:
                        m = n - 1
                        w = (m // QH + 1) * P
                        act.wait_ge(s_pt_turned, m + 1)
                        if m >= 2:
                            act.wait_ge(s_pv, m - 1)
                        act.activation(a_pt[:, m % 2, 0:w], ps(2 + m % 2)[:, 0:w], ACT.Copy).then_inc(s_pt_copied, 1)
                for g in range(2):
                    for b in range(4 * g, 4 * g + 4):
                        for i in range(4):
                            act.wait_ge(s_kt_turned, 4 * b + i + 1)
                            if b >= 1 and i == 0:
                                act.wait_ge(s_s_log, b)
                            act.activation(kTb[:, i // 2, 512 * (i % 2):512 * (i % 2) + 512], ps(3 + i), ACT.Copy).then_inc(s_kt_copied, 1)
                    act.wait_ge(s_s_neg, g + 1)
                    act.activation(s_prob, ps(0, 3)[:, 0:KEYS], ACT.Exp, bias=s_max[:, 0:1], scale=HD ** -0.5,
                                   accum_out=s_max[:, 1:2]).then_inc(s_s_exp, 1)
                    act.wait_ge(s_s_pt, g + 1)
                    act.activation(s_pt[:, 0:8, :].rearrange("p g c -> p (g c)"), ps(3, 2), ACT.Copy)
                    act.activation(s_pt[0:NS, 8, :], ps(5)[0:NS, 0:P], ACT.Copy).then_inc(s_s_ptc, 1)

                act.wait_ge(s_out_free, OUT0 + KT)
                norm(s_sq2, s_sum2, s_rstd2, rstd)
                for f in range(FT):
                    src = slot(FFN0 + 2 * f).rearrange("p (h t) -> p h t", h=2)[:, :, 0:HALF]
                    if f == 0:
                        act.wait_ge(s_xn2_ready, 1)
                    if f >= 2:
                        act.wait_ge(s_out_free, FFN0 + 2 * f - 2)
                    act.activation(sig(f), src, ACT.Exp, scale=-1.0).then_inc(s_gate_e, 1)
        def tensor_layer(block, l):
            @block.tensor
            def _(pe):
                def slot(n):
                    if n >= 2:
                        pe.wait_ge(s_out_free, n - 1)
                    return ps(2 * (n % 2), 2)

                def token_slab(i, n):
                    slab_arrived(pe, i)
                    w = slab_view(i)
                    for s in range(3):
                        out = slot(n + s)
                        for t in range(2 * s, min(2 * s + 2, 5)):
                            c, r = TILES[t]
                            for k in range(KT):
                                mm = pe.matmul(out[0:r, 512 * (t % 2):512 * (t % 2) + 512], xnv[:, k, c:c + r], w[:, k, :],
                                               start=(k == 0), stop=(k == KT - 1))
                        mm.then_inc(s_out_done, 1)

                def feature_tile(i, n, c, src):
                    slab_arrived(pe, i)
                    w = slab_view(i)
                    nk = w.shape[1]
                    out = slot(n)
                    for k in range(nk):
                        for hf in range(2):
                            mm = pe.matmul(out[:, 512 * hf:512 * hf + HALF], w[:, k, c:c + P],
                                           src[:, k, HALF * hf:HALF * hf + HALF], start=(k == 0), stop=(k == nk - 1))
                    mm.then_inc(s_out_done, 1)

                def sum_squares(squares, done):
                    pe.wait_ge(squares, 1)
                    for hf in range(2):
                        for k in range(KT):
                            mm = pe.matmul(ps(4 + hf)[:, 0:HALF], ones, cqv[:, k, HALF * hf:HALF * hf + HALF],
                                           start=(k == 0), stop=(k == KT - 1))
                    mm.then_inc(done, 1)

                pe.wait_ge(s_vec_in, 16 * 5)
                pe.transpose(ps(6)[:, 0:80], vec[0:80, :], ident[0:80, 0:80])
                for m in range(8):
                    mm = pe.transpose(ps(7)[:, 24 * m:24 * m + 24], R4[0:24, 3072 + P * m:3072 + P * m + P], ident[0:24, 0:24])
                mm.then_inc(s_conv_state_turned, 1)
                sum_squares(s_sq1, s_sum1)

                pe.wait_ge(s_xn_ready, 1)
                slab_arrived(pe, 0)
                out = slot(0)
                for t, (c, r) in enumerate(TILES):
                    for k in range(KT):
                        mm = pe.matmul(out[0:r, 80 * t:80 * t + 80], xnv[:, k, c:c + r], slab_view(0)[:, k, :],
                                       start=(k == 0), stop=(k == KT - 1))
                mm.then_inc(s_out_done, 1)
                token_slab(1, 1)
                pe.wait_ge(s_out_free, 1)
                pe.wait_ge(s_rstd1, 1)
                pe.wait_ge(s_vec_copied, 1)
                for q in range(2):
                    for c, r, t in [(c, r, t) for t, (c, r) in enumerate(TILES)]:
                        mm = pe.transpose(ps(4 + 2 * q, 2)[0:MH, c:c + r], g80[0:r, t, MH * q:MH * q + MH], ident[0:r, 0:r])
                mm.then_inc(s_gate_turned, 1)
                token_slab(2, 4)

                pe.wait_ge(s_qi_roped, 1)
                pe.wait_ge(s_gate_read, 1)
                for g in range(5):
                    if g >= 2:
                        pe.wait_ge(s_idx_copied, g - 1)
                    for t in range(4):
                        mm = pe.transpose(ps(4 + g % 2)[:, P * t:P * t + P], qi[:, t, 2 * g:2 * g + 2, :].rearrange("p h d -> p (h d)"), ident)
                    mm.then_inc(s_idx_turned, 1)
                for h in range(IH + 1):
                    pe.transpose(ps(6)[0:HD, NS * h:NS * h + NS], qi[0:NS, 4, h, :], ident[0:NS, 0:NS])
                pe.wait_ge(s_w_spread, 1)
                for g in range(2):
                    mm = pe.transpose(ps(7)[:, NS * g:NS * g + NS], wx[:, P * g:P * g + P], ident[0:NS, 0:NS])
                mm.then_inc(s_idx_turned, 1)
                token_slab(3, 7)

                pe.wait_ge(s_gate_exps, 1)
                pe.wait_ge(s_idx_copied, 6)
                for t, (c, r) in enumerate(TILES):
                    for q, row in enumerate((0, 4, 5)):
                        pe.transpose(ps(6)[0:r, 12 * t + MH * q:12 * t + MH * q + MH], gr[:, row, c:c + r], ident[0:MH, 0:MH])
                pe.transpose(ps(6)[0:NS, 60:64], winter, ident[0:MH, 0:MH])
                pe.transpose(ps(6)[0:DB, 64:68], winter.rearrange("p (b t) -> p b t", b=DB)[:, :, 3], ident[0:MH, 0:MH])\
                  .then_inc(s_gate_cols_turned, 1)

                for n in range(3 * IH):
                    j, h = n // IH + 1, n % IH
                    if n >= 2:
                        pe.wait_ge(s_relu_done, n - 1)
                    q0 = HD * (h % 2)
                    pe.matmul(ps(4 + n % 2)[:, 0:(j + 1) * P], qiT[q0:q0 + HD, h // 2, j * P:(j + 1) * P],
                              kiT[q0:q0 + HD, 0:(j + 1) * P], start=True, stop=True).then_inc(s_dots, 1)
                token_slab(4, 10)

                pe.wait_ge(s_gate_cols_ready, 1)
                pe.wait_ge(s_relu_done, 3 * IH)
                for b in range(DB):
                    if b % 2 == 0:
                        pe.wait_ge(s_kipage_in0, 16 * PAGES * (b // 2 + 1))
                    else:
                        pe.wait_ge(s_kipage_in1, 16 * PAGES * (b // 2 + 1))
                    for hf in range(2):
                        if b >= 1:
                            pe.wait_ge(s_kicopy, 2 * (b - 1) + hf + 1)
                        for g in range(4):
                            mm = pe.transpose(ps(6 + hf)[0:HD, PAGE * g:PAGE * g + PAGE], ki_pages[:, b % 2, 4 * hf + g, :], ident)
                        mm.then_inc(s_kiturn, 1)
                    r0 = NS * (b % 4)
                    if b == 4:
                        pe.wait_ge(s_srelu, 1)
                    for hf in range(2):
                        pe.wait_ge(s_kicopy, 2 * b + hf + 1)
                        pe.matmul(ps(4 + hf)[r0:r0 + NS, :], qiTs[:, b, :], kiTb[:, b % 2, 512 * hf:512 * hf + 512],
                                  start=True, stop=True).then_inc(s_sdots, 1)
                for b in range(DB):
                    r0 = NS * (b % 4)
                    mm = pe.matmul(ps(6)[r0:r0 + NS, NS * (b // 4):NS * (b // 4) + NS], qiTs[:, b, :], kiTs, start=True, stop=True)
                mm.then_inc(s_snew, 1)
                token_slab(5, 13)
                for c, n, dst in ((0, 512, ps(4)), (512, 512, ps(5)), (PAST, NS, ps(7))):
                    pe.wait_ge(s_srelu, 3)
                    for g in range(2):
                        mm = pe.matmul(dst[0:NS, 0:n], wS[:, g, :], relu_s[:, g, c:c + n], start=(g == 0), stop=(g == 1))
                mm.then_inc(s_sscore, 1)

                for m in range(8):
                    feature_tile(6 + m // 4, CONV0 + m, P * (m % 4), xnv)

                pe.wait_ge(s_out_free, OUT0)
                pe.wait_ge(s_conv_done, 8)
                for m in range(8):
                    mm = pe.transpose(ps(0, 2)[0:27, P * m:P * m + P], tails[:, 27 * m:27 * m + 27], ident)
                mm.then_inc(s_tail_turned, 1)
                pe.wait_ge(s_qk_mem_ready, 8)
                for t, (c, r) in enumerate(TILES):
                    if t >= 2:
                        pe.wait_ge(s_ktok_copied, t - 1)
                    for h in range(MH):
                        mm = pe.transpose(ps(2 + t % 2)[0:r, P * h:P * h + P], cqv[:, MH + h, c:c + r], ident)
                    mm.then_inc(s_ktok_turned, 1)
                pe.wait_ge(s_c0_in, 16 * DB)
                pe.wait_ge(s_index_used, 1)
                pe.wait_ge(s_tail_copied, 1)
                s0 = SEQ
                for g in range(9):
                    if g < 8:
                        h, b0 = g // 2, 4 * (g % 2)
                        if g >= 2:
                            pe.wait_ge(s_c0_copied, g - 1)
                        for i in range(4):
                            mm = pe.transpose(ps(g % 2)[:, P * i:P * i + P], c0[:, b0 + i, h, :], ident)
                        mm.then_inc(s_c0_turned, 1)
                    if g >= 1:
                        h, b0 = (g - 1) // 2, 4 * ((g - 1) % 2)
                        pe.wait_ge(s_c0_copied, g)
                        for i in range(4):
                            b = b0 + i
                            mm = pe.matmul(ps(6)[:, NS * h + DT * b:NS * h + DT * b + DT], ct[:, (g - 1) % 2, P * i:P * i + P],
                                           cqv[:, h, s0 + DT * b:s0 + DT * b + DT], start=True, stop=True)
                        mm.then_inc(s_cq_done, 1)
                for h in range(MH):
                    q, k = cqv[:, h, s0:T], cqv[:, MH + h, s0:T]
                    pe.matmul(ps(7)[0:NS, DB * h:DB * h + DB], q, vT[:, 48 + h:80:MH], start=True, stop=True)
                    pe.matmul(ps(4)[0:NS, NS * h:NS * h + NS], k, q, start=True, stop=True)
                    sel = const("sel", MH)[:, P * h:P * h + P]
                    pe.matmul(ps(4)[0:NS, P + NS * h:P + NS * h + NS], sel[:, 0:NS], negM[:, s0:T], start=True, stop=True)
                    mm = pe.matmul(ps(4)[:, 2 * P + DB * h:2 * P + DB * h + DB], sel,
                                   winter.rearrange("p (b t) -> p b t", b=DB)[:, :, 3], start=True, stop=True)
                mm.then_inc(s_s_small, 1)
                pe.wait_ge(s_cq_copied, 1)
                for h in range(MH):
                    mm = pe.transpose(ps(5)[0:NS, P * h:P * h + P], cqs[:, NS * h:NS * h + NS], ident)
                mm.then_inc(s_cq_turned, 1)
                pe.wait_ge(s_s_sd, 1)
                pe.wait_ge(s_ktok_copied, 5)
                pe.wait_ge(s_ones_set, 1)
                for h in range(MH):
                    mm = pe.matmul(ps(2, 2)[0:NS, 256 * h:256 * h + P + 1], sds[:, h, :], mv[0:NS, 4, h, :], start=True, stop=True)
                mm.then_inc(s_s_num, 1)
                for h in range(MH):
                    pe.wait_ge(s_kmask_ready, h + 1)
                    if h >= 1:
                        pe.wait_ge(s_c_new, h)
                    for hf in range(2):
                        mm = pe.matmul(ps(hf), mv[0:NS, 4, h, 0:P], kmask[:, 512 * hf:512 * hf + 512], start=True, stop=True)
                    mm.then_inc(s_u_sum, 1)
                pe.wait_ge(s_s_num_read, 1)
                pe.matmul(ps(5)[0:DB, :], const("blk", NS), kw[0:NS, 4, :, :].rearrange("p h d -> p (h d)"), start=True, stop=True)\
                  .then_inc(s_n_sum, 1)
                pe.wait_ge(s_c_new, MH)
                pe.wait_ge(s_n_new, 1)

                def mem_score(n):
                    h, s = n // 4, n % 4
                    if s == 0:
                        if h >= 2:
                            pe.wait_ge(s_dtmp_ready, 4 * (h - 1))
                        pe.matmul(ps(h % 2), const("sel", MH)[:, P * h:P * h + P], negM[:, 0:SEQ], start=True, stop=True).then_inc(s_negm_bc, 1)
                    if n >= 2:
                        pe.wait_ge(s_sd, n - 1)
                    pe.matmul(ps(2 + n % 2)[:, 0:SEQ - P * s], cqv[:, MH + h, P * s:P * s + P], cqv[:, h, P * s:SEQ],
                              start=True, stop=True).then_inc(s_mem_s, 1)

                mem_score(0)
                mem_score(1)
                for h in range(MH):
                    for n in range(4 * h + 2, min(4 * h + 6, 4 * MH)):
                        mem_score(n)
                    pe.wait_ge(s_sd_masked, 4 * (h + 1))
                    if h >= 2:
                        pe.wait_ge(s_num_read, h - 1)
                    for t in range(4):
                        for s in range(t + 1):
                            mm = pe.matmul(ps(4 + 2 * (h % 2), 2)[:, 256 * t:256 * t + P + 1], sd[:, s, P * t:P * t + P],
                                           mv[:, s, h, :], start=(s == 0), stop=(s == t))
                    mm.then_inc(s_num, 1)
                pe.wait_ge(s_sd, 4 * MH)
                for h in range(MH):
                    for s in range(4):
                        pe.matmul(ps(2)[:, P * h:P * h + P], mv[:, s, h, 0:P], kw[:, s, h, :], start=(s == 0), stop=(s == 3))
                for s in range(4):
                    mm = pe.matmul(ps(3)[0:1, :], ones[:, 0:1], kw[:, s, :, :].rearrange("p h d -> p (h d)"), start=(s == 0), stop=(s == 3))
                mm.then_inc(s_c_sum, 1)
                pe.wait_ge(s_hn_ready, 1)
                pe.wait_ge(s_c_copied, 1)
                for h in range(MH):
                    if h >= 2:
                        pe.wait_ge(s_mix_copied, h - 1)
                    for t, (c, r) in enumerate(TILES):
                        mm = pe.transpose(ps(2 * (h % 2), 2)[:, c:c + r], htok[0:r, t, h, :], ident[0:r, 0:r])
                    mm.then_inc(s_mix_turned, 1)

                pe.wait_ge(s_num_read, MH)
                for g in range(8):
                    if g >= 2:
                        pe.wait_ge(s_qt_copied, g - 1)
                    if g == 4:
                        pe.wait_ge(s_k_twice_ready, 1)
                    for t in range(4):
                        src = qk[:, t, 2 * g:2 * g + 2, :] if g < 4 else k_twice[:, t, g - 4, :, :]
                        mm = pe.transpose(ps(4 + g % 2)[:, P * t:P * t + P], src.rearrange("p h d -> p (h d)"), ident)
                    mm.then_inc(s_qt_turned, 1)
                for i in range(4):
                    pe.transpose(ps(6)[:, NS * i:NS * i + NS], qk[0:NS, 4, 2 * i:2 * i + 2, :].rearrange("p h d -> p (h d)"), ident[0:NS, 0:NS])
                for p in range(2):
                    mm = pe.transpose(ps(7)[:, NS * p:NS * p + NS], qk[0:NS, 4, 8 + 2 * p:10 + 2 * p, :].rearrange("p h d -> p (h d)"), ident[0:NS, 0:NS])
                mm.then_inc(s_s_turned, 1)
                pe.wait_ge(s_qt_copied, 8)
                pe.wait_ge(s_mix_copied, MH)
                pe.wait_ge(s_s_q_ready, 1)

                def turn_out(j):
                    pe.wait_ge(s_a_tok, j + 1)
                    if j >= 1:
                        pe.wait_ge(s_a_copied, j)
                    for f in range(4):
                        mm = pe.transpose(ps(6)[:, P * f:P * f + P], atok[:, P * f:P * f + P], ident)
                    mm.then_inc(s_a_turned, 1)

                for n in range(4 * QH + 2):
                    if n < 4 * QH:
                        j, h = n // QH, n % QH
                        q0 = HD * (h % 2)
                        if n >= 2:
                            pe.wait_ge(s_a_max, n - 1)
                        pe.matmul(ps(n % 2)[:, 0:(j + 1) * P], qT[q0:q0 + HD, h // 2, P * j:P * j + P],
                                  kT2[q0:q0 + HD, h // 2, 0:(j + 1) * P], start=True, stop=True).then_inc(s_a_s, 1)
                    if 1 <= n <= 4 * QH:
                        m = n - 1
                        pe.wait_ge(s_a_p, m + 1)
                        if m >= 2:
                            pe.wait_ge(s_pt_copied, m - 1)
                        for s in range(m // QH + 1):
                            mm = pe.transpose(ps(2 + m % 2)[:, P * s:P * s + P], a_score[:, m % 3, P * s:P * s + P], ident)
                        mm.then_inc(s_pt_turned, 1)
                    if n >= 2:
                        m = n - 2
                        j, h = m // QH, m % QH
                        pe.wait_ge(s_pt_copied, m + 1)
                        if h == 0 and j >= 2:
                            pe.wait_ge(s_a_tok, j - 1)
                        for s in range(j + 1):
                            mm = pe.matmul(ps(4 + j % 2)[:, HD * h:HD * h + HD], a_pt[:, m % 2, P * s:P * s + P],
                                           va[:, s, HD * (h // 2):HD * (h // 2) + HD], start=(s == 0), stop=(s == j))
                        mm.then_inc(s_pv, 1)
                        if h == 4 and j >= 1:
                            turn_out(j - 1)
                turn_out(3)

                pe.wait_ge(s_a_copied, 4)
                for g in range(2):
                    if g == 1:
                        pe.wait_ge(s_s_exp, 1)
                    for b in range(4 * g, 4 * g + 4):
                        r0 = NS * (b % 4)
                        pe.wait_ge(s_kpage_in0 if b % 2 == 0 else s_kpage_in1, 16 * PAGES * (b // 2 + 1))
                        for i in range(4):
                            if b >= 1:
                                pe.wait_ge(s_kt_copied, 4 * (b - 1) + i + 1)
                            if b == 4 and i == 0:
                                pe.wait_ge(s_s_ptc, 1)
                            for q in range(4):
                                pg = 4 * (i % 2) + q
                                mm = pe.transpose(ps(3 + i)[:, P * q:P * q + P], k_pages[:, b % 2, pg, P * (i // 2):P * (i // 2) + P], ident)
                            mm.then_inc(s_kt_turned, 1)
                        pe.wait_ge(s_kt_copied, 4 * b + 4)
                        for hf in range(3):
                            w = 512 if hf < 2 else NS
                            for p in range(2):
                                rhs = kTb[:, p, 512 * hf:512 * hf + 512] if hf < 2 else kTnew[:, p, :]
                                mm = pe.matmul(ps(hf)[r0:r0 + NS, 0:w], s_q[:, p, b, :], rhs, start=(p == 0), stop=False,
                                               skip_group_check=True)
                        mm.then_inc(s_s_log, 1)
                    for hf in range(3):
                        w = 512 if hf < 2 else NS
                        mm = pe.matmul(ps(hf)[:, 0:w], const("rep", NS)[:, P * g:P * g + P], pen_s[:, 512 * hf:512 * hf + w],
                                       start=False, stop=True, skip_group_check=True)
                    mm.then_inc(s_s_logits, 1)
                    pe.wait_ge(s_s_norm, g + 1)
                    for i in range(9):
                        w = P if i < 8 else NS
                        mm = pe.transpose(ps(3, 3)[0:w, P * i:P * i + P], s_prob[:, P * i:P * i + w], ident)
                    mm.then_inc(s_s_pt, 1)
                    pe.wait_ge(s_s_ptc, g + 1)
                    for b in range(4 * g, 4 * g + 4):
                        r0 = NS * (b % 4)
                        pe.wait_ge(s_vpage_in0 if b % 2 == 0 else s_vpage_in1, 16 * PAGES * (b // 2 + 1))
                        for p in range(2):
                            out = ps(7)[:, NS * (2 * b + p):NS * (2 * b + p) + NS]
                            for pg in range(PAGES):
                                pe.matmul(out, v_pages[:, b % 2, pg, P * p:P * p + P], s_pt[:, pg, r0:r0 + NS], start=(pg == 0), stop=False)
                            mm = pe.matmul(out, va[0:NS, 4, P * p:P * p + P], s_pt[0:NS, 8, r0:r0 + NS], start=False, stop=True)
                        mm.then_inc(s_s_pv, 1)

                pe.wait_ge(s_mix_ready, 1)
                for m in range(8):
                    feature_tile(8 + m // 4, OUT0 + m, P * (m % 4), mixv)
                sum_squares(s_sq2, s_sum2)
                pe.wait_ge(s_xn2_ready, 1)
                for f in range(FT):
                    feature_tile(10 + f // 2, FFN0 + 2 * f, P * (f % 2), xnv)
                    feature_tile(10 + f // 2, FFN0 + 2 * f + 1, 2 * P + P * (f % 2), xnv)
                pe.wait_ge(s_out_free, DOWN0)
                for m in range(KT):
                    feature_tile(10 + FT // 2 + m, DOWN0 + m, 0, hid)
        def vector_layer(block, l):
            @block.vector
            def _(dve):
                chain = [0]

                def step(ins):
                    chain[0] += 1
                    ins.then_inc(s_dve_chain, 1)
                    dve.wait_ge(s_dve_chain, chain[0])

                def spread(ap, shape, at):
                    return ap.unsqueeze(at).broadcast_to(shape)

                dve.wait_ge(s_conv_state_turned, 1)
                dve.tensor_copy(convst[:, :], ps(7)[:, 0:192])
                dve.tensor_copy(vT[:, :], ps(6)[:, 0:80]).then_inc(s_vec_copied, 1)
                dve.wait_ge(s_vec_copied, 1)

                def apply_norm(rstd, g0, ready):
                    for k in range(KT):
                        ins = dve.scalar_tensor_tensor(out=xnv[:, k, :], in0=xv[:, k, :], scalar=vT[:, g0 + k:g0 + k + 1],
                                                       in1=rstd, op0=ALU.mult, op1=ALU.mult)
                    ins.then_inc(ready, 1)

                rstd = R4[:, 0:T]
                dve.wait_ge(s_rstd1, 1)
                apply_norm(rstd, 32, s_xn_ready)

                dve.wait_ge(s_out_free, 1)
                dve.tensor_copy(qi[:, 0:4, 8, :], g80[:, 0:4, 8:72])
                dve.tensor_copy(qi[0:NS, 4, 8, :], g80[0:NS, 4, 8:72])
                dve.tensor_scalar(wP, g80[:, 0:4, 72:80], IH ** -0.5, None, ALU.mult)
                step(dve.tensor_scalar(g80[0:NS, 4, 72:80], g80[0:NS, 4, 72:80], IH ** -0.5, None, ALU.mult))
                dve.tensor_tensor(wx.rearrange("p (b h t) -> p b h t", b=DB, h=IH),
                                  const("rep", NS).rearrange("p (b h t) -> p b h t", b=DB, h=IH),
                                  g80[0:NS, 4, 72:80].unsqueeze(1).unsqueeze(3).broadcast_to([NS, DB, IH, DT]),
                                  ALU.mult).then_inc(s_w_spread, 1)

                def rope(buf, h0, nh, tmp):
                    for tiles, r in ((slice(0, 4), P), (slice(4, 5), NS)):
                        nt = 4 if r == P else 1
                        a = buf[0:r, tiles, h0:h0 + nh, 0:32]
                        b = buf[0:r, tiles, h0:h0 + nh, 32:64]
                        cos, sin = (const(n, r).rearrange("p (t d) -> p t d", t=5)[:, tiles, :].unsqueeze(2).broadcast_to([r, nt, nh, 32])
                                    for n in ("cos", "sin"))
                        n = nt * nh * 32
                        as_, bs = (tmp[0:r, i * n:(i + 1) * n].rearrange("p (t h d) -> p t h d", t=nt, h=nh) for i in range(2))
                        dve.tensor_tensor(as_, a, sin, ALU.mult)
                        step(dve.tensor_tensor(bs, b, sin, ALU.mult))
                        dve.tensor_tensor(a, a, cos, ALU.mult)
                        step(dve.tensor_tensor(b, b, cos, ALU.mult))
                        dve.tensor_tensor(a, a, bs, ALU.subtract)
                        step(dve.tensor_tensor(b, b, as_, ALU.add))

                dve.wait_ge(s_out_free, 4)
                rope(qi, 0, 9, R4)
                dve.tensor_copy(qi[:, 0:4, 9, :], qi[:, 0:4, 8, :]).then_inc(s_qi_roped, 1)

                dve.wait_ge(s_gate_turned, 1)
                dve.wait_ge(s_gate_in, 16 * 4)
                dve.tensor_scalar(gr[:, 0, :], ps(4, 2)[0:MH, 0:T], bgate[:, 0:1], None, ALU.add)
                dve.tensor_scalar(gr[:, 1, :], ps(6, 2)[0:MH, 0:T], bgate[:, 1:2], None, ALU.add).then_inc(s_gate_read, 1)
                dve.wait_ge(s_gate_read, 1)
                dve.wait_ge(s_gate_log, 1)
                step(dve.scalar_tensor_tensor(out=gr[:, 1, :], in0=gr[:, 1, :], scalar=0.0, in1=gr[:, 2, :],
                                              op0=ALU.min, op1=ALU.subtract))
                step(dve.tensor_tensor_scan(gr[:, 2, :], rm, gr[:, 1, :], 0.0, ALU.mult, ALU.add))
                step(dve.tensor_tensor(gr[:, 0, :], gr[:, 0, :], gr[:, 2, :], ALU.subtract))
                step(dve.tensor_copy(gr[:, 1, :], gr[:, 0, :]))

                def seqs(row):
                    return row[:, SEQ:T].rearrange("p (b t) -> p b t", b=DB)

                first = seqs(gr[:, 1, :])[:, :, 0]
                step(dve.tensor_tensor(first, first, m0T, ALU.max))
                step(dve.tensor_tensor_scan(gr[:, 3, :], ra, gr[:, 1, :], 0.0, ALU.add, ALU.max))
                dve.tensor_tensor(gr[:, 6, :], gr[:, 2, :], gr[:, 3, :], ALU.add)
                step(dve.tensor_scalar(negM[:, :], gr[:, 3, :], -1.0, None, ALU.mult))
                dve.tensor_copy(mrow[:, 0:1], gr[:, 6, SEQ - 1:SEQ])
                dve.tensor_copy(mrow[:, 1:9], seqs(gr[:, 6, :])[:, :, 3])
                dve.tensor_tensor(winter.rearrange("p (b t) -> p b t", b=DB), seqs(negM[:, :]),
                                  m0T.unsqueeze(2).broadcast_to([MH, DB, DT]), ALU.add)
                dve.tensor_tensor(seqs(gr[:, 5, :]), seqs(gr[:, 0, :]),
                                  seqs(negM[:, :])[:, :, 3].unsqueeze(2).broadcast_to([MH, DB, DT]), ALU.add).then_inc(s_gate_rows_ready, 1)
                dve.wait_ge(s_gate_cols_turned, 1)
                dve.tensor_copy(gcols[:, 0:48], ps(6)[:, 0:48])
                dve.tensor_copy(gcols[0:NS, 48:64], ps(6)[0:NS, 48:64])
                dve.tensor_copy(decT, ps(6)[0:DB, 64:68]).then_inc(s_gate_cols_ready, 1)

                for n in range(3 * IH):
                    j, h = n // IH + 1, n % IH
                    dve.wait_ge(s_relu_done, n + 1)
                    acc = penv[:, j - 1, 0:(j + 1) * P]
                    part = relu_p[:, n % 2, 0:(j + 1) * P]
                    if h == 0:
                        ins = dve.tensor_scalar(acc, part, wP[:, j, h:h + 1], None, ALU.mult)
                    else:
                        ins = dve.scalar_tensor_tensor(out=acc, in0=part, scalar=wP[:, j, h:h + 1], in1=acc, op0=ALU.mult, op1=ALU.add)
                    ins.then_inc(s_relu_free, 1)
                    dve.wait_ge(s_relu_free, n + 1)
                    if h == IH - 1:
                        dve.sem_inc(s_scored, 1)

                def pick(scores, rows, topk):
                    for _ in range(topk // 8):
                        step(dve.max(m8[0:rows, :], scores))
                        step(dve.match_replace(scores, m8[0:rows, :], scores, GONE))
                    step(dve.tensor_scalar(scores, scores, GONE / 2, NEG, ALU.is_gt, ALU.mult))

                for j in (1, 2, 3):
                    dve.wait_ge(s_masked, j)
                    pick(penv[:, j - 1, 0:(j + 1) * P], P, TOPK_P)

                dve.wait_ge(s_sscore, 1)
                dve.tensor_copy(pen_s[:, 0:PAST], ps(4, 2)[0:NS, :])
                step(dve.tensor_tensor(pen_s[:, PAST:KEYS], ps(7)[0:NS, 0:NS], const("newpen", NS), ALU.add))
                pick(pen_s[:, :], NS, TOPK_S)
                dve.sem_inc(s_index_used, 1)

                dve.wait_ge(s_out_free, 10)
                dve.wait_ge(s_g_in, 16 * 3)
                for t, (_, r) in enumerate(TILES):
                    sq = R4[0:r, 0:768].rearrange("p (h d) -> p h d", h=12)
                    step(dve.tensor_tensor(sq, qk[0:r, t, :, :], qk[0:r, t, :, :], ALU.mult))
                    ins = dve.tensor_reduce(small_ss[0:r, t, :], sq, AX.X, ALU.add)
                    step(ins)
                dve.sem_inc(s_qk_sums, 1)
                dve.wait_ge(s_qk_rstd, 1)
                for t, (_, r) in enumerate(TILES):
                    step(dve.tensor_tensor(qk[0:r, t, :, :], qk[0:r, t, :, :],
                                           small_ss[0:r, t, :].unsqueeze(2).broadcast_to([r, 12, HD]), ALU.mult))
                    dve.tensor_tensor(qk[0:r, t, 0:8, :], qk[0:r, t, 0:8, :],
                                      gqk[0:r, 0:HD].unsqueeze(1).broadcast_to([r, 8, HD]), ALU.mult)
                    step(dve.tensor_tensor(qk[0:r, t, 8:12, :], qk[0:r, t, 8:12, :],
                                           gqk[0:r, HD:2 * HD].unsqueeze(1).broadcast_to([r, 4, HD]), ALU.mult))
                rope(qk, 0, 8, R4)
                rope(qk, 8, 4, R4)
                dve.sem_inc(s_qk_ready, 1)

                for m in range(8):
                    r_ = raw[:, m % 3, :]
                    hist = r_[:, 3 + SEQ:571].rearrange("p (b c) -> p b c", b=DB)
                    step(dve.tensor_copy(hist[:, :, 0:3], convst[:, 24 * m:24 * m + 24].rearrange("p (b j) -> p b j", b=DB)))
                    dve.wait_ge(s_out_free, CONV0 + m + 1)
                    for j in range(4):
                        w = vT[:, 8 * j + m:8 * j + m + 1]
                        for out, src in ((cqv[:, m, 0:SEQ], r_[:, j:j + SEQ]), (seqs(cqv[:, m, :]), hist[:, :, j:j + DT])):
                            if j == 0:
                                ins = dve.tensor_scalar(out, src, w, None, ALU.mult)
                            else:
                                ins = dve.scalar_tensor_tensor(out=out, in0=src, scalar=w, in1=out, op0=ALU.mult, op1=ALU.add)
                        if j < 3:
                            step(ins)
                    ins.then_inc(s_conv_z, 1)
                    dve.tensor_copy(tails[:, 27 * m:27 * m + 3], r_[:, SEQ:SEQ + 3])
                    dve.tensor_copy(tails[:, 27 * m + 3:27 * m + 27].rearrange("p (b j) -> p b j", b=DB), hist[:, :, 4:7]).then_inc(s_conv_done, 1)
                    e = R4[:, T * (m % 2):T * (m % 2) + T]
                    dve.wait_ge(s_conv_e, m + 1)
                    step(dve.tensor_scalar(e, e, 1.0, None, ALU.add))
                    step(dve.reciprocal(e, e))
                    ins = dve.scalar_tensor_tensor(out=cqv[:, m, :], in0=cqv[:, m, :], scalar=1.0 if m < 4 else P ** -0.5, in1=e,
                                                   op0=ALU.mult, op1=ALU.mult)
                    ins.then_inc(s_qk_mem_ready, 1)

                def columns(t, rows, q):
                    return acol[0:rows, t, q, :]

                for t, (_, r) in enumerate(TILES):
                    dve.wait_ge(s_ktok_turned, t + 1)
                    if t == 0:
                        dve.wait_ge(s_out_done, OUT0)
                    dve.tensor_tensor(kw[0:r, t, :, :], ps(2 + t % 2)[0:r, :].rearrange("p (h d) -> p h d", h=MH),
                                      columns(t, r, 2).unsqueeze(2).broadcast_to([r, MH, P]), ALU.mult).then_inc(s_ktok_copied, 1)
                dve.wait_ge(s_s_small, 1)
                for h in range(MH):
                    ins = dve.tensor_scalar(sds[:, h, :], ps(4)[0:NS, P + NS * h:P + NS * h + NS], acol[0:NS, 4, 0, h:h + 1], 0.0, ALU.add, ALU.min)
                ins.then_inc(s_s_dt, 1)
                dve.tensor_copy(dec_bc, ps(4)[:, 2 * P:2 * P + NS])
                dve.wait_ge(s_cq_done, 8)
                dve.tensor_copy(cqs, ps(6)[:, 0:P]).then_inc(s_cq_copied, 1)
                dve.wait_ge(s_s_de, 1)
                step(dve.tensor_tensor(sds, sds, ps(4)[0:NS, 0:P].rearrange("p (h t) -> p h t", h=MH), ALU.mult))
                dve.tensor_tensor(sds, sds, const("bcm", NS).unsqueeze(1).broadcast_to([NS, MH, NS]), ALU.mult).then_inc(s_s_sd, 1)
                wi = gcols[0:NS, 60:64]
                nqm = R4[0:NS, 0:NS].rearrange("p (h b) -> p h b", h=MH)
                step(dve.tensor_tensor(nqm, ps(7)[0:NS, 0:NS].rearrange("p (h b) -> p h b", h=MH),
                                       const("blk", NS).unsqueeze(1).broadcast_to([NS, MH, DB]), ALU.mult))
                step(dve.tensor_reduce(den[0:NS, 4, :], nqm, AX.X, ALU.add))
                step(dve.tensor_tensor(den[0:NS, 4, :], den[0:NS, 4, :], wi, ALU.mult))
                dve.wait_ge(s_cq_turned, 1)
                dve.wait_ge(s_kv_stored, 16 * 8)
                step(dve.tensor_tensor(htok[0:NS, 4, :, :], ps(5)[0:NS, :].rearrange("p (h d) -> p h d", h=MH),
                                       wi.unsqueeze(2).broadcast_to([NS, MH, P]), ALU.mult))
                dve.wait_ge(s_s_num, 1)
                num_s = ps(2, 2)[0:NS, :].rearrange("p (h c) -> p h c", h=MH)
                step(dve.tensor_tensor(den[0:NS, 4, :], den[0:NS, 4, :], num_s[:, :, P], ALU.add))
                dve.tensor_tensor(htok[0:NS, 4, :, :], htok[0:NS, 4, :, :], num_s[:, :, 0:P], ALU.add).then_inc(s_s_num_read, 1)
                for h in range(MH):
                    if h >= 1:
                        dve.wait_ge(s_u_sum, h)
                    dve.tensor_tensor(kmask.rearrange("p (b d) -> p b d", b=DB), kw[0:NS, 4, h, :].unsqueeze(1).broadcast_to([NS, DB, P]),
                                      const("blk", NS).unsqueeze(2).broadcast_to([NS, DB, P]), ALU.mult).then_inc(s_kmask_ready, 1)
                    step(dve.tensor_tensor(c0[:, :, h, :], c0[:, :, h, :], dec_bc[:, DB * h:DB * h + DB].unsqueeze(2).broadcast_to([P, DB, P]), ALU.mult))
                    dve.wait_ge(s_u_sum, h + 1)
                    dve.tensor_tensor(c0[:, :, h, :], c0[:, :, h, :], ps(0, 2).rearrange("p (b d) -> p b d", b=DB), ALU.add).then_inc(s_c_new, 1)
                dve.wait_ge(s_n0_in, 16)
                nr = nrow.rearrange("p (h d) -> p h d", h=MH)
                step(dve.tensor_tensor(nr, nr, decT.unsqueeze(2).broadcast_to([DB, MH, P]), ALU.mult))
                dve.wait_ge(s_n_sum, 1)
                dve.tensor_tensor(nr, nr, ps(5)[0:DB, :].rearrange("p (h d) -> p h d", h=MH), ALU.add).then_inc(s_n_new, 1)

                def decays(n):
                    h, s = n // 4, n % 4
                    dve.wait_ge(s_negm_bc, h + 1)
                    if n >= 2:
                        dve.wait_ge(s_sd, n - 1)
                    dve.tensor_scalar(dtmp[:, n % 2, P * s:SEQ], ps(h % 2)[:, P * s:SEQ], acol[:, s, 0, h:h + 1], 0.0,
                                      ALU.add, ALU.min).then_inc(s_dtmp_ready, 1)

                def values(h):
                    dve.wait_ge(s_num, h + 1)
                    out = ps(4 + 2 * (h % 2), 2).rearrange("p (t c) -> p t c", t=4)
                    d, nq = den[:, 0:4, h], out[:, :, P]
                    step(dve.tensor_copy(d, nq))
                    step(dve.scalar_tensor_tensor(out=d, in0=d, scalar=-1.0, in1=nq, op0=ALU.mult, op1=ALU.max))
                    step(dve.tensor_tensor(d, d, acol[:, 0:4, 1, h], ALU.max))
                    step(dve.reciprocal(d, d))
                    dve.tensor_tensor(htok[:, 0:4, h, :], out[:, :, 0:P], d.unsqueeze(2).broadcast_to([P, 4, P]), ALU.mult).then_inc(s_num_read, 1)

                decays(0)
                for n in range(4 * MH):
                    h, s = n // 4, n % 4
                    if n + 1 < 4 * MH:
                        decays(n + 1)
                    dve.wait_ge(s_dexp, n + 1)
                    dve.wait_ge(s_mem_s, n + 1)
                    if s == 0 and h >= 1:
                        dve.wait_ge(s_num, h)
                    dve.tensor_tensor(sd[:, s, P * s:SEQ], dtmp[:, n % 2, P * s:SEQ], ps(2 + n % 2)[:, 0:SEQ - P * s], ALU.mult).then_inc(s_sd, 1)
                    if s == 1 and h >= 1:
                        values(h - 1)
                values(MH - 1)
                d = den[0:NS, 4, :]
                neg = small[0:NS, 356:360]
                step(dve.tensor_scalar(neg, d, -1.0, None, ALU.mult))
                step(dve.tensor_tensor(d, d, neg, ALU.max))
                step(dve.tensor_tensor(d, d, columns(4, NS, 1), ALU.max))
                step(dve.reciprocal(d, d))
                step(dve.tensor_tensor(htok[0:NS, 4, :, :], htok[0:NS, 4, :, :], d.unsqueeze(2).broadcast_to([NS, MH, P]), ALU.mult))
                for t, (_, r) in enumerate(TILES):
                    s = R4[0:r, 0:512].rearrange("p (h d) -> p h d", h=MH)
                    step(dve.tensor_tensor(s, htok[0:r, t, :, :], htok[0:r, t, :, :], ALU.mult))
                    ins = dve.tensor_reduce(hss[0:r, t, :], s, AX.X, ALU.add)
                    if t == 4:
                        ins.then_inc(s_hsq, 1)
                        dve.wait_ge(s_hsq, 1)
                    else:
                        step(ins)
                    step(dve.tensor_scalar(mo[0:r, t, :], mo[0:r, t, :], 1.0, None, ALU.add))
                    step(dve.reciprocal(mo[0:r, t, :], mo[0:r, t, :]))
                    step(dve.tensor_tensor(mo[0:r, t, :], mo[0:r, t, :], gmout[0:r, :], ALU.mult))
                dve.wait_ge(s_hrstd, 1)
                for t, (_, r) in enumerate(TILES):
                    step(dve.tensor_tensor(htok[0:r, t, :, :], htok[0:r, t, :, :], hss[0:r, t, :].unsqueeze(2).broadcast_to([r, MH, P]), ALU.mult))
                    ins = dve.tensor_tensor(htok[0:r, t, :, :].rearrange("p h d -> p (h d)"), htok[0:r, t, :, :].rearrange("p h d -> p (h d)"), mo[0:r, t, :], ALU.mult)
                    if t == 4:
                        ins.then_inc(s_hn_ready, 1)
                    else:
                        step(ins)

                for i in range(2):
                    ins = dve.tensor_copy(k_twice[:, :, :, i, :], qk[:, 0:4, 8:12, :])
                ins.then_inc(s_k_twice_ready, 1)
                dve.wait_ge(s_s_turned, 1)
                step(dve.memset(kiT[:, :], 0.0))
                for h in range(QH):
                    r0, src, p = HD * (h // 2 % 2), HD * (h % 2), h // 4
                    dve.tensor_copy(s_q[r0:r0 + HD, p, :, DT * h:DT * h + DT],
                                    ps(6)[src:src + HD, NS * (h // 2):NS * (h // 2) + NS].rearrange("p (b t) -> p b t", b=DB))
                dve.tensor_copy(kTnew.rearrange("p g s -> p (g s)"), ps(7)[:, 0:2 * NS]).then_inc(s_s_q_ready, 1)
                dve.wait_ge(s_mix_turned, MH)

                def copy_out(j):
                    dve.wait_ge(s_a_turned, j + 1)
                    dve.tensor_copy(mixv[:, 4:8, P * j:P * j + P], ps(6).rearrange("p (f t) -> p f t", f=4)).then_inc(s_a_copied, 1)

                for n in range(4 * QH + 1):
                    if n < 4 * QH:
                        j, h = n // QH, n % QH
                        w = (j + 1) * P
                        dve.wait_ge(s_a_s, n + 1)
                        if n >= 3:
                            dve.wait_ge(s_pt_turned, n - 2)
                        mask = const("pen0") if j == 0 else penv[:, j - 1, 0:w]
                        step(dve.tensor_tensor_reduce(a_score[:, n % 3, 0:w], ps(n % 2)[:, 0:w], mask, 1.0, GONE, ALU.add, ALU.max,
                                                      a_neg[:, 4 + n % 4:5 + n % 4]))
                        dve.tensor_scalar(a_neg[:, n % 4:n % 4 + 1], a_neg[:, 4 + n % 4:5 + n % 4], -HD ** -0.5, None, ALU.mult)\
                           .then_inc(s_a_max, 1)
                    if n >= QH and n % QH == 2 or n == 4 * QH:
                        j = n // QH - 1
                        dve.wait_ge(s_pv, QH * (j + 1))
                        dve.wait_ge(s_a_p, QH * (j + 1))
                        step(dve.reciprocal(a_sum[:, j % 2, :], a_sum[:, j % 2, :]))
                        if j >= 1:
                            dve.wait_ge(s_a_turned, j)
                        dve.tensor_tensor(atok.rearrange("p (h d) -> p h d", h=QH), ps(4 + j % 2).rearrange("p (h d) -> p h d", h=QH),
                                          a_sum[:, j % 2, :].unsqueeze(2).broadcast_to([P, QH, HD]), ALU.mult).then_inc(s_a_tok, 1)
                        if j >= 1:
                            copy_out(j - 1)
                copy_out(3)
                for g in range(2):
                    dve.wait_ge(s_s_logits, g + 1)
                    step(dve.tensor_reduce(s_max[:, 2:3], ps(0, 3)[:, 0:KEYS], AX.X, ALU.max))
                    dve.tensor_scalar(s_max[:, 0:1], s_max[:, 2:3], -HD ** -0.5, None, ALU.mult).then_inc(s_s_neg, 1)
                    dve.wait_ge(s_s_exp, g + 1)
                    step(dve.reciprocal(s_max[:, 1:2], s_max[:, 1:2]))
                    dve.tensor_scalar(s_prob, s_prob, s_max[:, 1:2], None, ALU.mult).then_inc(s_s_norm, 1)
                dve.wait_ge(s_s_pv, DB)
                for h in range(QH):
                    p, src, dst = h // 4, HD * (h // 2 % 2), HD * (h % 2)
                    ins = dve.tensor_copy(seqs(mixv[dst:dst + HD, 4 + h // 2, :]),
                                          ps(7)[src:src + HD, :].rearrange("p (b g c) -> p b g c", b=DB, g=2)[:, :, p, DT * h:DT * h + DT])
                ins.then_inc(s_mix_ready, 1)

                def halves(n):
                    dve.wait_ge(s_out_done, n + 1)
                    return ps(2 * (n % 2), 2).rearrange("p (h t) -> p h t", h=2)[:, :, 0:HALF]

                for m in range(KT):
                    v = xv[:, m, :].rearrange("p (h t) -> p h t", h=2)
                    dve.tensor_tensor(v, v, halves(OUT0 + m), ALU.add).then_inc(s_out_free, 1)
                dve.wait_ge(s_out_free, OUT0 + KT)
                dve.wait_ge(s_rstd2, 1)
                apply_norm(R4[:, 0:T], 40, s_xn2_ready)
                dve.wait_ge(s_xn2_ready, 1)
                for f in range(FT):
                    e = sig(f)
                    dve.wait_ge(s_gate_e, f + 1)
                    step(dve.tensor_scalar(e, e, 1.0, None, ALU.add))
                    step(dve.reciprocal(e, e))
                    dve.tensor_tensor(e, e, halves(FFN0 + 2 * f), ALU.mult).then_inc(s_out_free, 1)
                    dve.wait_ge(s_out_free, FFN0 + 2 * f + 1)
                    dve.tensor_tensor(hid[:, f, :].rearrange("p (h t) -> p h t", h=2), e, halves(FFN0 + 2 * f + 1), ALU.mult).then_inc(s_out_free, 1)
                dve.wait_ge(s_out_free, DOWN0)
                for m in range(KT):
                    v = xv[:, m, :].rearrange("p (h t) -> p h t", h=2)
                    dve.tensor_tensor(v, v, halves(DOWN0 + m), ALU.add).then_inc(s_out_free, 1)
                dve.wait_ge(s_out_free, DOWN0 + KT)
        xtok = proj[:, 0:5 * D].rearrange("p (t d) -> p t d", t=5)
        with nc.Block() as block:

            @block.sync
            def _(sp):
                sp.dma_start(con[:, :], A["consts"][:, :]).then_inc(s_const_in, 16)
                sp.dma_start(xtok[:, 0:4, :], A["x_prompt"][0, :, :].rearrange("(t p) d -> p t d", p=P)).then_inc(s_x_in, 16)
                sp.dma_start(xtok[0:NS, 4, :], A["x_sample"][:, :, :].rearrange("b t d -> (b t) d")).then_inc(s_x_in, 16)
                sp.dma_start(pages[:, :], A["page_table"][:, :].rearrange("(a b) g -> a (b g)", a=1)).then_inc(s_x_in, 16)

            @block.tensor
            def _(pe):
                pe.wait_ge(s_const_in, 16)
                pe.wait_ge(s_x_in, 48)
                for k in range(KT):
                    if k >= 4:
                        pe.wait_ge(s_x_copied, k - 3)
                    for t, (c, r) in enumerate(TILES):
                        mm = pe.transpose(ps(2 * (k % 4), 2)[:, c:c + r], xtok[0:r, t, P * k:P * k + P], ident[0:r, 0:r])
                    mm.then_inc(s_x_turned, 1)

            @block.vector
            def _(dve):
                dve.memset(eps[:, :], EPS)
                dve.memset(raw[:, :, 0:3], 0.0)
                for k in range(KT):
                    dve.wait_ge(s_x_turned, k + 1)
                    dve.tensor_copy(xv[:, k, :], ps(2 * (k % 4), 2)[:, 0:T]).then_inc(s_x_copied, 1)
                dve.wait_ge(s_x_copied, KT)

        with nc.Fori(0, DEPTH) as l:
            with nc.Block() as layer:
                sync_layer(layer, l)
                pool_layer(layer, l)
                act_layer(layer, l)
                tensor_layer(layer, l)
                vector_layer(layer, l)
            nc.all_engine_barrier()
            for s in layer_semaphores:
                nc.sync.sem_clear(s)
            nc.all_engine_barrier()

        with nc.Block() as block:
            @block.tensor
            def _(pe):
                for t, (c, r) in enumerate(TILES):
                    if t >= 4:
                        pe.wait_ge(s_y_copied, t - 3)
                    for k in range(KT):
                        mm = pe.transpose(ps(2 * (t % 4), 2)[0:r, P * k:P * k + P], xv[:, k, c:c + r], ident)
                    mm.then_inc(s_y_turned, 1)

            @block.vector
            def _(dve):
                for t, (c, r) in enumerate(TILES):
                    dve.wait_ge(s_y_turned, t + 1)
                    dve.tensor_copy(xtok[0:r, t, :], ps(2 * (t % 4), 2)[0:r, :]).then_inc(s_y_copied, 1)

            @block.sync
            def _(sp):
                for t, (c, r) in enumerate(TILES):
                    sp.wait_ge(s_y_copied, t + 1)
                    dst = O["y_p"][0, c:c + r, :] if t < 4 else O["y_s"][:, :, :].rearrange("b t d -> (b t) d")
                    sp.dma_start(dst, xtok[0:r, t, :]).then_inc(s_y_stored, 16)
                sp.wait_ge(s_y_stored, 16 * 5)

_OUTS = [("y_p", (1, SEQ, D)), ("y_s", (DB, DT, D)),
         ("k_p", (DEPTH, 1, SEQ, KVH, HD)), ("v_p", (DEPTH, 1, SEQ, KVH, HD)), ("kidx_p", (DEPTH, 1, SEQ, HD)),
         ("C_p", (DEPTH, 1, MH, P, P)), ("n_p", (DEPTH, 1, MH, P)), ("m_p", (DEPTH, 1, MH)), ("conv_p", (DEPTH, 1, 3, 1024)),
         ("k_s", (DEPTH, DB, DT, KVH, HD)), ("v_s", (DEPTH, DB, DT, KVH, HD)), ("kidx_s", (DEPTH, DB, DT, HD)),
         ("C_s", (DEPTH, DB, MH, P, P)), ("n_s", (DEPTH, DB, MH, P)), ("m_s", (DEPTH, DB, MH)), ("conv_s", (DEPTH, DB, 3, 1024))]
_INS = ["x_prompt", "x_sample", "cache_k", "cache_v", "cache_kidx", "page_table", "state_C", "state_n", "state_m", "state_conv",
        "g_mix", "w_in", "conv_w", "b_gate", "g_mout", "g_q", "g_k", "w_out", "g_ffn", "w_gate_up", "w_down"]


def _constants():
    import numpy as np
    c = np.zeros((P, NCONST), np.float32)

    def put(name, value):
        a, n = CAT[name]
        c[:value.shape[0], a:a + n] = value.reshape(value.shape[0], n)

    put("ident", np.eye(P))
    put("ones", np.ones((P, P)))
    half = HD // 2
    inv = np.float32(10000.0) ** (-np.arange(half, dtype=np.float32) / np.float32(half))
    pos = np.concatenate([np.arange(SEQ), np.tile(PAST + np.arange(DT), DB), np.zeros(P - NS)]).astype(np.float32)
    ang = (pos[:, None] * inv[None, :]).astype(np.float32)
    tiles = ang.reshape(5, P, half).transpose(1, 0, 2)
    put("cos", np.cos(tiles))
    put("sin", np.sin(tiles))
    row = np.arange(NS)
    same = row[:, None] // DT == row[None, :] // DT
    put("bcm", (same & (row[:, None] <= row[None, :])).astype(np.float32))
    put("newpen", np.where(same & (row[None, :] <= row[:, None]), 0.0, NEG))
    put("blk", (row[:, None] // DT == np.arange(DB)[None, :]).astype(np.float32))
    wide = np.arange(2 * P)
    put("rep", ((wide[None, :] // NS == row[:, None] // DT) & (wide[None, :] % DT == row[:, None] % DT)).astype(np.float32))
    put("sel", (np.arange(MH)[:, None] == np.arange(MH * P)[None, :] // P).astype(np.float32))
    put("pen0", np.where(np.arange(P)[None, :] <= np.arange(P)[:, None], 0.0, NEG))
    rows = np.zeros((MH, 2 * T), np.float32)
    rows[:, 0:T] = 1.0
    rows[:, SEQ:T:DT] = 0.0
    rows[:, T + SEQ::DT] = GONE
    return c, rows


def kernel(**inputs):
    import numpy as np
    import concourse.bacc as bacc
    from concourse.bass_utils import run_bass_kernel_spmd

    nc = bacc.Bacc("TRN2", target_bir_lowering=False, num_devices=1)
    data = {n: np.ascontiguousarray(inputs[n]) for n in _INS}
    for n in ("cache_k", "cache_v"):
        data[n] = data[n].reshape(DEPTH * POOL, PAGE, KVH * HD)
    data["cache_kidx"] = data["cache_kidx"].reshape(DEPTH * POOL, PAGE, HD)
    data["consts"], data["gate_rows"] = _constants()
    arrays, A, O = {}, {}, {}
    for n, a in data.items():
        arrays[f"in_{n}_dram"] = a
        A[n] = nc.dram_tensor(f"in_{n}_dram", a.shape, mybir.dt.from_np(a.dtype), kind="ExternalInput").ap()
    for n, shape in _OUTS:
        O[n] = nc.dram_tensor(f"out_{n}_dram", shape, F32, kind="ExternalOutput").ap()
    build(nc, A, O)
    r = run_bass_kernel_spmd(nc, [arrays], core_ids=[0])
    return tuple(r.results[0][f"out_{n}_dram"] for n, _ in _OUTS)
```

```python
from contextlib import ExitStack

import concourse.bass as bass
from concourse import mybir

F32 = mybir.dt.float32
I32 = mybir.dt.int32
ACT = mybir.ActivationFunctionType
ALU = mybir.AluOpType
AX = mybir.AxisListType

P = 128
D = 1024
KT = D // P
SEQ = 512
DB, DT = 8, 4
NS = DB * DT
T = SEQ + NS
HALF = T // 2
DEPTH = 2
PAGE = 128
PAGES = 8
PAST = PAGE * PAGES
POOL = DB * PAGES * 5 // 4
MH = 4
KVH, QH, IH, HD = 4, 8, 8, 64
DFF = 2816
FT = DFF // P
EPS = 1e-6
NEG = -1e30
GONE = -3e38
KEYS = PAST + NS
TOPK_P, TOPK_S = 128, 256
TILES = [(0, P), (P, P), (2 * P, P), (3 * P, P), (SEQ, NS)]
MQ, MK, MV, MO, MI, AQ, AK, IQ, IK = 0, 512, 1024, 1536, 2048, 2056, 2568, 3080, 3592
D_IN = 3664
SLABS = ([("small", 0, 80)]
         + [("tok", c, 512) for c in (IQ, AQ, AK, MV, MO)]
         + [("conv", MQ, 512), ("conv", MK, 512)]
         + [("out", 0, 512), ("out", 512, 512)] + [("ffn", 256 * j, 256) for j in range(FT // 2)]
         + [("down", P * j, P) for j in range(KT)])
CONV0 = 1 + 5 * 3
OUT0 = CONV0 + 8
FFN0 = OUT0 + 8
DOWN0 = FFN0 + 2 * FT
SLOTS = {"small": 1, "tok": 3, "conv": 4, "out": 4, "ffn": 4, "down": 1}


def slots_before(i):
    return sum(SLOTS[kind] for kind, _, _ in SLABS[:i])


STORES = 2 + DB + 1 + 2
CONST = [("ident", P), ("ones", P), ("cos", 160), ("sin", 160), ("bcm", NS), ("blk", DB), ("rep", 2 * P),
         ("sel", MH * P), ("newpen", NS), ("pen0", P)]
CAT = {}
NCONST = 0
for _name, _n in CONST:
    CAT[_name] = (NCONST, _n)
    NCONST += _n


def build(nc, A, O):
    ctx = ExitStack()
    with ctx:
        def sb(name, cols, rows=P, dt=F32):
            return ctx.enter_context(nc.sbuf_tensor(name, [rows, cols], dt))

        layer_semaphores = []

        def sem(name, layer=True):
            s = ctx.enter_context(nc.semaphore(name))
            if layer:
                layer_semaphores.append(s)
            return s

        s_kpage_in0 = sem("kpage_in0")
        s_kpage_in1 = sem("kpage_in1")
        s_kpage_in2 = sem("kpage_in2")
        s_kpage_in3 = sem("kpage_in3")
        s_vpage_in0 = sem("vpage_in0")
        s_vpage_in1 = sem("vpage_in1")
        s_vpage_in2 = sem("vpage_in2")
        s_vpage_in3 = sem("vpage_in3")
        s_vpage_in4 = sem("vpage_in4")
        s_vpage_in5 = sem("vpage_in5")
        s_vpage_in6 = sem("vpage_in6")
        s_vpage_in7 = sem("vpage_in7")
        s_slab_in_even = sem("slab_in_even")
        s_slab_in_odd = sem("slab_in_odd")
        s_vec_in = sem("vec_in")
        s_out_done = sem("out_done")
        s_kipage_in0 = sem("kipage_in0")
        s_kipage_in1 = sem("kipage_in1")
        s_gate_in = sem("gate_in")
        s_g_in = sem("g_in")
        s_conv_state_turned = sem("conv_state_turned")
        s_kiturn = sem("kiturn")
        s_sscore = sem("sscore")
        s_c0_in = sem("c0_in")
        s_qi_roped = sem("qi_roped")
        s_kv_stored = sem("kv_stored")
        s_out_free = sem("out_free")
        s_qk_ready = sem("qk_ready")
        s_gate_rows_ready = sem("gate_rows_ready")
        s_n0_in = sem("n0_in")
        s_tail_copied = sem("tail_copied")
        s_stored = sem("stored")
        s_c_new = sem("c_new")
        s_n_new = sem("n_new")
        s_c_copied = sem("c_copied")
        s_hn_ready = sem("hn_ready")
        s_kt_turned = sem("kt_turned")
        s_s_pv = sem("s_pv")
        s_ones_set = sem("ones_set")
        s_scored = sem("scored")
        s_masked = sem("masked")
        s_raw_zeroed = sem("raw_zeroed")
        s_conv_silu = sem("conv_silu")
        s_k_scaled = sem("k_scaled")
        s_kmask_ready = sem("kmask_ready")
        s_ktok_copied = sem("ktok_copied")
        s_dec_copied = sem("dec_copied")
        s_cq_done = sem("cq_done")
        s_c_decayed = sem("c_decayed")
        s_u_sum = sem("u_sum")
        s_sd = sem("sd")
        s_sd_masked = sem("sd_masked")
        s_act_chain = sem("act_chain")
        s_sq2 = sem("sq2")
        s_conv_z = sem("conv_z")
        s_sq1 = sem("sq1")
        s_sum1 = sem("sum1")
        s_rstd1 = sem("rstd1")
        s_gate_read = sem("gate_read")
        s_gate_log = sem("gate_log")
        s_gate_exps = sem("gate_exps")
        s_idx_turned = sem("idx_turned")
        s_idx_copied = sem("idx_copied")
        s_dots = sem("dots")
        s_relu_free = sem("relu_free")
        s_relu_done = sem("relu_done")
        s_sdots = sem("sdots")
        s_kicopy = sem("kicopy")
        s_srelu = sem("srelu")
        s_snew = sem("snew")
        s_qk_sums = sem("qk_sums")
        s_qk_rstd = sem("qk_rstd")
        s_tail_turned = sem("tail_turned")
        s_c0_turned = sem("c0_turned")
        s_c0_copied = sem("c0_copied")
        s_s_dt = sem("s_dt")
        s_s_de = sem("s_de")
        s_dtmp_ready = sem("dtmp_ready")
        s_dexp = sem("dexp")
        s_c_sum = sem("c_sum")
        s_hsq = sem("hsq")
        s_hrstd = sem("hrstd")
        s_mix_turned = sem("mix_turned")
        s_mix_copied = sem("mix_copied")
        s_qt_turned = sem("qt_turned")
        s_qt_copied = sem("qt_copied")
        s_a_max = sem("a_max")
        s_a_tok = sem("a_tok")
        s_a_p = sem("a_p")
        s_pt_turned = sem("pt_turned")
        s_pv = sem("pv")
        s_pt_copied = sem("pt_copied")
        s_s_log = sem("s_log")
        s_kt_copied = sem("kt_copied")
        s_s_neg = sem("s_neg")
        s_s_exp = sem("s_exp")
        s_s_pt = sem("s_pt")
        s_s_ptc = sem("s_ptc")
        s_sum2 = sem("sum2")
        s_rstd2 = sem("rstd2")
        s_xn2_ready = sem("xn2_ready")
        s_up_free = sem("up_free")
        s_gate_silu = sem("gate_silu")
        s_xn_ready = sem("xn_ready")
        s_vec_copied = sem("vec_copied")
        s_gate_turned = sem("gate_turned")
        s_w_spread = sem("w_spread")
        s_gate_cols_turned = sem("gate_cols_turned")
        s_gate_cols_ready = sem("gate_cols_ready")
        s_conv_done = sem("conv_done")
        s_ktok_turned = sem("ktok_turned")
        s_sscore_copied = sem("sscore_copied")
        s_s_small = sem("s_small")
        s_cq_copied = sem("cq_copied")
        s_cq_turned = sem("cq_turned")
        s_s_sd = sem("s_sd")
        s_s_num = sem("s_num")
        s_s_num_read = sem("s_num_read")
        s_n_sum = sem("n_sum")
        s_negm_bc = sem("negm_bc")
        s_mem_s = sem("mem_s")
        s_num_read = sem("num_read")
        s_num = sem("num")
        s_k_twice_ready = sem("k_twice_ready")
        s_s_turned = sem("s_turned")
        s_s_q_ready = sem("s_q_ready")
        s_a_copied = sem("a_copied")
        s_a_turned = sem("a_turned")
        s_a_s = sem("a_s")
        s_sample_mask = sem("sample_mask")
        s_s_logits = sem("s_logits")
        s_s_norm = sem("s_norm")
        s_mix_ready = sem("mix_ready")
        s_dve_chain = sem("dve_chain")
        s_const_in = sem("const_in", layer=False)
        s_x_in = sem("x_in", layer=False)
        s_x_turned = sem("x_turned", layer=False)
        s_x_copied = sem("x_copied", layer=False)
        s_y_turned = sem("y_turned", layer=False)
        s_y_copied = sem("y_copied", layer=False)
        s_y_stored = sem("y_stored", layer=False)

        x = sb("x", KT * T)
        xn = sb("xn", KT * T)
        ring = sb("ring", 2 * 4096)
        proj = sb("proj", 13860)
        rawr = sb("rawr", 3 * 571)
        cq = sb("cq", KT * T)
        qk2 = sb("qk2", 4096)
        kiT = sb("kiT", SEQ)
        pen = sb("pen", 3 * SEQ)
        R4 = sb("R4", 4224)
        pen_s = sb("pen_s", KEYS, NS)
        con = sb("con", NCONST)
        gmout = sb("gmout", 512)
        gqk = sb("gqk", 2 * HD)
        vec = sb("vec", P, 80)
        vT = sb("vT", 80)
        convst = sb("convst", 8 * 24)
        tails = sb("tails", 8 * 27)
        negM = sb("negM", T, MH)
        gcols = sb("gcols", 64)
        small = sb("small", 400)
        tiny = sb("tiny", 64, 8)
        pages = sb("pages", DB * PAGES, 1, I32)
        psum = ctx.enter_context(nc.psum_tensor("psum", [P, 8 * 512], F32))

        def ps(bank, n=1):
            return psum[:, 512 * bank:512 * (bank + n)]

        def const(name, rows=P):
            a, n = CAT[name]
            return con[0:rows, a:a + n]

        ident, ones = const("ident"), const("ones")
        xv = x[:, :].rearrange("p (k t) -> p k t", k=KT)
        xnv = xn[:, :].rearrange("p (k t) -> p k t", k=KT)
        cqv = cq[:, :].rearrange("p (k t) -> p k t", k=KT)
        g80 = proj[:, 0:400].rearrange("p (t c) -> p t c", t=5)
        qi = proj[:, 400:3600].rearrange("p (t h d) -> p t h d", t=5, h=10)
        qk = proj[:, 3600:7440].rearrange("p (t h d) -> p t h d", t=5, h=12)
        va = proj[:, 7440:8720].rearrange("p (t c) -> p t c", t=5)
        mv = proj[:, 8720:11300].rearrange("p (t h c) -> p t h c", t=5, h=MH)
        mo = proj[:, 11300:13860].rearrange("p (t c) -> p t c", t=5)
        hid = proj[:, 0:FT * T].rearrange("p (f t) -> p f t", f=FT)
        htok = proj[:, 400:2960].rearrange("p (t h d) -> p t h d", t=5, h=MH)
        kw = xn[:, 0:2560].rearrange("p (t h d) -> p t h d", t=5, h=MH)
        raw = [rawr[:, 571 * m:571 * m + 571] if m < 3 else R4[:, 1369 + 571 * (m - 3):1369 + 571 * (m - 2)] for m in range(8)]
        qiT = qk2[:, 0:2048].rearrange("p (g t) -> p g t", g=4)
        kiTb = qk2[0:HD, 2048:4096].rearrange("p (s c) -> p s c", s=2)
        c0 = qk2[:, :].rearrange("p (b h d) -> p b h d", b=DB, h=MH)
        qT = qk2[:, 0:2048].rearrange("p (g t) -> p g t", g=4)
        kT2 = qk2[:, 2048:4096].rearrange("p (g t) -> p g t", g=4)
        penv = pen[:, :].rearrange("p (j s) -> p j s", j=3)
        gr = cq[0:MH, 0:7 * T].rearrange("p (r t) -> p r t", r=7)
        rm, ra = pen[0:MH, 0:T], pen[0:MH, T:2 * T]
        relu_p = R4[:, 0:1024].rearrange("p (s c) -> p s c", s=2)
        relu_s = R4[:, 0:2 * KEYS].rearrange("p (g c) -> p g c", g=2)
        ki_pages = R4[:, 2400:3424].rearrange("p (s g d) -> p s g d", s=2, g=PAGES)
        wx = R4[0:NS, 3500:3756]
        sd = R4[:, 0:2048].rearrange("p (s t) -> p s t", s=4)
        dtmp = R4[:, 2048:3072].rearrange("p (s t) -> p s t", s=2)
        ct = R4[:, 3072:4096].rearrange("p (s t) -> p s t", s=2)
        kmask = (R4[0:NS, 2048:3072], R4[0:NS, 1024:2048])
        wP = small[:, 0:32].rearrange("p (t h) -> p t h", t=4)
        wS = small[:, 32:96].rearrange("p (g c) -> p g c", g=2)
        qiTs = small[0:HD, 96:352].rearrange("p (b c) -> p b c", b=DB)
        kiTs = small[0:HD, 352:384]
        eps = small[:, 392:393]
        m8 = small[:, 384:392]
        mixv = xnv
        tail_rows = xn[0:27, 2560:3584]
        nrow = xn[0:DB, 3584:4096]
        c_end, n_end = R4[:, 3072:3584], R4[0:1, 3584:4096]
        sds = small[0:NS, 0:P].rearrange("p (h t) -> p h t", h=MH)
        cqs, dec_bc = small[:, P:2 * P], small[:, 256:288]
        den = small[:, 288:308].rearrange("p (t h) -> p t h", t=5)
        hss = small[:, 308:328].rearrange("p (t h) -> p t h", t=5)
        a_score = proj[:, 400:1936].rearrange("p (s c) -> p s c", s=3)
        a_pt = proj[:, 1936:2960].rearrange("p (s c) -> p s c", s=2)
        atok = proj[:, 2960:3472]
        a_neg = small[:, 328:336]
        a_sum = small[:, 336:352].rearrange("p (s h) -> p s h", s=2)
        s_max = small[:, 352:355]
        s_q = kiT[:, :].rearrange("p (g b c) -> p g b c", g=2, b=DB)
        kTnew = small[:, 0:64].rearrange("p (g s) -> p g s", g=2)
        k_twice = proj[:, 11300:13348].rearrange("p (t h i d) -> p t h i d", t=4, h=KVH, i=2)
        kTb = [proj[:, c:c + 2048].rearrange("p (g s) -> p g s", g=2) for c in (8720, 400)]
        s_prob = proj[:, 10768:11824]
        s_pt = [proj[:, c:c + 1152].rearrange("p (g c) -> p g c", g=9) for c in (11824, 2448)]
        s_logit = (psum[:, 0:KEYS], psum[:, 3 * 512 - NS:3 * 512 - NS + KEYS])
        small_ss = rawr[:, 1024:1084].rearrange("p (t h) -> p t h", t=5)
        m0T = tiny[0:MH, 0:8]
        bgate = tiny[0:MH, 8:10]
        mrow = tiny[0:MH, 46:55]
        winter = tiny[0:MH, 10:42]
        decT = tiny[0:8, 42:46]
        acol = gcols[:, 0:60].rearrange("p (t q h) -> p t q h", t=5, q=3)

        def logit_parts(g, turned):
            c = NS * g
            return ((s_logit[g][:, c:c + 512], turned[:, :, 0:512]), (s_logit[g][:, c + 512:c + PAST], turned[:, :, 512:PAST]),
                    (s_logit[g][:, PAST * (1 - g):PAST * (1 - g) + NS], kTnew))

        K_PLACE = [b for buf in (ring[:, 0:4096], cq, qk2, ring[:, 0:4096]) for b in (buf, buf)]
        V_PLACE = [b for buf in (ring[:, 4096:8192], R4, cq, qk2) for b in (buf, buf)]

        def k_pages(b):
            return K_PLACE[b][:, 2048 * (b % 2):2048 * (b % 2) + 2048].rearrange("p (g c) -> p g c", g=PAGES)

        def v_pages(b):
            return V_PLACE[b][:, 2048 * (b % 2):2048 * (b % 2) + 2048].rearrange("p (g c) -> p g c", g=PAGES)

        k_in = (s_kpage_in0, s_kpage_in1, s_kpage_in2, s_kpage_in3)
        v_in = (s_vpage_in0, s_vpage_in1, s_vpage_in2, s_vpage_in3, s_vpage_in4, s_vpage_in5, s_vpage_in6, s_vpage_in7)

        def sig(f):
            return R4[:, T * (1 + f % 2):T * (1 + f % 2) + T].rearrange("p (h t) -> p h t", h=2)

        def slab_view(i):
            kind, _, n = SLABS[i]
            base = 4096 * (i % 2)
            nk = FT if kind == "down" else KT
            cols = 512 if kind == "ffn" else n
            return ring[:, base:base + nk * cols].rearrange("p (k n) -> p k n", k=nk)

        def slab_arrived(eng, i):
            pieces = sum(2 if SLABS[j][0] in ("small", "ffn") else 1 for j in range(i % 2, i + 1, 2))
            eng.wait_ge(s_slab_in_even if i % 2 == 0 else s_slab_in_odd, 16 * pieces)

        def sync_layer(block, l):
            @block.sync
            def _(sp):
                w_in, w_out, w_gu, w_down = (A[n][bass.ds(l, 1), :, :] for n in ("w_in", "w_out", "w_gate_up", "w_down"))
                lay = bass.ds(l, 1)

                sp.dma_start(vec[0:32, :], A["conv_w"][lay, :, :].rearrange("a j (m p) -> (a j m) p", p=P)).then_inc(s_vec_in, 16)
                sp.dma_start(vec[32:40, :], A["g_mix"][lay, :].rearrange("a (k p) -> (a k) p", p=P)).then_inc(s_vec_in, 16)
                sp.dma_start(vec[40:48, :], A["g_ffn"][lay, :].rearrange("a (k p) -> (a k) p", p=P)).then_inc(s_vec_in, 16)
                sp.dma_start(vec[48:80, :], A["state_n"][lay, :, :, :].rearrange("a b h d -> (a b h) d")).then_inc(s_vec_in, 16)
                sp.dma_start(R4[0:24, 3072:4096], A["state_conv"][lay, :, :, :].rearrange("a b j c -> (a b j) c")).then_inc(s_vec_in, 16)

                def load_slab(i):
                    kind, c, n = SLABS[i]
                    sem = s_slab_in_even if i % 2 == 0 else s_slab_in_odd
                    dst = slab_view(i)
                    if i >= 2:
                        sp.wait_ge(s_out_done, slots_before(i - 1))
                    if kind == "small":
                        for a, b, c in ((0, 8, MI), (8, 80, IK)):
                            sp.dma_start(dst[:, :, a:b], w_in[:, :, c:c + b - a].rearrange("a (k p) n -> p (a k) n", p=P)).then_inc(sem, 16)
                    elif kind == "ffn":
                        for a, c in ((0, c), (256, DFF + c)):
                            sp.dma_start(dst[:, :, a:a + 256], w_gu[:, :, c:c + 256].rearrange("a (k p) n -> p (a k) n", p=P)).then_inc(sem, 16)
                    else:
                        w = {"tok": w_in, "conv": w_in, "out": w_out, "down": w_down}[kind]
                        sp.dma_start(dst, w[:, :, c:c + n].rearrange("a (k p) n -> p (a k) n", p=P)).then_inc(sem, 16)

                def page(i):
                    return bass.ds(l * POOL + sp.value_load(pages[0:1, i:i + 1], min_val=0, max_val=POOL - 1), 1)

                def load_index_keys(b):
                    for g in range(PAGES):
                        src = A["cache_kidx"][page(b * PAGES + g), :, :].rearrange("a p d -> p (a d)")
                        sp.dma_start(ki_pages[:, b % 2, g, :], src).then_inc(s_kipage_in0 if b % 2 == 0 else s_kipage_in1, 16)

                load_slab(0)
                load_slab(1)
                sp.dma_start(pen[0:MH, 0:2 * T], A["gate_rows"][:, :]).then_inc(s_gate_in, 16)
                sp.dma_start(m0T, A["state_m"][lay, :, :].rearrange("a b h -> h (a b)"), allow_slow_non_contiguous=True).then_inc(s_gate_in, 16)
                sp.dma_start(bgate[:, 0:1], A["b_gate"][lay, 0:MH].rearrange("a h -> h a"), allow_slow_non_contiguous=True).then_inc(s_gate_in, 16)
                sp.dma_start(bgate[:, 1:2], A["b_gate"][lay, MH:2 * MH].rearrange("a h -> h a"), allow_slow_non_contiguous=True).then_inc(s_gate_in, 16)
                sp.dma_start(gqk[:, 0:HD], A["g_q"][lay, :].partition_broadcast(P).rearrange("p a n -> p (a n)")).then_inc(s_g_in, 16)
                sp.dma_start(gqk[:, HD:2 * HD], A["g_k"][lay, :].partition_broadcast(P).rearrange("p a n -> p (a n)")).then_inc(s_g_in, 16)
                sp.dma_start(gmout[:, :], A["g_mout"][lay, :].partition_broadcast(P).rearrange("p a n -> p (a n)")).then_inc(s_g_in, 16)
                sp.wait_ge(s_conv_state_turned, 1)
                load_index_keys(0)
                load_index_keys(1)
                for i in range(2, 6):
                    load_slab(i)
                for b in range(2, DB):
                    sp.wait_ge(s_kiturn, 2 * b - 2)
                    load_index_keys(b)
                    if b == 6:
                        load_slab(6)
                load_slab(7)
                sp.wait_ge(s_sscore, 1)
                for b in range(DB):
                    sp.dma_start(c0[:, b, :, :], A["state_C"][lay, b, :, :, :].rearrange("a h v d -> v (a h) d")).then_inc(s_c0_in, 16)
                sp.wait_ge(s_qi_roped, 1)
                sp.dma_start(O["kidx_p"][lay, 0, :, :].rearrange("a (t p) d -> p (a t) d", p=P), qi[:, 0:4, 8, :]).then_inc(s_kv_stored, 16)
                sp.dma_start(O["kidx_s"][lay, :, :, :].rearrange("a b t d -> (a b t) d"), qi[0:NS, 4, 8, :]).then_inc(s_kv_stored, 16)
                sp.wait_ge(s_out_free, 10)
                sp.dma_start(O["v_p"][lay, 0, :, :, :].rearrange("a (t p) h d -> p (a t) (h d)", p=P), va[:, 0:4, :]).then_inc(s_kv_stored, 16)
                sp.dma_start(O["v_s"][lay, :, :, :, :].rearrange("a b t h d -> (a b t) (h d)"), va[0:NS, 4, :]).then_inc(s_kv_stored, 16)
                sp.wait_ge(s_qk_ready, 1)
                sp.dma_start(O["k_p"][lay, 0, :, :, :].rearrange("a (t p) h d -> p (a t) (h d)", p=P), qk[:, 0:4, 8:12, :].rearrange("p t h d -> p t (h d)")).then_inc(s_kv_stored, 16)
                sp.dma_start(O["k_s"][lay, :, :, :, :].rearrange("a b t h d -> (a b t) (h d)"), qk[0:NS, 4, 8:12, :].rearrange("p h d -> p (h d)")).then_inc(s_kv_stored, 16)
                sp.wait_ge(s_gate_rows_ready, 1)
                sp.dma_start(O["m_p"][lay, 0, :].rearrange("a h -> h a"), mrow[:, 0:1], allow_slow_non_contiguous=True).then_inc(s_kv_stored, 16)
                sp.dma_start(O["m_s"][lay, :, :].rearrange("a b h -> h (a b)"), mrow[:, 1:9], allow_slow_non_contiguous=True).then_inc(s_kv_stored, 16)
                sp.wait_ge(s_out_done, OUT0)
                sp.dma_start(nrow, A["state_n"][lay, :, :, :].rearrange("a b h d -> (a b) (h d)")).then_inc(s_n0_in, 16)

                def load_pages(b, names):
                    for g in range(PAGES):
                        at = page(b * PAGES + g)
                        for name in names:
                            buf, sem = (k_pages(b), k_in[b % 4]) if name == "cache_k" else (v_pages(b), v_in[b])
                            sp.dma_start(buf[:, g, :], A[name][at, :, :].rearrange("a p d -> p (a d)")).then_inc(sem, 16)

                def load_both(b):
                    load_pages(b, ("cache_k", "cache_v"))

                sp.wait_ge(s_tail_copied, 1)
                sp.dma_start(O["conv_p"][lay, 0, :, :].rearrange("a j c -> (a j) c"), tail_rows[0:3, :]).then_inc(s_stored, 16)
                sp.dma_start(O["conv_s"][lay, :, :, :].rearrange("a b j c -> (a b j) c"), tail_rows[3:27, :]).then_inc(s_stored, 16)
                load_both(0)
                load_both(1)
                sp.wait_ge(s_c_new, MH)
                for b in range(DB):
                    sp.dma_start(O["C_s"][lay, b, :, :, :].rearrange("a h v d -> v (a h) d"), c0[:, b, :, :]).then_inc(s_stored, 16)
                sp.wait_ge(s_n_new, 1)
                sp.dma_start(O["n_s"][lay, :, :, :].rearrange("a b h d -> (a b) (h d)"), nrow).then_inc(s_stored, 16)
                sp.wait_ge(s_c_copied, 1)
                sp.dma_start(O["C_p"][lay, 0, :, :, :].rearrange("a h v d -> v (a h) d"), c_end.rearrange("p (h d) -> p h d", h=MH)).then_inc(s_stored, 16)
                sp.dma_start(O["n_p"][lay, 0, :, :].rearrange("a h d -> a (h d)"), n_end).then_inc(s_stored, 16)
                sp.wait_ge(s_stored, 16 * STORES)
                sp.wait_ge(s_kv_stored, 16 * 8)
                sp.wait_ge(s_hn_ready, 1)
                load_both(2)
                load_both(3)
                for b in range(4, DB):
                    sp.wait_ge(s_kt_turned, 4 * (b - 3))
                    load_pages(b, ("cache_k",))
                for b in range(4, DB):
                    if b == 6:
                        sp.wait_ge(s_kt_turned, 4 * 6)
                    load_pages(b, ("cache_v",))
                sp.wait_ge(s_kt_turned, 4 * DB)
                load_slab(8)
                sp.wait_ge(s_s_pv, 2)
                load_slab(9)
                for i in range(10, len(SLABS)):
                    load_slab(i)
        def pool_layer(block, l):
            @block.gpsimd
            def _(pool):
                pool.memset(mv[:, 0:4, :, P:P + 1], 1.0)
                pool.memset(mv[0:NS, 4, :, P:P + 1], 1.0).then_inc(s_ones_set, 1)
                for j in range(3):
                    pool.wait_ge(s_scored, j + 1)
                    blk = penv[:, j, (j + 1) * P:(j + 2) * P]
                    pool.affine_select(out=blk, in_=blk, compare_op=ALU.is_ge, fill=NEG, base=0,
                                       pattern=[[-1, P]], channel_multiplier=1).then_inc(s_masked, 1)
                pool.wait_ge(s_qk_ready, 1)
                pool.wait_ge(s_sscore, 1)
                for m in range(8):
                    ins = pool.memset(raw[m][:, 0:3], 0.0)
                ins.then_inc(s_raw_zeroed, 1)
                for m in range(MH, 2 * MH):
                    pool.wait_ge(s_conv_silu, m + 1)
                    pool.tensor_scalar(cqv[:, m, :], cqv[:, m, :], P ** -0.5, None, ALU.mult).then_inc(s_k_scaled, 1)
                def mask_keys(h):
                    pool.tensor_tensor(kmask[h % 2].rearrange("p (b d) -> p b d", b=DB), kw[0:NS, 4, h, :].unsqueeze(1).broadcast_to([NS, DB, P]),
                                       const("blk", NS).unsqueeze(2).broadcast_to([NS, DB, P]), ALU.mult).then_inc(s_kmask_ready, 1)

                pool.wait_ge(s_ktok_copied, 5)
                mask_keys(0)
                mask_keys(1)
                pool.wait_ge(s_dec_copied, 1)
                pool.wait_ge(s_cq_done, 8)
                for h in range(MH):
                    pool.tensor_tensor(c0[:, :, h, :], c0[:, :, h, :], dec_bc[:, DB * h:DB * h + DB].unsqueeze(2).broadcast_to([P, DB, P]), ALU.mult)\
                        .then_inc(s_c_decayed, 1)
                    if h < 2:
                        pool.wait_ge(s_u_sum, h + 1)
                        mask_keys(h + 2)
                for n in range(4 * MH):
                    s = n % 4
                    pool.wait_ge(s_sd, n + 1)
                    blk = sd[:, s, P * s:P * s + P]
                    pool.affine_select(out=blk, in_=blk, compare_op=ALU.is_ge, fill=0.0, base=0,
                                       pattern=[[1, P]], channel_multiplier=-1).then_inc(s_sd_masked, 1)
        def act_layer(block, l):
            @block.scalar
            def _(act):
                chain = [0]

                def step(ins):
                    chain[0] += 1
                    ins.then_inc(s_act_chain, 1)
                    act.wait_ge(s_act_chain, chain[0])

                def norm(squares, summed, rstd_ready, out):
                    for k in range(KT):
                        if squares is s_sq2:
                            act.wait_ge(s_out_free, OUT0 + k + 1)
                        act.activation(cqv[:, k, :], xv[:, k, :], ACT.Square).then_inc(squares, 1)
                    act.wait_ge(summed, 1)
                    step(act.activation(out, ps(4, 2).rearrange("p (h t) -> p h t", h=2)[:, :, 0:HALF], ACT.Ln,
                                        bias=eps[:, :], scale=1.0 / D))
                    act.activation(out, out, ACT.Exp, scale=-0.5).then_inc(rstd_ready, 1)

                def slot(n):
                    act.wait_ge(s_out_done, n + 1)
                    return ps(2 * (n % 2), 2)

                def token_slab(n, parts):
                    for i in range(3):
                        src = slot(n + i).rearrange("p (t c) -> p t c", t=2)
                        for c, m, dst in parts:
                            if i < 2:
                                ins = act.activation(dst[:, 2 * i:2 * i + 2], like(src[:, :, c:c + m], dst, 1), ACT.Copy)
                            else:
                                ins = act.activation(dst[0:NS, 4], like(src[0:NS, 0, c:c + m], dst, 0), ACT.Copy)
                        ins.then_inc(s_out_free, 1)

                def like(src, dst, free):
                    if len(dst.shape) == 3:
                        return src
                    if free:
                        return src.rearrange("p t (h d) -> p t h d", h=dst.shape[2])
                    return src.rearrange("p (h d) -> p h d", h=dst.shape[2])

                def token_group(n, i, m, dst, func):
                    src = slot(n + i).rearrange("p (t c) -> p t c", t=2)
                    if i < 2:
                        ins = act.activation(dst[:, 2 * i:2 * i + 2], like(src[:, :, 0:m], dst, 1), func)
                    else:
                        ins = act.activation(dst[0:NS, 4], like(src[0:NS, 0, 0:m], dst, 0), func)
                    ins.then_inc(s_out_free, 1)

                def conv_silu(m):
                    act.wait_ge(s_conv_z, m + 1)
                    act.activation(cqv[:, m, :], cqv[:, m, :], ACT.Silu).then_inc(s_conv_silu, 1)

                rstd = R4[:, 0:T].rearrange("p (h t) -> p h t", h=2)
                norm(s_sq1, s_sum1, s_rstd1, rstd)

                src = slot(0)[:, 0:400].rearrange("p (t c) -> p t c", t=5)
                act.activation(g80[:, 0:4, :], src[:, 0:4, :], ACT.Copy)
                act.activation(g80[0:NS, 4, :], src[0:NS, 4, :], ACT.Copy).then_inc(s_out_free, 1)
                token_slab(1, [(0, 512, qi[:, :, 0:8, :])])
                token_slab(4, [(0, 512, qk[:, :, 0:8, :])])

                act.wait_ge(s_gate_read, 1)
                step(act.activation(gr[:, 2, :], gr[:, 1, :], ACT.Abs))
                step(act.activation(gr[:, 2, :], gr[:, 2, :], ACT.Exp, scale=-1.0))
                act.activation(gr[:, 2, :], gr[:, 2, :], ACT.Ln, bias=1.0).then_inc(s_gate_log, 1)
                act.wait_ge(s_gate_rows_ready, 1)
                act.activation(gr[:, 4, :], gr[:, 6, :], ACT.Exp, scale=-1.0)
                act.activation(gr[:, 5, 0:SEQ], gr[:, 0, 0:SEQ], ACT.Exp, bias=negM[:, SEQ - 1:SEQ])
                act.activation(gr[:, 5, SEQ:T], gr[:, 5, SEQ:T], ACT.Exp)
                act.activation(winter, winter, ACT.Exp).then_inc(s_gate_exps, 1)

                for i in range(5):
                    act.wait_ge(s_idx_turned, i + 1)
                    act.activation(qiT[:, i, :] if i < 4 else kiT[:, :], ps(4 + i % 2), ACT.Copy).then_inc(s_idx_copied, 1)
                act.wait_ge(s_idx_turned, 6)
                act.activation(qiTs.rearrange("p b (h t) -> p h b t", h=IH),
                               ps(6)[0:HD, 0:256].rearrange("p (h b t) -> p h b t", h=IH, b=DB), ACT.Copy)
                act.activation(kiTs, ps(6)[0:HD, 256:288], ACT.Copy)
                act.activation(wS, ps(7)[:, 0:64].rearrange("p (g c) -> p g c", g=2), ACT.Copy).then_inc(s_idx_copied, 1)

                token_slab(7, [(0, 256, qk[:, :, 8:12, :]), (256, 256, va)])

                for n in range(3 * IH):
                    j = n // IH + 1
                    act.wait_ge(s_dots, n + 1)
                    if n >= 2:
                        act.wait_ge(s_relu_free, n - 1)
                    act.activation(relu_p[:, n % 2, 0:(j + 1) * P], ps(4 + n % 2)[:, 0:(j + 1) * P], ACT.Relu,
                                   scale=HD ** -0.5).then_inc(s_relu_done, 1)

                for u in range(10):
                    if u < DB:
                        b = u
                        for hf in range(2):
                            act.wait_ge(s_kiturn, 2 * b + hf + 1)
                            if b >= 2:
                                act.wait_ge(s_sdots, 2 * (b - 2) + hf + 1)
                            act.activation(kiTb[:, b % 2, 512 * hf:512 * hf + 512], ps(6 + hf)[0:HD, :], ACT.Copy).then_inc(s_kicopy, 1)
                    if u % 5 in (1, 3, 4):
                        if u < 5:
                            token_group(10, u // 2, 512, mv[:, :, :, 0:P], ACT.Copy)
                        else:
                            token_group(13, (u - 5) // 2, 512, mo, ACT.Sigmoid)
                    if u in (3, 7):
                        act.wait_ge(s_sdots, 2 * u + 2)
                        if u == 3:
                            act.wait_ge(s_relu_free, 3 * IH)
                        act.activation(relu_s[:, u // 4, 0:PAST], ps(4, 2), ACT.Relu, scale=HD ** -0.5).then_inc(s_srelu, 1)
                act.wait_ge(s_snew, 1)
                act.activation(relu_s[:, :, PAST:KEYS], ps(6)[:, 0:64].rearrange("p (g c) -> p g c", g=2), ACT.Relu,
                               scale=HD ** -0.5).then_inc(s_srelu, 1)

                act.wait_ge(s_qk_sums, 1)
                for rows, t in ((P, slice(0, 4)), (NS, slice(4, 5))):
                    step(act.activation(small_ss[0:rows, t, :], small_ss[0:rows, t, :], ACT.Ln, bias=eps[0:rows, :], scale=1.0 / HD))
                    ins = act.activation(small_ss[0:rows, t, :], small_ss[0:rows, t, :], ACT.Exp, scale=-0.5)
                ins.then_inc(s_qk_rstd, 1)

                for m in range(8):
                    src = slot(CONV0 + m).rearrange("p (h t) -> p h t", h=2)
                    if m == 0:
                        act.wait_ge(s_qk_ready, 1)
                    if m == 3:
                        act.wait_ge(s_sscore, 1)
                    r_ = raw[m]
                    act.activation(r_[:, 3:3 + HALF], src[:, 0, 0:HALF], ACT.Copy)
                    act.activation(r_[:, 3 + HALF:3 + SEQ], src[:, 1, 0:SEQ - HALF], ACT.Copy)
                    act.activation(r_[:, 3 + SEQ:571].rearrange("p (b c) -> p b c", b=DB)[:, :, 3:7],
                                   src[:, 1, SEQ - HALF:HALF].rearrange("p (b c) -> p b c", b=DB), ACT.Copy).then_inc(s_out_free, 1)
                    if m >= 2:
                        conv_silu(m - 2)
                conv_silu(6)
                conv_silu(7)
                act.wait_ge(s_tail_turned, 1)
                act.activation(tail_rows, ps(0, 2)[0:27, :], ACT.Copy).then_inc(s_tail_copied, 1)
                for g in range(8):
                    act.wait_ge(s_c0_turned, g + 1)
                    if g >= 2:
                        act.wait_ge(s_cq_done, g - 1)
                    act.activation(ct[:, g % 2, :], ps(g % 2), ACT.Copy).then_inc(s_c0_copied, 1)
                act.wait_ge(s_s_dt, 1)
                act.activation(sds.rearrange("p h t -> p (h t)"), sds.rearrange("p h t -> p (h t)"), ACT.Exp).then_inc(s_s_de, 1)
                for n in range(4 * MH):
                    act.wait_ge(s_dtmp_ready, n + 1)
                    d = dtmp[:, n % 2, P * (n % 4):SEQ]
                    act.activation(d, d, ACT.Exp).then_inc(s_dexp, 1)
                act.wait_ge(s_c_sum, 1)
                act.activation(c_end, ps(2), ACT.Copy)
                act.activation(n_end, ps(3)[0:1, :], ACT.Copy).then_inc(s_c_copied, 1)
                act.wait_ge(s_hsq, 1)
                for rows, t in ((P, slice(0, 4)), (NS, slice(4, 5))):
                    step(act.activation(hss[0:rows, t, :], hss[0:rows, t, :], ACT.Ln, bias=eps[0:rows, :], scale=1.0 / P))
                    ins = act.activation(hss[0:rows, t, :], hss[0:rows, t, :], ACT.Exp, scale=-0.5)
                ins.then_inc(s_hrstd, 1)
                for h in range(MH):
                    act.wait_ge(s_mix_turned, h + 1)
                    if h == 0:
                        act.wait_ge(s_c_new, MH)
                        act.wait_ge(s_stored, 16 * STORES)
                    act.activation(mixv[:, h, :], ps(2 * (h % 2), 2)[:, 0:T], ACT.Copy).then_inc(s_mix_copied, 1)

                for g in range(8):
                    act.wait_ge(s_qt_turned, g + 1)
                    act.activation(qT[:, g, :] if g < 4 else kT2[:, g - 4, :], ps(4 + g % 2), ACT.Copy).then_inc(s_qt_copied, 1)
                for n in range(4 * QH + 1):
                    if n < 4 * QH:
                        j, h = n // QH, n % QH
                        w = (j + 1) * P
                        act.wait_ge(s_a_max, n + 1)
                        if h == 0 and j >= 2:
                            act.wait_ge(s_a_tok, j - 1)
                        act.activation(a_score[:, n % 3, 0:w], a_score[:, n % 3, 0:w], ACT.Exp, bias=a_neg[:, n % 4:n % 4 + 1],
                                       scale=HD ** -0.5, accum_out=a_sum[:, j % 2, h:h + 1]).then_inc(s_a_p, 1)
                    if n >= 1:
                        m = n - 1
                        w = (m // QH + 1) * P
                        act.wait_ge(s_pt_turned, m + 1)
                        if m >= 2:
                            act.wait_ge(s_pv, m - 1)
                        act.activation(a_pt[:, m % 2, 0:w], ps(2 + m % 2)[:, 0:w], ACT.Copy).then_inc(s_pt_copied, 1)
                def copy_keys(b):
                    for i in range(4):
                        act.wait_ge(s_kt_turned, 4 * b + i + 1)
                        if b >= 2 and i == 0:
                            act.wait_ge(s_s_log, b - 1)
                        act.activation(kTb[b % 2][:, i // 2, 512 * (i % 2):512 * (i % 2) + 512], ps(5 + i % 2), ACT.Copy).then_inc(s_kt_copied, 1)

                def sample_probs(g):
                    act.wait_ge(s_s_neg, g + 1)
                    act.activation(s_prob, s_logit[g], ACT.Exp, bias=s_max[:, 0:1], scale=HD ** -0.5,
                                   accum_out=s_max[:, 1:2]).then_inc(s_s_exp, 1)
                    act.wait_ge(s_s_pt, g + 1)
                    act.activation(s_pt[g][:, 0:8, :].rearrange("p g c -> p (g c)"), ps(5, 2), ACT.Copy)
                    act.activation(s_pt[g][0:NS, 8, :], ps(2)[0:NS, P:2 * P], ACT.Copy).then_inc(s_s_ptc, 1)

                for b in range(6):
                    copy_keys(b)
                sample_probs(0)
                copy_keys(6)
                copy_keys(7)
                sample_probs(1)

                norm(s_sq2, s_sum2, s_rstd2, rstd)
                for f in range(FT):
                    act.wait_ge(s_out_done, FFN0 + 2 * f + 1)
                    if f == 0:
                        act.wait_ge(s_xn2_ready, KT)
                    if f >= 2:
                        act.wait_ge(s_up_free, f - 1)
                    act.activation(sig(f), ps(0, 2).rearrange("p (h t) -> p h t", h=2)[:, :, 0:HALF], ACT.Silu).then_inc(s_gate_silu, 1)
        def tensor_layer(block, l):
            @block.tensor
            def _(pe):
                def slot(n):
                    if n > FFN0 + 1 and n < DOWN0:
                        pe.wait_ge(s_up_free if n % 2 else s_gate_silu, (n - FFN0) // 2)
                    elif n >= DOWN0:
                        pe.wait_ge(s_out_free, n - 1 - 2 * FT)
                    elif n >= 2:
                        pe.wait_ge(s_out_free, n - 1)
                    return ps(2 * (n % 2), 2)

                def token_tile(i, n, t):
                    if t == 0:
                        slab_arrived(pe, i)
                    w = slab_view(i)
                    out = slot(n + t // 2) if t % 2 == 0 else ps(2 * ((n + t // 2) % 2), 2)
                    c, r = TILES[t]
                    for k in range(KT):
                        mm = pe.matmul(out[0:r, 512 * (t % 2):512 * (t % 2) + 512], xnv[:, k, c:c + r], w[:, k, :],
                                       start=(k == 0), stop=(k == KT - 1))
                    if t in (1, 3, 4):
                        mm.then_inc(s_out_done, 1)

                def token_slab(i, n):
                    for t in range(5):
                        token_tile(i, n, t)

                def feature_tile(i, n, c, src):
                    slab_arrived(pe, i)
                    w = slab_view(i)
                    nk = w.shape[1]
                    out = slot(n)
                    for k in range(nk):
                        if n == FFN0:
                            pe.wait_ge(s_xn2_ready, k + 1)
                        for hf in range(2):
                            mm = pe.matmul(out[:, 512 * hf:512 * hf + HALF], w[:, k, c:c + P],
                                           src[:, k, HALF * hf:HALF * hf + HALF], start=(k == 0), stop=(k == nk - 1))
                    mm.then_inc(s_out_done, 1)

                def sum_squares(squares, k):
                    pe.wait_ge(squares, k + 1)
                    for hf in range(2):
                        mm = pe.matmul(ps(4 + hf)[:, 0:HALF], ones, cqv[:, k, HALF * hf:HALF * hf + HALF],
                                       start=(k == 0), stop=(k == KT - 1))
                    return mm

                pe.wait_ge(s_vec_in, 16 * 5)
                pe.transpose(ps(6)[:, 0:80], vec[0:80, :], ident[0:80, 0:80])
                for m in range(8):
                    mm = pe.transpose(ps(7)[:, 24 * m:24 * m + 24], R4[0:24, 3072 + P * m:3072 + P * m + P], ident[0:24, 0:24])
                mm.then_inc(s_conv_state_turned, 1)
                for k in range(KT):
                    mm = sum_squares(s_sq1, k)
                mm.then_inc(s_sum1, 1)

                slab_arrived(pe, 0)
                out = slot(0)
                for t, (c, r) in enumerate(TILES):
                    for k in range(KT):
                        if t == 0:
                            pe.wait_ge(s_xn_ready, k + 1)
                        mm = pe.matmul(out[0:r, 80 * t:80 * t + 80], xnv[:, k, c:c + r], slab_view(0)[:, k, :],
                                       start=(k == 0), stop=(k == KT - 1))
                mm.then_inc(s_out_done, 1)
                token_slab(1, 1)
                pe.wait_ge(s_out_free, 1)
                pe.wait_ge(s_rstd1, 1)
                pe.wait_ge(s_vec_copied, 1)
                for q in range(2):
                    for c, r, t in [(c, r, t) for t, (c, r) in enumerate(TILES)]:
                        mm = pe.transpose(ps(4 + 2 * q, 2)[0:MH, c:c + r], g80[0:r, t, MH * q:MH * q + MH], ident[0:r, 0:r])
                mm.then_inc(s_gate_turned, 1)
                token_slab(2, 4)

                pe.wait_ge(s_qi_roped, 1)
                pe.wait_ge(s_gate_read, 1)
                for g in range(5):
                    if g >= 2:
                        pe.wait_ge(s_idx_copied, g - 1)
                    for t in range(4):
                        mm = pe.transpose(ps(4 + g % 2)[:, P * t:P * t + P], qi[:, t, 2 * g:2 * g + 2, :].rearrange("p h d -> p (h d)"), ident)
                    mm.then_inc(s_idx_turned, 1)
                for h in range(IH + 1):
                    pe.transpose(ps(6)[0:HD, NS * h:NS * h + NS], qi[0:NS, 4, h, :], ident[0:NS, 0:NS])
                pe.wait_ge(s_w_spread, 1)
                for g in range(2):
                    mm = pe.transpose(ps(7)[:, NS * g:NS * g + NS], wx[:, P * g:P * g + P], ident[0:NS, 0:NS])
                mm.then_inc(s_idx_turned, 1)
                token_slab(3, 7)

                pe.wait_ge(s_gate_exps, 1)
                pe.wait_ge(s_idx_copied, 6)
                for t, (c, r) in enumerate(TILES):
                    for q, row in enumerate((0, 4, 5)):
                        pe.transpose(ps(6)[0:r, 12 * t + MH * q:12 * t + MH * q + MH], gr[:, row, c:c + r], ident[0:MH, 0:MH])
                pe.transpose(ps(6)[0:NS, 60:64], winter, ident[0:MH, 0:MH])
                pe.transpose(ps(6)[0:DB, 64:68], winter.rearrange("p (b t) -> p b t", b=DB)[:, :, 3], ident[0:MH, 0:MH])\
                  .then_inc(s_gate_cols_turned, 1)

                for n in range(3 * IH):
                    j, h = n // IH + 1, n % IH
                    if n >= 2:
                        pe.wait_ge(s_relu_done, n - 1)
                    q0 = HD * (h % 2)
                    pe.matmul(ps(4 + n % 2)[:, 0:(j + 1) * P], qiT[q0:q0 + HD, h // 2, j * P:(j + 1) * P],
                              kiT[q0:q0 + HD, 0:(j + 1) * P], start=True, stop=True).then_inc(s_dots, 1)

                pe.wait_ge(s_gate_cols_ready, 1)
                pe.wait_ge(s_relu_done, 3 * IH)
                for u in range(10):
                    b = u
                    if b < DB:
                        pe.wait_ge(s_kipage_in0 if b % 2 == 0 else s_kipage_in1, 16 * PAGES * (b // 2 + 1))
                        for hf in range(2):
                            if b >= 1:
                                pe.wait_ge(s_kicopy, 2 * (b - 1) + hf + 1)
                            for g in range(4):
                                mm = pe.transpose(ps(6 + hf)[0:HD, PAGE * g:PAGE * g + PAGE], ki_pages[:, b % 2, 4 * hf + g, :], ident)
                            mm.then_inc(s_kiturn, 1)
                    token_tile(4 + u // 5, 10 + 3 * (u // 5), u % 5)
                    if b < DB:
                        r0 = NS * (b % 4)
                        if b == 4:
                            pe.wait_ge(s_srelu, 1)
                        for hf in range(2):
                            pe.wait_ge(s_kicopy, 2 * b + hf + 1)
                            pe.matmul(ps(4 + hf)[r0:r0 + NS, :], qiTs[:, b, :], kiTb[:, b % 2, 512 * hf:512 * hf + 512],
                                      start=True, stop=True).then_inc(s_sdots, 1)
                    if b == DB:
                        for b in range(DB):
                            r0 = NS * (b % 4)
                            mm = pe.matmul(ps(6)[r0:r0 + NS, NS * (b // 4):NS * (b // 4) + NS], qiTs[:, b, :], kiTs, start=True, stop=True)
                        mm.then_inc(s_snew, 1)

                for m in range(8):
                    feature_tile(6 + m // 4, CONV0 + m, P * (m % 4), xnv)
                    if m == 0:
                        for c, n, dst in ((0, 512, ps(4)), (512, 512, ps(5)), (PAST, NS, ps(7))):
                            pe.wait_ge(s_srelu, 3)
                            for g in range(2):
                                mm = pe.matmul(dst[0:NS, 0:n], wS[:, g, :], relu_s[:, g, c:c + n], start=(g == 0), stop=(g == 1))
                        mm.then_inc(s_sscore, 1)

                pe.wait_ge(s_out_free, OUT0)
                pe.wait_ge(s_conv_done, 8)
                for m in range(8):
                    mm = pe.transpose(ps(0, 2)[0:27, P * m:P * m + P], tails[:, 27 * m:27 * m + 27], ident)
                mm.then_inc(s_tail_turned, 1)
                pe.wait_ge(s_conv_silu, 8)
                pe.wait_ge(s_k_scaled, MH)
                for t, (c, r) in enumerate(TILES):
                    if t >= 2:
                        pe.wait_ge(s_ktok_copied, t - 1)
                    for h in range(MH):
                        mm = pe.transpose(ps(2 + t % 2)[0:r, P * h:P * h + P], cqv[:, MH + h, c:c + r], ident)
                    mm.then_inc(s_ktok_turned, 1)
                pe.wait_ge(s_c0_in, 16 * DB)
                pe.wait_ge(s_sscore_copied, 1)
                pe.wait_ge(s_tail_copied, 1)
                s0 = SEQ
                for g in range(9):
                    if g < 8:
                        h, b0 = g // 2, 4 * (g % 2)
                        if g >= 2:
                            pe.wait_ge(s_c0_copied, g - 1)
                        for i in range(4):
                            mm = pe.transpose(ps(g % 2)[:, P * i:P * i + P], c0[:, b0 + i, h, :], ident)
                        mm.then_inc(s_c0_turned, 1)
                    if g >= 1:
                        h, b0 = (g - 1) // 2, 4 * ((g - 1) % 2)
                        pe.wait_ge(s_c0_copied, g)
                        for i in range(4):
                            b = b0 + i
                            mm = pe.matmul(ps(6)[:, NS * h + DT * b:NS * h + DT * b + DT], ct[:, (g - 1) % 2, P * i:P * i + P],
                                           cqv[:, h, s0 + DT * b:s0 + DT * b + DT], start=True, stop=True)
                        mm.then_inc(s_cq_done, 1)
                for h in range(MH):
                    q, k = cqv[:, h, s0:T], cqv[:, MH + h, s0:T]
                    pe.matmul(ps(7)[0:NS, DB * h:DB * h + DB], q, vT[:, 48 + h:80:MH], start=True, stop=True)
                    pe.matmul(ps(4)[0:NS, NS * h:NS * h + NS], k, q, start=True, stop=True)
                    sel = const("sel", MH)[:, P * h:P * h + P]
                    pe.matmul(ps(4)[0:NS, P + NS * h:P + NS * h + NS], sel[:, 0:NS], negM[:, s0:T], start=True, stop=True)
                    mm = pe.matmul(ps(4)[:, 2 * P + DB * h:2 * P + DB * h + DB], sel,
                                   winter.rearrange("p (b t) -> p b t", b=DB)[:, :, 3], start=True, stop=True)
                mm.then_inc(s_s_small, 1)
                pe.wait_ge(s_cq_copied, 1)
                for h in range(MH):
                    mm = pe.transpose(ps(5)[0:NS, P * h:P * h + P], cqs[:, NS * h:NS * h + NS], ident)
                mm.then_inc(s_cq_turned, 1)
                pe.wait_ge(s_s_sd, 1)
                pe.wait_ge(s_ktok_copied, 5)
                pe.wait_ge(s_ones_set, 1)
                for h in range(MH):
                    mm = pe.matmul(ps(2, 2)[0:NS, 256 * h:256 * h + P + 1], sds[:, h, :], mv[0:NS, 4, h, :], start=True, stop=True)
                mm.then_inc(s_s_num, 1)
                pe.wait_ge(s_s_num_read, 1)
                for h in range(MH):
                    pe.wait_ge(s_kmask_ready, h + 1)
                    if h >= 2:
                        pe.wait_ge(s_c_new, h - 1)
                    for hf in range(2):
                        mm = pe.matmul(ps(2 * (h % 2) + hf), mv[0:NS, 4, h, 0:P], kmask[h % 2][:, 512 * hf:512 * hf + 512], start=True, stop=True)
                    mm.then_inc(s_u_sum, 1)
                pe.matmul(ps(5)[0:DB, :], const("blk", NS), kw[0:NS, 4, :, :].rearrange("p h d -> p (h d)"), start=True, stop=True)\
                  .then_inc(s_n_sum, 1)
                pe.wait_ge(s_c_new, MH)
                pe.wait_ge(s_n_new, 1)

                def mem_score(n):
                    h, s = n // 4, n % 4
                    if s == 0:
                        if h >= 2:
                            pe.wait_ge(s_dtmp_ready, 4 * (h - 1))
                        pe.matmul(ps(h % 2), const("sel", MH)[:, P * h:P * h + P], negM[:, 0:SEQ], start=True, stop=True).then_inc(s_negm_bc, 1)
                    if n >= 2:
                        pe.wait_ge(s_sd, n - 1)
                    pe.matmul(ps(2 + n % 2)[:, 0:SEQ - P * s], cqv[:, MH + h, P * s:P * s + P], cqv[:, h, P * s:SEQ],
                              start=True, stop=True).then_inc(s_mem_s, 1)

                mem_score(0)
                mem_score(1)
                for h in range(MH):
                    for n in range(4 * h + 2, min(4 * h + 6, 4 * MH)):
                        mem_score(n)
                    pe.wait_ge(s_sd_masked, 4 * (h + 1))
                    if h >= 2:
                        pe.wait_ge(s_num_read, h - 1)
                    for t in range(4):
                        for s in range(t + 1):
                            mm = pe.matmul(ps(4 + 2 * (h % 2), 2)[:, 256 * t:256 * t + P + 1], sd[:, s, P * t:P * t + P],
                                           mv[:, s, h, :], start=(s == 0), stop=(s == t))
                    mm.then_inc(s_num, 1)
                pe.wait_ge(s_sd, 4 * MH)
                for h in range(MH):
                    for s in range(4):
                        pe.matmul(ps(2)[:, P * h:P * h + P], mv[:, s, h, 0:P], kw[:, s, h, :], start=(s == 0), stop=(s == 3))
                for s in range(4):
                    mm = pe.matmul(ps(3)[0:1, :], ones[:, 0:1], kw[:, s, :, :].rearrange("p h d -> p (h d)"), start=(s == 0), stop=(s == 3))
                mm.then_inc(s_c_sum, 1)
                pe.wait_ge(s_hn_ready, 1)
                pe.wait_ge(s_c_copied, 1)
                for h in range(MH):
                    if h >= 2:
                        pe.wait_ge(s_mix_copied, h - 1)
                    for t, (c, r) in enumerate(TILES):
                        mm = pe.transpose(ps(2 * (h % 2), 2)[:, c:c + r], htok[0:r, t, h, :], ident[0:r, 0:r])
                    mm.then_inc(s_mix_turned, 1)

                pe.wait_ge(s_num_read, MH)
                for g in range(8):
                    if g >= 2:
                        pe.wait_ge(s_qt_copied, g - 1)
                    if g == 4:
                        pe.wait_ge(s_k_twice_ready, 1)
                    for t in range(4):
                        src = qk[:, t, 2 * g:2 * g + 2, :] if g < 4 else k_twice[:, t, g - 4, :, :]
                        mm = pe.transpose(ps(4 + g % 2)[:, P * t:P * t + P], src.rearrange("p h d -> p (h d)"), ident)
                    mm.then_inc(s_qt_turned, 1)
                for i in range(4):
                    pe.transpose(ps(6)[:, NS * i:NS * i + NS], qk[0:NS, 4, 2 * i:2 * i + 2, :].rearrange("p h d -> p (h d)"), ident[0:NS, 0:NS])
                for p in range(2):
                    mm = pe.transpose(ps(7)[:, NS * p:NS * p + NS], qk[0:NS, 4, 8 + 2 * p:10 + 2 * p, :].rearrange("p h d -> p (h d)"), ident[0:NS, 0:NS])
                mm.then_inc(s_s_turned, 1)
                pe.wait_ge(s_qt_copied, 8)
                pe.wait_ge(s_mix_copied, MH)
                pe.wait_ge(s_s_q_ready, 1)

                def turn_out(j):
                    pe.wait_ge(s_a_tok, j + 1)
                    if j >= 1:
                        pe.wait_ge(s_a_copied, j)
                    for f in range(4):
                        mm = pe.transpose(ps(6)[:, P * f:P * f + P], atok[:, P * f:P * f + P], ident)
                    mm.then_inc(s_a_turned, 1)

                for n in range(4 * QH + 2):
                    if n < 4 * QH:
                        j, h = n // QH, n % QH
                        q0 = HD * (h % 2)
                        if n >= 2:
                            pe.wait_ge(s_a_max, n - 1)
                        pe.matmul(ps(n % 2)[:, 0:(j + 1) * P], qT[q0:q0 + HD, h // 2, P * j:P * j + P],
                                  kT2[q0:q0 + HD, h // 2, 0:(j + 1) * P], start=True, stop=True).then_inc(s_a_s, 1)
                    if 1 <= n <= 4 * QH:
                        m = n - 1
                        pe.wait_ge(s_a_p, m + 1)
                        if m >= 2:
                            pe.wait_ge(s_pt_copied, m - 1)
                        for s in range(m // QH + 1):
                            mm = pe.transpose(ps(2 + m % 2)[:, P * s:P * s + P], a_score[:, m % 3, P * s:P * s + P], ident)
                        mm.then_inc(s_pt_turned, 1)
                    if n >= 2:
                        m = n - 2
                        j, h = m // QH, m % QH
                        pe.wait_ge(s_pt_copied, m + 1)
                        if h == 0 and j >= 2:
                            pe.wait_ge(s_a_tok, j - 1)
                        for s in range(j + 1):
                            mm = pe.matmul(ps(4 + j % 2)[:, HD * h:HD * h + HD], a_pt[:, m % 2, P * s:P * s + P],
                                           va[:, s, HD * (h // 2):HD * (h // 2) + HD], start=(s == 0), stop=(s == j))
                        mm.then_inc(s_pv, 1)
                        if h == 4 and j >= 1:
                            turn_out(j - 1)
                turn_out(3)

                def turn_keys(b):
                    pe.wait_ge(k_in[b % 4], 16 * PAGES * (b // 4 + 1))
                    if b == 6:
                        pe.wait_ge(s_s_ptc, 1)
                    for i in range(4):
                        if 4 * b + i >= 2:
                            pe.wait_ge(s_kt_copied, 4 * b + i - 1)
                        for q in range(4):
                            pg = 4 * (i % 2) + q
                            mm = pe.transpose(ps(5 + i % 2)[:, P * q:P * q + P], k_pages(b)[:, pg, P * (i // 2):P * (i // 2) + P], ident)
                        mm.then_inc(s_kt_turned, 1)

                def sample_logits(b):
                    pe.wait_ge(s_kt_copied, 4 * b + 4)
                    g, r0 = b // 4, NS * (b % 4)
                    for dst, keys in logit_parts(g, kTb[b % 2])[0:2]:
                        for p in range(2):
                            mm = pe.matmul(dst[r0:r0 + NS, :], s_q[:, p, b, :], keys[:, p, :], start=(p == 0), stop=False,
                                           skip_group_check=True)
                    mm.then_inc(s_s_log, 1)

                def finish_logits(g):
                    new = logit_parts(g, kTb[0])[2][0]
                    for b in range(4 * g, 4 * g + 4):
                        for p in range(2):
                            pe.matmul(new[NS * (b % 4):NS * (b % 4) + NS, :], s_q[:, p, b, :], kTnew[:, p, :], start=(p == 0), stop=False,
                                      skip_group_check=True)
                    pe.wait_ge(s_sample_mask, 1)
                    for (dst, _), (c, w) in zip(logit_parts(g, kTb[0]), ((0, 512), (512, 512), (PAST, NS))):
                        mm = pe.matmul(dst, const("rep", NS)[:, P * g:P * g + P], pen_s[:, c:c + w], start=False, stop=True,
                                       skip_group_check=True)
                    mm.then_inc(s_s_logits, 1)

                def turn_probs(g):
                    pe.wait_ge(s_s_norm, g + 1)
                    pe.wait_ge(s_kt_copied, 24 if g == 0 else 32)
                    for i in range(8):
                        pe.transpose(ps(5, 2)[:, P * i:P * i + P], s_prob[:, NS * g + P * i:NS * g + P * i + P], ident)
                    new = PAST * (1 - g)
                    pe.transpose(ps(2)[0:NS, P:2 * P], s_prob[:, new:new + NS], ident).then_inc(s_s_pt, 1)

                def sample_values(b):
                    g, r0 = b // 4, NS * (b % 4)
                    pe.wait_ge(s_s_ptc, g + 1)
                    pe.wait_ge(v_in[b], 16 * PAGES)
                    for p in range(2):
                        out = ps(7)[:, NS * (2 * b + p):NS * (2 * b + p) + NS]
                        for pg in range(PAGES):
                            pe.matmul(out, v_pages(b)[:, pg, P * p:P * p + P], s_pt[g][:, pg, r0:r0 + NS], start=(pg == 0), stop=False)
                        mm = pe.matmul(out, va[0:NS, 4, P * p:P * p + P], s_pt[g][0:NS, 8, r0:r0 + NS], start=False, stop=True)
                    mm.then_inc(s_s_pv, 1)

                pe.wait_ge(s_a_copied, 4)
                turn_keys(0)
                for b in range(5):
                    turn_keys(b + 1)
                    sample_logits(b)
                    if b == 3:
                        finish_logits(0)
                turn_probs(0)
                sample_logits(5)
                turn_keys(6)
                turn_keys(7)
                sample_logits(6)
                sample_logits(7)
                finish_logits(1)
                for b in range(DB):
                    if b == 4:
                        turn_probs(1)
                    sample_values(b)

                pe.wait_ge(s_mix_ready, 1)
                for m in range(8):
                    feature_tile(8 + m // 4, OUT0 + m, P * (m % 4), mixv)
                    if m >= 2:
                        sum_squares(s_sq2, m - 2)
                sum_squares(s_sq2, KT - 2)
                sum_squares(s_sq2, KT - 1).then_inc(s_sum2, 1)
                for f in range(FT):
                    feature_tile(10 + f // 2, FFN0 + 2 * f, P * (f % 2), xnv)
                    feature_tile(10 + f // 2, FFN0 + 2 * f + 1, 2 * P + P * (f % 2), xnv)
                pe.wait_ge(s_up_free, FT)
                for m in range(KT):
                    feature_tile(10 + FT // 2 + m, DOWN0 + m, 0, hid)
        def vector_layer(block, l):
            @block.vector
            def _(dve):
                chain = [0]

                def step(ins):
                    chain[0] += 1
                    ins.then_inc(s_dve_chain, 1)
                    dve.wait_ge(s_dve_chain, chain[0])

                def spread(ap, shape, at):
                    return ap.unsqueeze(at).broadcast_to(shape)

                dve.wait_ge(s_conv_state_turned, 1)
                dve.tensor_copy(convst[:, :], ps(7)[:, 0:192])
                dve.tensor_copy(vT[:, :], ps(6)[:, 0:80]).then_inc(s_vec_copied, 1)
                dve.wait_ge(s_vec_copied, 1)

                def apply_norm(rstd, g0, ready):
                    for k in range(KT):
                        ins = dve.scalar_tensor_tensor(out=xnv[:, k, :], in0=xv[:, k, :], scalar=vT[:, g0 + k:g0 + k + 1],
                                                       in1=rstd, op0=ALU.mult, op1=ALU.mult)
                        ins.then_inc(ready, 1)

                rstd = R4[:, 0:T]
                dve.wait_ge(s_rstd1, 1)
                apply_norm(rstd, 32, s_xn_ready)

                dve.wait_ge(s_out_free, 1)
                dve.tensor_copy(qi[:, 0:4, 8, :], g80[:, 0:4, 8:72])
                dve.tensor_copy(qi[0:NS, 4, 8, :], g80[0:NS, 4, 8:72])
                dve.tensor_scalar(wP, g80[:, 0:4, 72:80], IH ** -0.5, None, ALU.mult)
                step(dve.tensor_scalar(g80[0:NS, 4, 72:80], g80[0:NS, 4, 72:80], IH ** -0.5, None, ALU.mult))
                dve.tensor_tensor(wx.rearrange("p (b h t) -> p b h t", b=DB, h=IH),
                                  const("rep", NS).rearrange("p (b h t) -> p b h t", b=DB, h=IH),
                                  g80[0:NS, 4, 72:80].unsqueeze(1).unsqueeze(3).broadcast_to([NS, DB, IH, DT]),
                                  ALU.mult).then_inc(s_w_spread, 1)

                def rope(buf, h0, nh, tmp):
                    for tiles, r in ((slice(0, 4), P), (slice(4, 5), NS)):
                        nt = 4 if r == P else 1
                        a = buf[0:r, tiles, h0:h0 + nh, 0:32]
                        b = buf[0:r, tiles, h0:h0 + nh, 32:64]
                        cos, sin = (const(n, r).rearrange("p (t d) -> p t d", t=5)[:, tiles, :].unsqueeze(2).broadcast_to([r, nt, nh, 32])
                                    for n in ("cos", "sin"))
                        n = nt * nh * 32
                        as_, bs = (tmp[0:r, i * n:(i + 1) * n].rearrange("p (t h d) -> p t h d", t=nt, h=nh) for i in range(2))
                        dve.tensor_tensor(as_, a, sin, ALU.mult)
                        step(dve.tensor_tensor(bs, b, sin, ALU.mult))
                        dve.tensor_tensor(a, a, cos, ALU.mult)
                        step(dve.tensor_tensor(b, b, cos, ALU.mult))
                        dve.tensor_tensor(a, a, bs, ALU.subtract)
                        step(dve.tensor_tensor(b, b, as_, ALU.add))

                dve.wait_ge(s_out_free, 4)
                rope(qi, 0, 9, R4)
                dve.tensor_copy(qi[:, 0:4, 9, :], qi[:, 0:4, 8, :]).then_inc(s_qi_roped, 1)

                dve.wait_ge(s_gate_turned, 1)
                dve.wait_ge(s_gate_in, 16 * 4)
                dve.tensor_scalar(gr[:, 0, :], ps(4, 2)[0:MH, 0:T], bgate[:, 0:1], None, ALU.add)
                dve.tensor_scalar(gr[:, 1, :], ps(6, 2)[0:MH, 0:T], bgate[:, 1:2], None, ALU.add).then_inc(s_gate_read, 1)
                dve.wait_ge(s_gate_read, 1)
                dve.wait_ge(s_gate_log, 1)
                step(dve.scalar_tensor_tensor(out=gr[:, 1, :], in0=gr[:, 1, :], scalar=0.0, in1=gr[:, 2, :],
                                              op0=ALU.min, op1=ALU.subtract))
                step(dve.tensor_tensor_scan(gr[:, 2, :], rm, gr[:, 1, :], 0.0, ALU.mult, ALU.add))
                step(dve.tensor_tensor(gr[:, 0, :], gr[:, 0, :], gr[:, 2, :], ALU.subtract))
                step(dve.tensor_copy(gr[:, 1, :], gr[:, 0, :]))

                def seqs(row):
                    return row[:, SEQ:T].rearrange("p (b t) -> p b t", b=DB)

                first = seqs(gr[:, 1, :])[:, :, 0]
                step(dve.tensor_tensor(first, first, m0T, ALU.max))
                step(dve.tensor_tensor_scan(gr[:, 3, :], ra, gr[:, 1, :], 0.0, ALU.add, ALU.max))
                dve.tensor_tensor(gr[:, 6, :], gr[:, 2, :], gr[:, 3, :], ALU.add)
                step(dve.tensor_scalar(negM[:, :], gr[:, 3, :], -1.0, None, ALU.mult))
                dve.tensor_copy(mrow[:, 0:1], gr[:, 6, SEQ - 1:SEQ])
                dve.tensor_copy(mrow[:, 1:9], seqs(gr[:, 6, :])[:, :, 3])
                dve.tensor_tensor(winter.rearrange("p (b t) -> p b t", b=DB), seqs(negM[:, :]),
                                  m0T.unsqueeze(2).broadcast_to([MH, DB, DT]), ALU.add)
                dve.tensor_tensor(seqs(gr[:, 5, :]), seqs(gr[:, 0, :]),
                                  seqs(negM[:, :])[:, :, 3].unsqueeze(2).broadcast_to([MH, DB, DT]), ALU.add).then_inc(s_gate_rows_ready, 1)
                dve.wait_ge(s_gate_cols_turned, 1)
                dve.tensor_copy(gcols[:, 0:48], ps(6)[:, 0:48])
                dve.tensor_copy(gcols[0:NS, 48:64], ps(6)[0:NS, 48:64])
                dve.tensor_copy(decT, ps(6)[0:DB, 64:68]).then_inc(s_gate_cols_ready, 1)

                for n in range(3 * IH):
                    j, h = n // IH + 1, n % IH
                    dve.wait_ge(s_relu_done, n + 1)
                    acc = penv[:, j - 1, 0:(j + 1) * P]
                    part = relu_p[:, n % 2, 0:(j + 1) * P]
                    if h == 0:
                        ins = dve.tensor_scalar(acc, part, wP[:, j, h:h + 1], None, ALU.mult)
                    else:
                        ins = dve.scalar_tensor_tensor(out=acc, in0=part, scalar=wP[:, j, h:h + 1], in1=acc, op0=ALU.mult, op1=ALU.add)
                    ins.then_inc(s_relu_free, 1)
                    dve.wait_ge(s_relu_free, n + 1)
                    if h == IH - 1:
                        dve.sem_inc(s_scored, 1)

                def pick(scores, rows, topk):
                    for _ in range(topk // 8):
                        step(dve.max(m8[0:rows, :], scores))
                        step(dve.match_replace(scores, m8[0:rows, :], scores, GONE))
                    step(dve.tensor_scalar(scores, scores, GONE / 2, NEG, ALU.is_gt, ALU.mult))

                for j in (1, 2, 3):
                    dve.wait_ge(s_masked, j)
                    pick(penv[:, j - 1, 0:(j + 1) * P], P, TOPK_P)

                dve.wait_ge(s_out_free, 10)
                dve.wait_ge(s_g_in, 16 * 3)
                for t, (_, r) in enumerate(TILES):
                    sq = rawr[0:r, 0:768].rearrange("p (h d) -> p h d", h=12)
                    step(dve.tensor_tensor(sq, qk[0:r, t, :, :], qk[0:r, t, :, :], ALU.mult))
                    ins = dve.tensor_reduce(small_ss[0:r, t, :], sq, AX.X, ALU.add)
                    step(ins)
                dve.sem_inc(s_qk_sums, 1)
                dve.wait_ge(s_qk_rstd, 1)
                for t, (_, r) in enumerate(TILES):
                    step(dve.tensor_tensor(qk[0:r, t, :, :], qk[0:r, t, :, :],
                                           small_ss[0:r, t, :].unsqueeze(2).broadcast_to([r, 12, HD]), ALU.mult))
                    dve.tensor_tensor(qk[0:r, t, 0:8, :], qk[0:r, t, 0:8, :],
                                      gqk[0:r, 0:HD].unsqueeze(1).broadcast_to([r, 8, HD]), ALU.mult)
                    step(dve.tensor_tensor(qk[0:r, t, 8:12, :], qk[0:r, t, 8:12, :],
                                           gqk[0:r, HD:2 * HD].unsqueeze(1).broadcast_to([r, 4, HD]), ALU.mult))
                for h0 in (0, 4, 8):
                    rope(qk, h0, 4, rawr)
                dve.sem_inc(s_qk_ready, 1)

                dve.wait_ge(s_sscore, 1)
                dve.tensor_copy(pen_s[:, 0:PAST], ps(4, 2)[0:NS, :])
                dve.tensor_tensor(pen_s[:, PAST:KEYS], ps(7)[0:NS, 0:NS], const("newpen", NS), ALU.add).then_inc(s_sscore_copied, 1)
                dve.wait_ge(s_sscore_copied, 1)

                def pick_sample(rounds):
                    for _ in range(rounds):
                        step(dve.max(m8[0:NS, :], pen_s[:, :]))
                        step(dve.match_replace(pen_s[:, :], m8[0:NS, :], pen_s[:, :], GONE))

                for m in range(8):
                    r_ = raw[m]
                    hist = r_[:, 3 + SEQ:571].rearrange("p (b c) -> p b c", b=DB)
                    step(dve.tensor_copy(hist[:, :, 0:3], convst[:, 24 * m:24 * m + 24].rearrange("p (b j) -> p b j", b=DB)))
                    dve.wait_ge(s_out_free, CONV0 + m + 1)
                    if m == 0:
                        dve.wait_ge(s_raw_zeroed, 1)
                    for j in range(4):
                        w = vT[:, 8 * j + m:8 * j + m + 1]
                        for out, src in ((cqv[:, m, 0:SEQ], r_[:, j:j + SEQ]), (seqs(cqv[:, m, :]), hist[:, :, j:j + DT])):
                            if j == 0:
                                ins = dve.tensor_scalar(out, src, w, None, ALU.mult)
                            else:
                                ins = dve.scalar_tensor_tensor(out=out, in0=src, scalar=w, in1=out, op0=ALU.mult, op1=ALU.add)
                        if j < 3:
                            step(ins)
                    ins.then_inc(s_conv_z, 1)
                    dve.tensor_copy(tails[:, 27 * m:27 * m + 3], r_[:, SEQ:SEQ + 3])
                    dve.tensor_copy(tails[:, 27 * m + 3:27 * m + 27].rearrange("p (b j) -> p b j", b=DB), hist[:, :, 4:7]).then_inc(s_conv_done, 1)
                    if m < 7:
                        pick_sample(1)

                def columns(t, rows, q):
                    return acol[0:rows, t, q, :]

                for t, (_, r) in enumerate(TILES):
                    dve.wait_ge(s_ktok_turned, t + 1)
                    if t == 0:
                        dve.wait_ge(s_out_done, OUT0)
                    dve.tensor_tensor(kw[0:r, t, :, :], ps(2 + t % 2)[0:r, :].rearrange("p (h d) -> p h d", h=MH),
                                      columns(t, r, 2).unsqueeze(2).broadcast_to([r, MH, P]), ALU.mult).then_inc(s_ktok_copied, 1)
                dve.wait_ge(s_s_small, 1)
                for h in range(MH):
                    ins = dve.tensor_scalar(sds[:, h, :], ps(4)[0:NS, P + NS * h:P + NS * h + NS], acol[0:NS, 4, 0, h:h + 1], 0.0, ALU.add, ALU.min)
                ins.then_inc(s_s_dt, 1)
                dve.tensor_copy(dec_bc, ps(4)[:, 2 * P:2 * P + NS]).then_inc(s_dec_copied, 1)
                dve.wait_ge(s_cq_done, 8)
                dve.tensor_copy(cqs, ps(6)[:, 0:P]).then_inc(s_cq_copied, 1)
                dve.wait_ge(s_s_de, 1)
                step(dve.tensor_tensor(sds, sds, ps(4)[0:NS, 0:P].rearrange("p (h t) -> p h t", h=MH), ALU.mult))
                dve.tensor_tensor(sds, sds, const("bcm", NS).unsqueeze(1).broadcast_to([NS, MH, NS]), ALU.mult).then_inc(s_s_sd, 1)
                wi = gcols[0:NS, 60:64]
                nqm = R4[0:NS, 0:NS].rearrange("p (h b) -> p h b", h=MH)
                step(dve.tensor_tensor(nqm, ps(7)[0:NS, 0:NS].rearrange("p (h b) -> p h b", h=MH),
                                       const("blk", NS).unsqueeze(1).broadcast_to([NS, MH, DB]), ALU.mult))
                step(dve.tensor_reduce(den[0:NS, 4, :], nqm, AX.X, ALU.add))
                step(dve.tensor_tensor(den[0:NS, 4, :], den[0:NS, 4, :], wi, ALU.mult))
                dve.wait_ge(s_cq_turned, 1)
                dve.wait_ge(s_kv_stored, 16 * 8)
                step(dve.tensor_tensor(htok[0:NS, 4, :, :], ps(5)[0:NS, :].rearrange("p (h d) -> p h d", h=MH),
                                       wi.unsqueeze(2).broadcast_to([NS, MH, P]), ALU.mult))
                dve.wait_ge(s_s_num, 1)
                num_s = ps(2, 2)[0:NS, :].rearrange("p (h c) -> p h c", h=MH)
                step(dve.tensor_tensor(den[0:NS, 4, :], den[0:NS, 4, :], num_s[:, :, P], ALU.add))
                dve.tensor_tensor(htok[0:NS, 4, :, :], htok[0:NS, 4, :, :], num_s[:, :, 0:P], ALU.add).then_inc(s_s_num_read, 1)
                for h in range(MH):
                    dve.wait_ge(s_c_decayed, h + 1)
                    dve.wait_ge(s_u_sum, h + 1)
                    dve.tensor_tensor(c0[:, :, h, :], c0[:, :, h, :], ps(2 * (h % 2), 2).rearrange("p (b d) -> p b d", b=DB), ALU.add).then_inc(s_c_new, 1)
                dve.wait_ge(s_n0_in, 16)
                nr = nrow.rearrange("p (h d) -> p h d", h=MH)
                step(dve.tensor_tensor(nr, nr, decT.unsqueeze(2).broadcast_to([DB, MH, P]), ALU.mult))
                dve.wait_ge(s_n_sum, 1)
                dve.tensor_tensor(nr, nr, ps(5)[0:DB, :].rearrange("p (h d) -> p h d", h=MH), ALU.add).then_inc(s_n_new, 1)

                def decays(n):
                    h, s = n // 4, n % 4
                    dve.wait_ge(s_negm_bc, h + 1)
                    if n >= 2:
                        dve.wait_ge(s_sd, n - 1)
                    dve.tensor_scalar(dtmp[:, n % 2, P * s:SEQ], ps(h % 2)[:, P * s:SEQ], acol[:, s, 0, h:h + 1], 0.0,
                                      ALU.add, ALU.min).then_inc(s_dtmp_ready, 1)

                def values(h):
                    dve.wait_ge(s_num, h + 1)
                    out = ps(4 + 2 * (h % 2), 2).rearrange("p (t c) -> p t c", t=4)
                    d, nq = den[:, 0:4, h], out[:, :, P]
                    step(dve.tensor_copy(d, nq))
                    step(dve.scalar_tensor_tensor(out=d, in0=d, scalar=-1.0, in1=nq, op0=ALU.mult, op1=ALU.max))
                    step(dve.tensor_tensor(d, d, acol[:, 0:4, 1, h], ALU.max))
                    step(dve.reciprocal(d, d))
                    dve.tensor_tensor(htok[:, 0:4, h, :], out[:, :, 0:P], d.unsqueeze(2).broadcast_to([P, 4, P]), ALU.mult).then_inc(s_num_read, 1)

                decays(0)
                for n in range(4 * MH):
                    h, s = n // 4, n % 4
                    if n + 1 < 4 * MH:
                        decays(n + 1)
                    dve.wait_ge(s_dexp, n + 1)
                    dve.wait_ge(s_mem_s, n + 1)
                    if s == 0 and h >= 1:
                        dve.wait_ge(s_num, h)
                    dve.tensor_tensor(sd[:, s, P * s:SEQ], dtmp[:, n % 2, P * s:SEQ], ps(2 + n % 2)[:, 0:SEQ - P * s], ALU.mult).then_inc(s_sd, 1)
                    if s == 1 and h >= 1:
                        values(h - 1)
                values(MH - 1)
                d = den[0:NS, 4, :]
                neg = small[0:NS, 356:360]
                step(dve.tensor_scalar(neg, d, -1.0, None, ALU.mult))
                step(dve.tensor_tensor(d, d, neg, ALU.max))
                step(dve.tensor_tensor(d, d, columns(4, NS, 1), ALU.max))
                step(dve.reciprocal(d, d))
                step(dve.tensor_tensor(htok[0:NS, 4, :, :], htok[0:NS, 4, :, :], d.unsqueeze(2).broadcast_to([NS, MH, P]), ALU.mult))
                for t, (_, r) in enumerate(TILES):
                    s = R4[0:r, 0:512].rearrange("p (h d) -> p h d", h=MH)
                    step(dve.tensor_tensor(s, htok[0:r, t, :, :], htok[0:r, t, :, :], ALU.mult))
                    ins = dve.tensor_reduce(hss[0:r, t, :], s, AX.X, ALU.add)
                    if t == 4:
                        ins.then_inc(s_hsq, 1)
                        dve.wait_ge(s_hsq, 1)
                    else:
                        step(ins)
                    step(dve.tensor_tensor(mo[0:r, t, :], mo[0:r, t, :], gmout[0:r, :], ALU.mult))
                dve.wait_ge(s_hrstd, 1)
                for t, (_, r) in enumerate(TILES):
                    step(dve.tensor_tensor(htok[0:r, t, :, :], htok[0:r, t, :, :], hss[0:r, t, :].unsqueeze(2).broadcast_to([r, MH, P]), ALU.mult))
                    ins = dve.tensor_tensor(htok[0:r, t, :, :].rearrange("p h d -> p (h d)"), htok[0:r, t, :, :].rearrange("p h d -> p (h d)"), mo[0:r, t, :], ALU.mult)
                    if t == 4:
                        ins.then_inc(s_hn_ready, 1)
                    else:
                        step(ins)

                for i in range(2):
                    ins = dve.tensor_copy(k_twice[:, :, :, i, :], qk[:, 0:4, 8:12, :])
                ins.then_inc(s_k_twice_ready, 1)
                dve.wait_ge(s_s_turned, 1)
                step(dve.memset(kiT[:, :], 0.0))
                for h in range(QH):
                    r0, src, p = HD * (h // 2 % 2), HD * (h % 2), h // 4
                    dve.tensor_copy(s_q[r0:r0 + HD, p, :, DT * h:DT * h + DT],
                                    ps(6)[src:src + HD, NS * (h // 2):NS * (h // 2) + NS].rearrange("p (b t) -> p b t", b=DB))
                dve.tensor_copy(kTnew.rearrange("p g s -> p (g s)"), ps(7)[:, 0:2 * NS]).then_inc(s_s_q_ready, 1)
                dve.wait_ge(s_mix_turned, MH)

                def copy_out(j):
                    dve.wait_ge(s_a_turned, j + 1)
                    dve.tensor_copy(mixv[:, 4:8, P * j:P * j + P], ps(6).rearrange("p (f t) -> p f t", f=4)).then_inc(s_a_copied, 1)

                for n in range(4 * QH + 1):
                    if n < 4 * QH:
                        j, h = n // QH, n % QH
                        w = (j + 1) * P
                        dve.wait_ge(s_a_s, n + 1)
                        if n >= 3:
                            dve.wait_ge(s_pt_turned, n - 2)
                        mask = const("pen0") if j == 0 else penv[:, j - 1, 0:w]
                        step(dve.tensor_tensor_reduce(a_score[:, n % 3, 0:w], ps(n % 2)[:, 0:w], mask, 1.0, GONE, ALU.add, ALU.max,
                                                      a_neg[:, 4 + n % 4:5 + n % 4]))
                        dve.tensor_scalar(a_neg[:, n % 4:n % 4 + 1], a_neg[:, 4 + n % 4:5 + n % 4], -HD ** -0.5, None, ALU.mult)\
                           .then_inc(s_a_max, 1)
                    if 7 <= n < 4 * QH:
                        pick_sample(1)
                    elif n == 4 * QH:
                        dve.tensor_scalar(pen_s[:, :], pen_s[:, :], GONE / 2, NEG, ALU.is_gt, ALU.mult).then_inc(s_sample_mask, 1)
                    if n >= QH and n % QH == 2 or n == 4 * QH:
                        j = n // QH - 1
                        dve.wait_ge(s_pv, QH * (j + 1))
                        dve.wait_ge(s_a_p, QH * (j + 1))
                        step(dve.reciprocal(a_sum[:, j % 2, :], a_sum[:, j % 2, :]))
                        if j >= 1:
                            dve.wait_ge(s_a_turned, j)
                        dve.tensor_tensor(atok.rearrange("p (h d) -> p h d", h=QH), ps(4 + j % 2).rearrange("p (h d) -> p h d", h=QH),
                                          a_sum[:, j % 2, :].unsqueeze(2).broadcast_to([P, QH, HD]), ALU.mult).then_inc(s_a_tok, 1)
                        if j >= 1:
                            copy_out(j - 1)
                copy_out(3)
                for g in range(2):
                    dve.wait_ge(s_s_logits, g + 1)
                    step(dve.tensor_reduce(s_max[:, 2:3], s_logit[g], AX.X, ALU.max))
                    dve.tensor_scalar(s_max[:, 0:1], s_max[:, 2:3], -HD ** -0.5, None, ALU.mult).then_inc(s_s_neg, 1)
                    dve.wait_ge(s_s_exp, g + 1)
                    step(dve.reciprocal(s_max[:, 1:2], s_max[:, 1:2]))
                    dve.tensor_scalar(s_prob, s_prob, s_max[:, 1:2], None, ALU.mult).then_inc(s_s_norm, 1)
                dve.wait_ge(s_s_pv, DB)
                for h in range(QH):
                    p, src, dst = h // 4, HD * (h // 2 % 2), HD * (h % 2)
                    ins = dve.tensor_copy(seqs(mixv[dst:dst + HD, 4 + h // 2, :]),
                                          ps(7)[src:src + HD, :].rearrange("p (b g c) -> p b g c", b=DB, g=2)[:, :, p, DT * h:DT * h + DT])
                ins.then_inc(s_mix_ready, 1)

                def halves(n):
                    dve.wait_ge(s_out_done, n + 1)
                    return ps(2 * (n % 2), 2).rearrange("p (h t) -> p h t", h=2)[:, :, 0:HALF]

                for m in range(KT):
                    v = xv[:, m, :].rearrange("p (h t) -> p h t", h=2)
                    dve.tensor_tensor(v, v, halves(OUT0 + m), ALU.add).then_inc(s_out_free, 1)
                dve.wait_ge(s_out_free, OUT0 + KT)
                dve.wait_ge(s_rstd2, 1)
                apply_norm(R4[:, 0:T], 40, s_xn2_ready)
                dve.wait_ge(s_xn2_ready, KT)
                for f in range(FT):
                    dve.wait_ge(s_gate_silu, f + 1)
                    dve.tensor_tensor(hid[:, f, :].rearrange("p (h t) -> p h t", h=2), sig(f), halves(FFN0 + 2 * f + 1), ALU.mult).then_inc(s_up_free, 1)
                dve.wait_ge(s_up_free, FT)
                for m in range(KT):
                    v = xv[:, m, :].rearrange("p (h t) -> p h t", h=2)
                    dve.tensor_tensor(v, v, halves(DOWN0 + m), ALU.add).then_inc(s_out_free, 1)
                dve.wait_ge(s_out_free, FFN0 + KT)
        xtok = proj[:, 0:5 * D].rearrange("p (t d) -> p t d", t=5)
        with nc.Block() as block:

            @block.sync
            def _(sp):
                sp.dma_start(con[:, :], A["consts"][:, :]).then_inc(s_const_in, 16)
                sp.dma_start(xtok[:, 0:4, :], A["x_prompt"][0, :, :].rearrange("(t p) d -> p t d", p=P)).then_inc(s_x_in, 16)
                sp.dma_start(xtok[0:NS, 4, :], A["x_sample"][:, :, :].rearrange("b t d -> (b t) d")).then_inc(s_x_in, 16)
                sp.dma_start(pages[:, :], A["page_table"][:, :].rearrange("(a b) g -> a (b g)", a=1)).then_inc(s_x_in, 16)

            @block.tensor
            def _(pe):
                pe.wait_ge(s_const_in, 16)
                pe.wait_ge(s_x_in, 48)
                for k in range(KT):
                    if k >= 4:
                        pe.wait_ge(s_x_copied, k - 3)
                    for t, (c, r) in enumerate(TILES):
                        mm = pe.transpose(ps(2 * (k % 4), 2)[:, c:c + r], xtok[0:r, t, P * k:P * k + P], ident[0:r, 0:r])
                    mm.then_inc(s_x_turned, 1)

            @block.vector
            def _(dve):
                dve.memset(eps[:, :], EPS)
                for k in range(KT):
                    dve.wait_ge(s_x_turned, k + 1)
                    dve.tensor_copy(xv[:, k, :], ps(2 * (k % 4), 2)[:, 0:T]).then_inc(s_x_copied, 1)
                dve.wait_ge(s_x_copied, KT)

        with nc.Fori(0, DEPTH) as l:
            with nc.Block() as layer:
                sync_layer(layer, l)
                pool_layer(layer, l)
                act_layer(layer, l)
                tensor_layer(layer, l)
                vector_layer(layer, l)
            nc.all_engine_barrier()
            for s in layer_semaphores:
                nc.sync.sem_clear(s)
            nc.all_engine_barrier()

        with nc.Block() as block:
            @block.tensor
            def _(pe):
                for t, (c, r) in enumerate(TILES):
                    if t >= 4:
                        pe.wait_ge(s_y_copied, t - 3)
                    for k in range(KT):
                        mm = pe.transpose(ps(2 * (t % 4), 2)[0:r, P * k:P * k + P], xv[:, k, c:c + r], ident)
                    mm.then_inc(s_y_turned, 1)

            @block.vector
            def _(dve):
                for t, (c, r) in enumerate(TILES):
                    dve.wait_ge(s_y_turned, t + 1)
                    dve.tensor_copy(xtok[0:r, t, :], ps(2 * (t % 4), 2)[0:r, :]).then_inc(s_y_copied, 1)

            @block.sync
            def _(sp):
                for t, (c, r) in enumerate(TILES):
                    sp.wait_ge(s_y_copied, t + 1)
                    dst = O["y_p"][0, c:c + r, :] if t < 4 else O["y_s"][:, :, :].rearrange("b t d -> (b t) d")
                    sp.dma_start(dst, xtok[0:r, t, :]).then_inc(s_y_stored, 16)
                sp.wait_ge(s_y_stored, 16 * 5)

_OUTS = [("y_p", (1, SEQ, D)), ("y_s", (DB, DT, D)),
         ("k_p", (DEPTH, 1, SEQ, KVH, HD)), ("v_p", (DEPTH, 1, SEQ, KVH, HD)), ("kidx_p", (DEPTH, 1, SEQ, HD)),
         ("C_p", (DEPTH, 1, MH, P, P)), ("n_p", (DEPTH, 1, MH, P)), ("m_p", (DEPTH, 1, MH)), ("conv_p", (DEPTH, 1, 3, 1024)),
         ("k_s", (DEPTH, DB, DT, KVH, HD)), ("v_s", (DEPTH, DB, DT, KVH, HD)), ("kidx_s", (DEPTH, DB, DT, HD)),
         ("C_s", (DEPTH, DB, MH, P, P)), ("n_s", (DEPTH, DB, MH, P)), ("m_s", (DEPTH, DB, MH)), ("conv_s", (DEPTH, DB, 3, 1024))]
_INS = ["x_prompt", "x_sample", "cache_k", "cache_v", "cache_kidx", "page_table", "state_C", "state_n", "state_m", "state_conv",
        "g_mix", "w_in", "conv_w", "b_gate", "g_mout", "g_q", "g_k", "w_out", "g_ffn", "w_gate_up", "w_down"]


def _constants():
    import numpy as np
    c = np.zeros((P, NCONST), np.float32)

    def put(name, value):
        a, n = CAT[name]
        c[:value.shape[0], a:a + n] = value.reshape(value.shape[0], n)

    put("ident", np.eye(P))
    put("ones", np.ones((P, P)))
    half = HD // 2
    inv = np.float32(10000.0) ** (-np.arange(half, dtype=np.float32) / np.float32(half))
    pos = np.concatenate([np.arange(SEQ), np.tile(PAST + np.arange(DT), DB), np.zeros(P - NS)]).astype(np.float32)
    ang = (pos[:, None] * inv[None, :]).astype(np.float32)
    tiles = ang.reshape(5, P, half).transpose(1, 0, 2)
    put("cos", np.cos(tiles))
    put("sin", np.sin(tiles))
    row = np.arange(NS)
    same = row[:, None] // DT == row[None, :] // DT
    put("bcm", (same & (row[:, None] <= row[None, :])).astype(np.float32))
    put("newpen", np.where(same & (row[None, :] <= row[:, None]), 0.0, NEG))
    put("blk", (row[:, None] // DT == np.arange(DB)[None, :]).astype(np.float32))
    wide = np.arange(2 * P)
    put("rep", ((wide[None, :] // NS == row[:, None] // DT) & (wide[None, :] % DT == row[:, None] % DT)).astype(np.float32))
    put("sel", (np.arange(MH)[:, None] == np.arange(MH * P)[None, :] // P).astype(np.float32))
    put("pen0", np.where(np.arange(P)[None, :] <= np.arange(P)[:, None], 0.0, NEG))
    rows = np.zeros((MH, 2 * T), np.float32)
    rows[:, 0:T] = 1.0
    rows[:, SEQ:T:DT] = 0.0
    rows[:, T + SEQ::DT] = GONE
    return c, rows


def kernel(**inputs):
    import numpy as np
    import concourse.bacc as bacc
    from concourse.bass_utils import run_bass_kernel_spmd

    nc = bacc.Bacc("TRN2", target_bir_lowering=False, num_devices=1)
    data = {n: np.ascontiguousarray(inputs[n]) for n in _INS}
    for n in ("cache_k", "cache_v"):
        data[n] = data[n].reshape(DEPTH * POOL, PAGE, KVH * HD)
    data["cache_kidx"] = data["cache_kidx"].reshape(DEPTH * POOL, PAGE, HD)
    data["consts"], data["gate_rows"] = _constants()
    arrays, A, O = {}, {}, {}
    for n, a in data.items():
        arrays[f"in_{n}_dram"] = a
        A[n] = nc.dram_tensor(f"in_{n}_dram", a.shape, mybir.dt.from_np(a.dtype), kind="ExternalInput").ap()
    for n, shape in _OUTS:
        O[n] = nc.dram_tensor(f"out_{n}_dram", shape, F32, kind="ExternalOutput").ap()
    build(nc, A, O)
    r = run_bass_kernel_spmd(nc, [arrays], core_ids=[0])
    return tuple(r.results[0][f"out_{n}_dram"] for n, _ in _OUTS)
```

```python
from contextlib import ExitStack

import concourse.bass as bass
from concourse import mybir

F32 = mybir.dt.float32
F32R = mybir.dt.float32r
I32 = mybir.dt.int32
ACT = mybir.ActivationFunctionType
ALU = mybir.AluOpType
AX = mybir.AxisListType

P = 128
D = 1024
KT = D // P
SEQ = 512
DB, DT = 8, 4
NS = DB * DT
T = SEQ + NS
HALF = T // 2
DEPTH = 2
PAGE = 128
PAGES = 8
PAST = PAGE * PAGES
POOL = DB * PAGES * 5 // 4
MH = 4
KVH, QH, IH, HD = 4, 8, 8, 64
DFF = 2816
FT = DFF // P
EPS = 1e-6
NEG = -1e30
GONE = -3e38
KEYS = PAST + NS
TOPK_P, TOPK_S = 128, 256
PICKS_CONV, PICKS_PROMPT = 7, 21
TILES = [(0, P), (P, P), (2 * P, P), (3 * P, P), (SEQ, NS)]
MQ, MK, MV, MO, MI, AQ, AK, IQ, IK = 0, 512, 1024, 1536, 2048, 2056, 2568, 3080, 3592
SLABS = ([("small", 0, 80)]
         + [("tok", c, 512) for c in (IQ, AQ, AK, MV, MO)]
         + [("conv", MQ, 512), ("conv", MK, 512)]
         + [("out", 0, 512), ("out", 512, 512)] + [("ffn", 256 * j, 256) for j in range(FT // 2)]
         + [("down", P * j, P) for j in range(KT)])
CONV0 = 1 + 5 * 3
OUT0 = CONV0 + 8
FFN0 = OUT0 + 8
DOWN0 = FFN0 + 2 * FT
SLOTS = {"small": 1, "tok": 3, "conv": 4, "out": 4, "ffn": 4, "down": 1}


def slots_before(i):
    return sum(SLOTS[kind] for kind, _, _ in SLABS[:i])


STORES = 2 + DB + 1 + 2
CONST = [("ident", P), ("ones", P), ("cos", 160), ("sin", 160), ("bcm", NS), ("blk", DB), ("rep", 2 * P),
         ("sel", MH * P), ("newpen", NS), ("pen0", P)]
CAT = {}
NCONST = 0
for _name, _n in CONST:
    CAT[_name] = (NCONST, _n)
    NCONST += _n


def build(nc, A, O):
    ctx = ExitStack()
    with ctx:
        def sb(name, cols, rows=P, dt=F32):
            return ctx.enter_context(nc.sbuf_tensor(name, [rows, cols], dt))

        layer_semaphores = []

        def sem(name, layer=True):
            s = ctx.enter_context(nc.semaphore(name))
            if layer:
                layer_semaphores.append(s)
            return s

        s_kpage_in0 = sem("kpage_in0")
        s_kpage_in1 = sem("kpage_in1")
        s_kpage_in2 = sem("kpage_in2")
        s_kpage_in3 = sem("kpage_in3")
        s_kpage_in4 = sem("kpage_in4")
        s_kpage_in5 = sem("kpage_in5")
        s_kpage_in6 = sem("kpage_in6")
        s_kpage_in7 = sem("kpage_in7")
        s_vpage_in0 = sem("vpage_in0")
        s_vpage_in1 = sem("vpage_in1")
        s_vpage_in2 = sem("vpage_in2")
        s_vpage_in3 = sem("vpage_in3")
        s_vpage_in4 = sem("vpage_in4")
        s_vpage_in5 = sem("vpage_in5")
        s_vpage_in6 = sem("vpage_in6")
        s_vpage_in7 = sem("vpage_in7")
        s_slab_in_even = sem("slab_in_even")
        s_slab_in_odd = sem("slab_in_odd")
        s_vec_in = sem("vec_in")
        s_out_done = sem("out_done")
        s_kipage_in0 = sem("kipage_in0")
        s_kipage_in1 = sem("kipage_in1")
        s_gate_in = sem("gate_in")
        s_g_in = sem("g_in")
        s_conv_state_turned = sem("conv_state_turned")
        s_kiturn = sem("kiturn")
        s_sscore = sem("sscore")
        s_c0_in = sem("c0_in")
        s_qi_roped = sem("qi_roped")
        s_kv_stored = sem("kv_stored")
        s_out_free = sem("out_free")
        s_qk_ready = sem("qk_ready")
        s_gate_rows_ready = sem("gate_rows_ready")
        s_n0_in = sem("n0_in")
        s_tail_copied = sem("tail_copied")
        s_stored = sem("stored")
        s_c_new = sem("c_new")
        s_n_new = sem("n_new")
        s_c_copied = sem("c_copied")
        s_mix_turned = sem("mix_turned")
        s_qt_turned = sem("qt_turned")
        s_a_s = sem("a_s")
        s_kt_turned = sem("kt_turned")
        s_s_pv = sem("s_pv")
        s_ones_set = sem("ones_set")
        s_relu_free = sem("relu_free")
        s_masked = sem("masked")
        s_raw_zeroed = sem("raw_zeroed")
        s_mo_scaled = sem("mo_scaled")
        s_s_q_zeroed = sem("s_q_zeroed")
        s_conv_silu = sem("conv_silu")
        s_k_scaled = sem("k_scaled")
        s_kmask_ready = sem("kmask_ready")
        s_ktok_copied = sem("ktok_copied")
        s_cq_done = sem("cq_done")
        s_dec_copied = sem("dec_copied")
        s_c_decayed = sem("c_decayed")
        s_sd = sem("sd")
        s_sd_masked = sem("sd_masked")
        s_u_sum = sem("u_sum")
        s_act_chain = sem("act_chain")
        s_sq2 = sem("sq2")
        s_conv_z = sem("conv_z")
        s_sq1 = sem("sq1")
        s_sum1 = sem("sum1")
        s_rstd1 = sem("rstd1")
        s_gate_read = sem("gate_read")
        s_gate_log = sem("gate_log")
        s_gate_exps = sem("gate_exps")
        s_idx_turned = sem("idx_turned")
        s_idx_copied = sem("idx_copied")
        s_dots = sem("dots")
        s_relu_done = sem("relu_done")
        s_sdots = sem("sdots")
        s_kicopy = sem("kicopy")
        s_srelu = sem("srelu")
        s_snew = sem("snew")
        s_qk_sums = sem("qk_sums")
        s_qk_rstd = sem("qk_rstd")
        s_tail_turned = sem("tail_turned")
        s_c0_turned = sem("c0_turned")
        s_c0_copied = sem("c0_copied")
        s_s_dt = sem("s_dt")
        s_s_de = sem("s_de")
        s_head_squared = sem("head_squared")
        s_dtmp_ready = sem("dtmp_ready")
        s_dexp = sem("dexp")
        s_num_read = sem("num_read")
        s_hrstd = sem("hrstd")
        s_c_sum = sem("c_sum")
        s_qt_copied = sem("qt_copied")
        s_mix_copied = sem("mix_copied")
        s_a_max = sem("a_max")
        s_a_tok = sem("a_tok")
        s_a_p = sem("a_p")
        s_pt_turned = sem("pt_turned")
        s_pv = sem("pv")
        s_pt_copied = sem("pt_copied")
        s_s_log = sem("s_log")
        s_kt_copied = sem("kt_copied")
        s_s_neg = sem("s_neg")
        s_s_exp = sem("s_exp")
        s_s_pt = sem("s_pt")
        s_s_ptc = sem("s_ptc")
        s_sum2 = sem("sum2")
        s_rstd2 = sem("rstd2")
        s_up_free = sem("up_free")
        s_gate_silu = sem("gate_silu")
        s_high_copied = sem("high_copied")
        s_low_ready = sem("low_ready")
        s_hid_split = sem("hid_split")
        s_down_split = sem("down_split")
        s_down_used = sem("down_used")
        s_w_split = sem("w_split")
        s_xn2_split = sem("xn2_split")
        s_xn_ready = sem("xn_ready")
        s_vec_copied = sem("vec_copied")
        s_gate_turned = sem("gate_turned")
        s_w_spread = sem("w_spread")
        s_gate_cols_turned = sem("gate_cols_turned")
        s_gate_cols_ready = sem("gate_cols_ready")
        s_conv_done = sem("conv_done")
        s_ktok_turned = sem("ktok_turned")
        s_sscore_copied = sem("sscore_copied")
        s_s_small = sem("s_small")
        s_cq_copied = sem("cq_copied")
        s_cq_turned = sem("cq_turned")
        s_s_sd = sem("s_sd")
        s_s_num = sem("s_num")
        s_s_num_read = sem("s_num_read")
        s_n_sum = sem("n_sum")
        s_negm_bc = sem("negm_bc")
        s_mem_s = sem("mem_s")
        s_num = sem("num")
        s_s_turned = sem("s_turned")
        s_hn_ready = sem("hn_ready")
        s_k_twice_ready = sem("k_twice_ready")
        s_s_q_ready = sem("s_q_ready")
        s_a_copied = sem("a_copied")
        s_a_turned = sem("a_turned")
        s_sample_mask = sem("sample_mask")
        s_s_logits = sem("s_logits")
        s_s_rows_ready = sem("s_rows_ready")
        s_s_rows_turned = sem("s_rows_turned")
        s_mix_ready = sem("mix_ready")
        s_dve_chain = sem("dve_chain")
        s_const_in = sem("const_in", layer=False)
        s_x_in = sem("x_in", layer=False)
        s_x_turned = sem("x_turned", layer=False)
        s_x_copied = sem("x_copied", layer=False)
        s_y_turned = sem("y_turned", layer=False)
        s_y_copied = sem("y_copied", layer=False)
        s_y_stored = sem("y_stored", layer=False)

        x = sb("x", KT * T)
        ring = sb("ring", 2 * 4096)
        rawr = sb("rawr", 3 * 571)
        kiT = sb("kiT", SEQ)
        pen = sb("pen", 3 * SEQ)
        pen_s = sb("pen_s", KEYS, NS)
        con = sb("con", NCONST)
        gmout = sb("gmout", 512)
        gqk = sb("gqk", 2 * HD)
        vec = sb("vec", P, 80)
        vT = sb("vT", 80)
        convst = sb("convst", 8 * 24)
        tails = sb("tails", 8 * 27)
        negM = sb("negM", T, MH)
        gcols = sb("gcols", 64)
        small = sb("small", 400)
        tiny = sb("tiny", 64, 8)
        pages = sb("pages", DB * PAGES, 1, I32)
        with ExitStack() as mixing:
            proj, xn, cq, qk2, R4 = (mixing.enter_context(nc.sbuf_tensor(name, [P, cols], F32)) for name, cols in (
                ("proj", 13860),
                ("xn", KT * T),
                ("cq", KT * T),
                ("qk2", 4096),
                ("R4", 4224)))
        h_high, x_high, x_low, w_split_even, w_split_odd = (ctx.enter_context(nc.sbuf_tensor(name, [P, cols], F32R)) for name, cols in (
            ("h_high", 13860), ("x_high", KT * T), ("x_low", KT * T), ("w_split_even", 4096), ("w_split_odd", 4096)))
        psum = ctx.enter_context(nc.psum_tensor("psum", [P, 8 * 512], F32))

        def ps(bank, n=1):
            return psum[:, 512 * bank:512 * (bank + n)]

        def const(name, rows=P):
            a, n = CAT[name]
            return con[0:rows, a:a + n]

        ident, ones = const("ident"), const("ones")
        xv = x[:, :].rearrange("p (k t) -> p k t", k=KT)
        xnv = xn[:, :].rearrange("p (k t) -> p k t", k=KT)
        cqv = cq[:, :].rearrange("p (k t) -> p k t", k=KT)
        g80 = proj[:, 0:400].rearrange("p (t c) -> p t c", t=5)
        qi = proj[:, 400:3600].rearrange("p (t h d) -> p t h d", t=5, h=10)
        qk = proj[:, 3600:7440].rearrange("p (t h d) -> p t h d", t=5, h=12)
        va = proj[:, 7440:8720].rearrange("p (t c) -> p t c", t=5)
        mv = proj[:, 8720:11300].rearrange("p (t h c) -> p t h c", t=5, h=MH)
        mo = proj[:, 11300:13860].rearrange("p (t c) -> p t c", t=5)
        hid = proj[:, 0:FT * T].rearrange("p (f t) -> p f t", f=FT)
        htok = proj[:, 400:2960].rearrange("p (t h d) -> p t h d", t=5, h=MH)
        kw = xn[:, 0:2560].rearrange("p (t h d) -> p t h d", t=5, h=MH)
        raw = [rawr[:, 571 * m:571 * m + 571] if m < 3 else R4[:, 1369 + 571 * (m - 3):1369 + 571 * (m - 2)] for m in range(8)]
        qiT = qk2[:, 0:2048].rearrange("p (g t) -> p g t", g=4)
        kiTb = qk2[0:HD, 2048:4096].rearrange("p (s c) -> p s c", s=2)
        c0 = qk2[:, :].rearrange("p (b h d) -> p b h d", b=DB, h=MH)
        qT = qk2[:, 0:2048].rearrange("p (g t) -> p g t", g=4)
        kT2 = qk2[:, 2048:4096].rearrange("p (g t) -> p g t", g=4)
        penv = pen[:, :].rearrange("p (j s) -> p j s", j=3)
        gr = cq[0:MH, 0:7 * T].rearrange("p (r t) -> p r t", r=7)
        rm, ra = pen[0:MH, 0:T], pen[0:MH, T:2 * T]
        relu_p = R4[:, 0:1024].rearrange("p (s c) -> p s c", s=2)
        relu_s = R4[:, 0:2 * KEYS].rearrange("p (g c) -> p g c", g=2)
        ki_pages = R4[:, 2400:3424].rearrange("p (s g d) -> p s g d", s=2, g=PAGES)
        wx = R4[0:NS, 3500:3756]
        sd = [buf.rearrange("p (s t) -> p s t", s=4) for buf in (R4[:, 0:2048], ring[:, 4096:6144])]
        dtmp = R4[:, 2048:3072].rearrange("p (s t) -> p s t", s=2)
        ct = R4[:, 3072:4096].rearrange("p (s t) -> p s t", s=2)
        kmask = R4[0:NS, 3072:4096]
        wP = small[:, 0:32].rearrange("p (t h) -> p t h", t=4)
        wS = small[:, 32:96].rearrange("p (g c) -> p g c", g=2)
        qiTs = small[0:HD, 96:352].rearrange("p (b c) -> p b c", b=DB)
        kiTs = small[0:HD, 352:384]
        eps = small[:, 392:393]
        m8 = small[:, 384:392]
        mixv = xnv
        tail_rows = xn[0:27, 2560:3584]
        nrow = xn[0:DB, 3584:4096]
        c_end, n_end = R4[:, 3072:3584], R4[0:1, 3584:4096]
        sds = small[0:NS, 0:P].rearrange("p (h t) -> p h t", h=MH)
        cqs, dec_bc = small[:, P:2 * P], small[:, 256:288]
        den = small[:, 288:308].rearrange("p (t h) -> p t h", t=5)
        hss = small[:, 308:328].rearrange("p (t h) -> p t h", t=5)
        a_score = proj[:, 400:1936].rearrange("p (s c) -> p s c", s=3)
        a_pt = proj[:, 1936:2960].rearrange("p (s c) -> p s c", s=2)
        atok = rawr[:, 1152:1664]
        a_neg = small[:, 328:336]
        a_sum = small[:, 336:352].rearrange("p (s h) -> p s h", s=2)
        s_stat = small[:, 352:357]
        s_rows = [proj[:, c:c + 256] for c in (12976, 13232)]
        s_q = kiT[:, :].rearrange("p (g b c) -> p g b c", g=2, b=DB)
        kTnew = small[:, 0:64].rearrange("p (g s) -> p g s", g=2)
        k_twice = xn[:, KT * T - 2048:KT * T].rearrange("p (t h i d) -> p t h i d", t=4, h=KVH, i=2)
        kTb = [proj[:, c:c + 2048].rearrange("p (g s) -> p g s", g=2) for c in (8720, 400)]
        s_prob = proj[:, 10768:11824]
        s_pt = [buf.rearrange("p (g c) -> p g c", g=9) for buf in (proj[:, 11824:12976], rawr[:, 0:1152])]
        s_value = (ps(7)[:, 0:256], ps(0)[:, 0:256])
        s_logit = (psum[:, 0:KEYS], psum[:, 3 * 512 - NS:3 * 512 - NS + KEYS])
        small_ss = rawr[:, 1024:1084].rearrange("p (t h) -> p t h", t=5)
        m0T = tiny[0:MH, 0:8]
        bgate = tiny[0:MH, 8:10]
        mrow = tiny[0:MH, 46:55]
        winter = tiny[0:MH, 10:42]
        decT = tiny[0:8, 42:46]
        acol = gcols[:, 0:60].rearrange("p (t q h) -> p t q h", t=5, q=3)

        def logit_parts(g, turned):
            c = NS * g
            return ((s_logit[g][:, c:c + 512], turned[:, :, 0:512]), (s_logit[g][:, c + 512:c + PAST], turned[:, :, 512:PAST]),
                    (s_logit[g][:, PAST * (1 - g):PAST * (1 - g) + NS], kTnew))

        def halves_of(buf):
            return [buf[:, c:c + 2048] for c in (0, 2048)]

        (first0, first1), (cq0, cq1), (qk0, qk1) = (halves_of(buf) for buf in (ring[:, 0:4096], cq, qk2))
        spare0, spare1 = proj[:, 5392:7440], proj[:, 3344:5392]
        K_PLACE = (first0, first1, cq0, cq1, spare0, qk0, cq0, first0)
        V_PLACE = halves_of(ring[:, 4096:8192]) + halves_of(R4) + [spare1, qk1, cq1, spare0]

        def k_pages(b):
            return K_PLACE[b].rearrange("p (g c) -> p g c", g=PAGES)

        def v_pages(b):
            return V_PLACE[b].rearrange("p (g c) -> p g c", g=PAGES)

        k_in = (s_kpage_in0, s_kpage_in1, s_kpage_in2, s_kpage_in3, s_kpage_in4, s_kpage_in5, s_kpage_in6, s_kpage_in7)
        v_in = (s_vpage_in0, s_vpage_in1, s_vpage_in2, s_vpage_in3, s_vpage_in4, s_vpage_in5, s_vpage_in6, s_vpage_in7)

        def sig(f):
            return rawr[:, T * (f % 2):T * (f % 2) + T].rearrange("p (h t) -> p h t", h=2)

        def w_part(f, part):
            w = (w_split_even if f % 2 == 0 else w_split_odd)[:, 2048 * part:2048 * part + 2048]
            return w.rearrange("p (k u c) -> p k u c", k=KT, u=2)

        xh = x_high[:, :].rearrange("p (k t) -> p k t", k=KT)
        xl = x_low[:, :].rearrange("p (k t) -> p k t", k=KT)
        rstd_ffn = pen[:, 0:T]
        hh = h_high[:, 0:FT * T].rearrange("p (f t) -> p f t", f=FT)

        def hid_low(f):
            buf, c = (x_high, T * f) if f < 8 else (x_low, T * (f - 8)) if f < 16 else (w_split_odd, T * (f - 16))
            return buf[:, c:c + T]

        def down_part(c, part):
            at = 512 * (c % 8) + 256 * part
            return w_split_even[:, at:at + 256]

        CHUNKS = FT // 2

        def slab_view(i):
            kind, _, n = SLABS[i]
            base = 4096 * (i % 2)
            nk = FT if kind == "down" else KT
            cols = 512 if kind == "ffn" else n
            return ring[:, base:base + nk * cols].rearrange("p (k n) -> p k n", k=nk)

        def slab_arrived(eng, i):
            pieces = sum(2 if SLABS[j][0] in ("small", "ffn") else 1 for j in range(i % 2, i + 1, 2))
            eng.wait_ge(s_slab_in_even if i % 2 == 0 else s_slab_in_odd, 16 * pieces)

        def sync_layer(block, l):
            @block.sync
            def _(sp):
                w_in, w_out, w_gu, w_down = (A[n][bass.ds(l, 1), :, :] for n in ("w_in", "w_out", "w_gate_up", "w_down"))
                lay = bass.ds(l, 1)

                sp.dma_start(vec[0:32, :], A["conv_w"][lay, :, :].rearrange("a j (m p) -> (a j m) p", p=P)).then_inc(s_vec_in, 16)
                sp.dma_start(vec[32:40, :], A["g_mix"][lay, :].rearrange("a (k p) -> (a k) p", p=P)).then_inc(s_vec_in, 16)
                sp.dma_start(vec[40:48, :], A["g_ffn"][lay, :].rearrange("a (k p) -> (a k) p", p=P)).then_inc(s_vec_in, 16)
                sp.dma_start(vec[48:80, :], A["state_n"][lay, :, :, :].rearrange("a b h d -> (a b h) d")).then_inc(s_vec_in, 16)
                sp.dma_start(R4[0:24, 3072:4096], A["state_conv"][lay, :, :, :].rearrange("a b j c -> (a b j) c")).then_inc(s_vec_in, 16)

                def load_slab(i):
                    kind, c, n = SLABS[i]
                    sem = s_slab_in_even if i % 2 == 0 else s_slab_in_odd
                    dst = slab_view(i)
                    if i >= 2:
                        sp.wait_ge(s_out_done, slots_before(i - 1))
                    if kind == "small":
                        for a, b, c in ((0, 8, MI), (8, 80, IK)):
                            sp.dma_start(dst[:, :, a:b], w_in[:, :, c:c + b - a].rearrange("a (k p) n -> p (a k) n", p=P)).then_inc(sem, 16)
                    elif kind == "ffn":
                        for a, c in ((0, c), (256, DFF + c)):
                            sp.dma_start(dst[:, :, a:a + 256], w_gu[:, :, c:c + 256].rearrange("a (k p) n -> p (a k) n", p=P)).then_inc(sem, 16)
                    else:
                        w = {"tok": w_in, "conv": w_in, "out": w_out, "down": w_down}[kind]
                        sp.dma_start(dst, w[:, :, c:c + n].rearrange("a (k p) n -> p (a k) n", p=P)).then_inc(sem, 16)

                def page(i):
                    return bass.ds(l * POOL + sp.value_load(pages[0:1, i:i + 1], min_val=0, max_val=POOL - 1), 1)

                def load_index_keys(b):
                    for g in range(PAGES):
                        src = A["cache_kidx"][page(b * PAGES + g), :, :].rearrange("a p d -> p (a d)")
                        sp.dma_start(ki_pages[:, b % 2, g, :], src).then_inc(s_kipage_in0 if b % 2 == 0 else s_kipage_in1, 16)

                load_slab(0)
                load_slab(1)
                sp.dma_start(pen[0:MH, 0:2 * T], A["gate_rows"][:, :]).then_inc(s_gate_in, 16)
                sp.dma_start(m0T, A["state_m"][lay, :, :].rearrange("a b h -> h (a b)"), allow_slow_non_contiguous=True).then_inc(s_gate_in, 16)
                sp.dma_start(bgate[:, 0:1], A["b_gate"][lay, 0:MH].rearrange("a h -> h a"), allow_slow_non_contiguous=True).then_inc(s_gate_in, 16)
                sp.dma_start(bgate[:, 1:2], A["b_gate"][lay, MH:2 * MH].rearrange("a h -> h a"), allow_slow_non_contiguous=True).then_inc(s_gate_in, 16)
                sp.dma_start(gqk[:, 0:HD], A["g_q"][lay, :].partition_broadcast(P).rearrange("p a n -> p (a n)")).then_inc(s_g_in, 16)
                sp.dma_start(gqk[:, HD:2 * HD], A["g_k"][lay, :].partition_broadcast(P).rearrange("p a n -> p (a n)")).then_inc(s_g_in, 16)
                sp.dma_start(gmout[:, :], A["g_mout"][lay, :].partition_broadcast(P).rearrange("p a n -> p (a n)")).then_inc(s_g_in, 16)
                sp.wait_ge(s_conv_state_turned, 1)
                load_index_keys(0)
                load_index_keys(1)
                for i in range(2, 6):
                    load_slab(i)
                for b in range(2, DB):
                    sp.wait_ge(s_kiturn, 2 * b - 2)
                    load_index_keys(b)
                    if b == 6:
                        load_slab(6)
                load_slab(7)
                sp.wait_ge(s_sscore, 1)
                for b in range(DB):
                    sp.dma_start(c0[:, b, :, :], A["state_C"][lay, b, :, :, :].rearrange("a h v d -> v (a h) d")).then_inc(s_c0_in, 16)
                sp.wait_ge(s_qi_roped, 1)
                sp.dma_start(O["kidx_p"][lay, 0, :, :].rearrange("a (t p) d -> p (a t) d", p=P), qi[:, 0:4, 8, :]).then_inc(s_kv_stored, 16)
                sp.dma_start(O["kidx_s"][lay, :, :, :].rearrange("a b t d -> (a b t) d"), qi[0:NS, 4, 8, :]).then_inc(s_kv_stored, 16)
                sp.wait_ge(s_out_free, 10)
                sp.dma_start(O["v_p"][lay, 0, :, :, :].rearrange("a (t p) h d -> p (a t) (h d)", p=P), va[:, 0:4, :]).then_inc(s_kv_stored, 16)
                sp.dma_start(O["v_s"][lay, :, :, :, :].rearrange("a b t h d -> (a b t) (h d)"), va[0:NS, 4, :]).then_inc(s_kv_stored, 16)
                sp.wait_ge(s_qk_ready, 1)
                sp.dma_start(O["k_p"][lay, 0, :, :, :].rearrange("a (t p) h d -> p (a t) (h d)", p=P), qk[:, 0:4, 8:12, :].rearrange("p t h d -> p t (h d)")).then_inc(s_kv_stored, 16)
                sp.dma_start(O["k_s"][lay, :, :, :, :].rearrange("a b t h d -> (a b t) (h d)"), qk[0:NS, 4, 8:12, :].rearrange("p h d -> p (h d)")).then_inc(s_kv_stored, 16)
                sp.wait_ge(s_gate_rows_ready, 1)
                sp.dma_start(O["m_p"][lay, 0, :].rearrange("a h -> h a"), mrow[:, 0:1], allow_slow_non_contiguous=True).then_inc(s_kv_stored, 16)
                sp.dma_start(O["m_s"][lay, :, :].rearrange("a b h -> h (a b)"), mrow[:, 1:9], allow_slow_non_contiguous=True).then_inc(s_kv_stored, 16)
                sp.wait_ge(s_out_done, OUT0)
                sp.dma_start(nrow, A["state_n"][lay, :, :, :].rearrange("a b h d -> (a b) (h d)")).then_inc(s_n0_in, 16)

                def load_pages(b, names):
                    for g in range(PAGES):
                        at = page(b * PAGES + g)
                        for name in names:
                            buf, sem = (k_pages(b), k_in[b]) if name == "cache_k" else (v_pages(b), v_in[b])
                            sp.dma_start(buf[:, g, :], A[name][at, :, :].rearrange("a p d -> p (a d)")).then_inc(sem, 16)

                def load_both(b):
                    load_pages(b, ("cache_k", "cache_v"))

                sp.wait_ge(s_tail_copied, 1)
                sp.dma_start(O["conv_p"][lay, 0, :, :].rearrange("a j c -> (a j) c"), tail_rows[0:3, :]).then_inc(s_stored, 16)
                sp.dma_start(O["conv_s"][lay, :, :, :].rearrange("a b j c -> (a b j) c"), tail_rows[3:27, :]).then_inc(s_stored, 16)
                load_pages(0, ("cache_k",))
                load_pages(1, ("cache_k",))
                sp.wait_ge(s_c_new, MH)
                for b in range(DB):
                    sp.dma_start(O["C_s"][lay, b, :, :, :].rearrange("a h v d -> v (a h) d"), c0[:, b, :, :]).then_inc(s_stored, 16)
                sp.wait_ge(s_n_new, 1)
                sp.dma_start(O["n_s"][lay, :, :, :].rearrange("a b h d -> (a b) (h d)"), nrow).then_inc(s_stored, 16)
                sp.wait_ge(s_c_copied, 1)
                sp.dma_start(O["C_p"][lay, 0, :, :, :].rearrange("a h v d -> v (a h) d"), c_end.rearrange("p (h d) -> p h d", h=MH)).then_inc(s_stored, 16)
                sp.dma_start(O["n_p"][lay, 0, :, :].rearrange("a h d -> a (h d)"), n_end).then_inc(s_stored, 16)
                sp.wait_ge(s_stored, 16 * STORES)
                sp.wait_ge(s_kv_stored, 16 * 8)
                sp.wait_ge(s_mix_turned, MH)
                load_both(2)
                load_both(3)
                load_pages(0, ("cache_v",))
                load_pages(1, ("cache_v",))
                sp.wait_ge(s_qt_turned, 8)
                load_both(4)
                sp.wait_ge(s_a_s, 4 * QH)
                load_both(5)
                sp.wait_ge(s_kt_turned, 4)
                load_pages(7, ("cache_k",))
                sp.wait_ge(s_kt_turned, 4 * 4)
                load_both(6)
                sp.wait_ge(s_kt_turned, 4 * 5)
                load_pages(7, ("cache_v",))
                sp.wait_ge(s_kt_turned, 4 * DB)
                load_slab(8)
                sp.wait_ge(s_s_pv, 2)
                load_slab(9)
                for i in range(10, len(SLABS)):
                    load_slab(i)
        def pool_layer(block, l):
            @block.gpsimd
            def _(pool):
                pool.memset(mv[:, 0:4, :, P:P + 1], 1.0)
                pool.memset(mv[0:NS, 4, :, P:P + 1], 1.0).then_inc(s_ones_set, 1)
                for j in range(3):
                    pool.wait_ge(s_relu_free, IH * (j + 1))
                    blk = penv[:, j, (j + 1) * P:(j + 2) * P]
                    pool.affine_select(out=blk, in_=blk, compare_op=ALU.is_ge, fill=NEG, base=0,
                                       pattern=[[-1, P]], channel_multiplier=1).then_inc(s_masked, 1)
                pool.wait_ge(s_qk_ready, 1)
                pool.wait_ge(s_sscore, 1)
                for m in range(8):
                    ins = pool.memset(raw[m][:, 0:3], 0.0)
                ins.then_inc(s_raw_zeroed, 1)
                pool.wait_ge(s_out_free, CONV0)
                pool.wait_ge(s_g_in, 16 * 3)
                pool.tensor_tensor(mo[:, 0:4, :], mo[:, 0:4, :], gmout[:, :].unsqueeze(1).broadcast_to([P, 4, 512]), ALU.mult)
                pool.tensor_tensor(mo[0:NS, 4, :], mo[0:NS, 4, :], gmout[0:NS, :], ALU.mult).then_inc(s_mo_scaled, 1)
                pool.memset(kiT[:, :], 0.0).then_inc(s_s_q_zeroed, 1)
                for m in range(MH, 2 * MH):
                    pool.wait_ge(s_conv_silu, m + 1)
                    pool.tensor_scalar(cqv[:, m, :], cqv[:, m, :], P ** -0.5, None, ALU.mult).then_inc(s_k_scaled, 1)
                def mask_keys(h):
                    pool.tensor_tensor(kmask.rearrange("p (b d) -> p b d", b=DB), kw[0:NS, 4, h, :].unsqueeze(1).broadcast_to([NS, DB, P]),
                                       const("blk", NS).unsqueeze(2).broadcast_to([NS, DB, P]), ALU.mult).then_inc(s_kmask_ready, 1)

                pool.wait_ge(s_ktok_copied, 5)
                pool.wait_ge(s_cq_done, 8)
                mask_keys(0)
                pool.wait_ge(s_dec_copied, 1)
                for h in range(MH):
                    pool.tensor_tensor(c0[:, :, h, :], c0[:, :, h, :], dec_bc[:, DB * h:DB * h + DB].unsqueeze(2).broadcast_to([P, DB, P]), ALU.mult)\
                        .then_inc(s_c_decayed, 1)
                for n in range(4 * MH):
                    s = n % 4
                    pool.wait_ge(s_sd, n + 1)
                    blk = sd[n // 4 % 2][:, s, P * s:P * s + P]
                    pool.affine_select(out=blk, in_=blk, compare_op=ALU.is_ge, fill=0.0, base=0,
                                       pattern=[[1, P]], channel_multiplier=-1).then_inc(s_sd_masked, 1)
                    if s == 3 and n < 4 * MH - 1:
                        pool.wait_ge(s_u_sum, n // 4 + 1)
                        mask_keys(n // 4 + 1)
        def act_layer(block, l):
            @block.scalar
            def _(act):
                chain = [0]

                def step(ins):
                    chain[0] += 1
                    ins.then_inc(s_act_chain, 1)
                    act.wait_ge(s_act_chain, chain[0])

                def norm(squares, summed, rstd_ready, out):
                    for k in range(KT):
                        if squares is s_sq2:
                            act.wait_ge(s_out_free, OUT0 + k + 1)
                        act.activation(cqv[:, k, :], xv[:, k, :], ACT.Square).then_inc(squares, 1)
                    act.wait_ge(summed, 1)
                    step(act.activation(out, ps(4, 2).rearrange("p (h t) -> p h t", h=2)[:, :, 0:HALF], ACT.Ln,
                                        bias=eps[:, :], scale=1.0 / D))
                    act.activation(out, out, ACT.Exp, scale=-0.5).then_inc(rstd_ready, 1)

                def slot(n):
                    act.wait_ge(s_out_done, n + 1)
                    return ps(2 * (n % 2), 2)

                def token_slab(n, parts):
                    for i in range(3):
                        src = slot(n + i).rearrange("p (t c) -> p t c", t=2)
                        for c, m, dst in parts:
                            if i < 2:
                                ins = act.activation(dst[:, 2 * i:2 * i + 2], like(src[:, :, c:c + m], dst, 1), ACT.Copy)
                            else:
                                ins = act.activation(dst[0:NS, 4], like(src[0:NS, 0, c:c + m], dst, 0), ACT.Copy)
                        ins.then_inc(s_out_free, 1)

                def like(src, dst, free):
                    if len(dst.shape) == 3:
                        return src
                    if free:
                        return src.rearrange("p t (h d) -> p t h d", h=dst.shape[2])
                    return src.rearrange("p (h d) -> p h d", h=dst.shape[2])

                def token_group(n, i, m, dst, func):
                    src = slot(n + i).rearrange("p (t c) -> p t c", t=2)
                    if i < 2:
                        ins = act.activation(dst[:, 2 * i:2 * i + 2], like(src[:, :, 0:m], dst, 1), func)
                    else:
                        ins = act.activation(dst[0:NS, 4], like(src[0:NS, 0, 0:m], dst, 0), func)
                    ins.then_inc(s_out_free, 1)

                def conv_silu(m):
                    act.wait_ge(s_conv_z, m + 1)
                    act.activation(cqv[:, m, :], cqv[:, m, :], ACT.Silu).then_inc(s_conv_silu, 1)

                rstd = R4[:, 0:T].rearrange("p (h t) -> p h t", h=2)
                norm(s_sq1, s_sum1, s_rstd1, rstd)

                src = slot(0)[:, 0:400].rearrange("p (t c) -> p t c", t=5)
                act.activation(g80[:, 0:4, :], src[:, 0:4, :], ACT.Copy)
                act.activation(g80[0:NS, 4, :], src[0:NS, 4, :], ACT.Copy).then_inc(s_out_free, 1)
                token_slab(1, [(0, 512, qi[:, :, 0:8, :])])
                token_slab(4, [(0, 512, qk[:, :, 0:8, :])])

                act.wait_ge(s_gate_read, 1)
                step(act.activation(gr[:, 2, :], gr[:, 1, :], ACT.Abs))
                step(act.activation(gr[:, 2, :], gr[:, 2, :], ACT.Exp, scale=-1.0))
                act.activation(gr[:, 2, :], gr[:, 2, :], ACT.Ln, bias=1.0).then_inc(s_gate_log, 1)
                act.wait_ge(s_gate_rows_ready, 1)
                act.activation(gr[:, 4, :], gr[:, 6, :], ACT.Exp, scale=-1.0)
                act.activation(gr[:, 5, 0:SEQ], gr[:, 0, 0:SEQ], ACT.Exp, bias=negM[:, SEQ - 1:SEQ])
                act.activation(gr[:, 5, SEQ:T], gr[:, 5, SEQ:T], ACT.Exp)
                act.activation(winter, winter, ACT.Exp).then_inc(s_gate_exps, 1)

                for i in range(5):
                    act.wait_ge(s_idx_turned, i + 1)
                    act.activation(qiT[:, i, :] if i < 4 else kiT[:, :], ps(4 + i % 2), ACT.Copy).then_inc(s_idx_copied, 1)
                act.wait_ge(s_idx_turned, 6)
                act.activation(qiTs.rearrange("p b (h t) -> p h b t", h=IH),
                               ps(6)[0:HD, 0:256].rearrange("p (h b t) -> p h b t", h=IH, b=DB), ACT.Copy)
                act.activation(kiTs, ps(6)[0:HD, 256:288], ACT.Copy)
                act.activation(wS, ps(7)[:, 0:64].rearrange("p (g c) -> p g c", g=2), ACT.Copy).then_inc(s_idx_copied, 1)

                token_slab(7, [(0, 256, qk[:, :, 8:12, :]), (256, 256, va)])

                for n in range(3 * IH):
                    j = n // IH + 1
                    act.wait_ge(s_dots, n + 1)
                    if n >= 2:
                        act.wait_ge(s_relu_free, n - 1)
                    act.activation(relu_p[:, n % 2, 0:(j + 1) * P], ps(4 + n % 2)[:, 0:(j + 1) * P], ACT.Relu,
                                   scale=HD ** -0.5).then_inc(s_relu_done, 1)

                for u in range(10):
                    if u < DB:
                        b = u
                        for hf in range(2):
                            act.wait_ge(s_kiturn, 2 * b + hf + 1)
                            if b >= 2:
                                act.wait_ge(s_sdots, 2 * (b - 2) + hf + 1)
                            act.activation(kiTb[:, b % 2, 512 * hf:512 * hf + 512], ps(6 + hf)[0:HD, :], ACT.Copy).then_inc(s_kicopy, 1)
                    if u % 5 in (1, 3, 4):
                        if u < 5:
                            token_group(10, u // 2, 512, mv[:, :, :, 0:P], ACT.Copy)
                        else:
                            token_group(13, (u - 5) // 2, 512, mo, ACT.Sigmoid)
                    if u in (3, 7):
                        act.wait_ge(s_sdots, 2 * u + 2)
                        if u == 3:
                            act.wait_ge(s_relu_free, 3 * IH)
                        act.activation(relu_s[:, u // 4, 0:PAST], ps(4, 2), ACT.Relu, scale=HD ** -0.5).then_inc(s_srelu, 1)
                act.wait_ge(s_snew, 1)
                act.activation(relu_s[:, :, PAST:KEYS], ps(6)[:, 0:64].rearrange("p (g c) -> p g c", g=2), ACT.Relu,
                               scale=HD ** -0.5).then_inc(s_srelu, 1)

                act.wait_ge(s_qk_sums, 1)
                parts = [small_ss[0:rows, t, :] for rows, t in ((P, slice(0, 4)), (NS, slice(4, 5)))]
                for part in parts:
                    ins = act.activation(part, part, ACT.Ln, bias=eps[0:part.shape[0], :], scale=1.0 / HD)
                step(ins)
                for part in parts:
                    ins = act.activation(part, part, ACT.Exp, scale=-0.5)
                ins.then_inc(s_qk_rstd, 1)

                for m in range(8):
                    src = slot(CONV0 + m).rearrange("p (h t) -> p h t", h=2)
                    if m == 0:
                        act.wait_ge(s_qk_ready, 1)
                    if m == 3:
                        act.wait_ge(s_sscore, 1)
                    r_ = raw[m]
                    act.activation(r_[:, 3:3 + HALF], src[:, 0, 0:HALF], ACT.Copy)
                    act.activation(r_[:, 3 + HALF:3 + SEQ], src[:, 1, 0:SEQ - HALF], ACT.Copy)
                    act.activation(r_[:, 3 + SEQ:571].rearrange("p (b c) -> p b c", b=DB)[:, :, 3:7],
                                   src[:, 1, SEQ - HALF:HALF].rearrange("p (b c) -> p b c", b=DB), ACT.Copy).then_inc(s_out_free, 1)
                    if m >= 2:
                        conv_silu(m - 2)
                conv_silu(6)
                conv_silu(7)
                act.wait_ge(s_tail_turned, 1)
                act.activation(tail_rows, ps(0, 2)[0:27, :], ACT.Copy).then_inc(s_tail_copied, 1)
                for g in range(8):
                    act.wait_ge(s_c0_turned, g + 1)
                    if g >= 2:
                        act.wait_ge(s_cq_done, g - 1)
                    act.activation(ct[:, g % 2, :], ps(g % 2), ACT.Copy).then_inc(s_c0_copied, 1)
                act.wait_ge(s_s_dt, 1)
                act.activation(sds.rearrange("p h t -> p (h t)"), sds.rearrange("p h t -> p (h t)"), ACT.Exp).then_inc(s_s_de, 1)

                def head_squares(h, rows, tiles):
                    if rows == P and h >= 2:
                        act.wait_ge(s_head_squared, h - 1)
                    for t in tiles:
                        at = P * (4 * (h % 2) + t if rows == P else 8 + h)
                        ins = act.activation(rawr[0:rows, at:at + P], htok[0:rows, t, h, :], ACT.Square, accum_out=hss[0:rows, t, h:h + 1])
                    ins.then_inc(s_head_squared, 1)

                for n in range(4 * MH):
                    act.wait_ge(s_dtmp_ready, n + 1)
                    d = dtmp[:, n % 2, P * (n % 4):SEQ]
                    act.activation(d, d, ACT.Exp).then_inc(s_dexp, 1)
                    if n % 4 == 3 and n >= 7:
                        act.wait_ge(s_num_read, n // 4)
                        head_squares(n // 4 - 1, P, range(4))
                act.wait_ge(s_num_read, MH)
                head_squares(MH - 1, P, range(4))
                act.wait_ge(s_num_read, MH + 1)
                for h in range(MH):
                    head_squares(h, NS, (4,))
                act.wait_ge(s_head_squared, 2 * MH)
                parts = [hss[0:rows, t, :] for rows, t in ((P, slice(0, 4)), (NS, slice(4, 5)))]
                for part in parts:
                    ins = act.activation(part, part, ACT.Ln, bias=eps[0:part.shape[0], :], scale=1.0 / P)
                step(ins)
                for part in parts:
                    ins = act.activation(part, part, ACT.Exp, scale=-0.5)
                ins.then_inc(s_hrstd, 1)
                act.wait_ge(s_c_sum, 1)
                act.activation(c_end, ps(2), ACT.Copy)
                act.activation(n_end, ps(3)[0:1, :], ACT.Copy).then_inc(s_c_copied, 1)

                act.wait_ge(s_c_new, MH)
                act.wait_ge(s_stored, 16 * STORES)
                for g in range(4):
                    act.wait_ge(s_qt_turned, g + 1)
                    act.activation(qT[:, g, :], ps(4 + g % 2), ACT.Copy).then_inc(s_qt_copied, 1)
                for h in range(MH):
                    act.wait_ge(s_mix_turned, h + 1)
                    act.activation(mixv[:, h, :], ps(2 * (h % 2), 2)[:, 0:T], ACT.Copy).then_inc(s_mix_copied, 1)
                for g in range(4, 8):
                    act.wait_ge(s_qt_turned, g + 1)
                    act.activation(kT2[:, g - 4, :], ps(4 + g % 2), ACT.Copy).then_inc(s_qt_copied, 1)
                for n in range(4 * QH + 1):
                    if n < 4 * QH:
                        j, h = n // QH, n % QH
                        w = (j + 1) * P
                        act.wait_ge(s_a_max, n + 1)
                        if h == 0 and j >= 2:
                            act.wait_ge(s_a_tok, j - 1)
                        act.activation(a_score[:, n % 3, 0:w], a_score[:, n % 3, 0:w], ACT.Exp, bias=a_neg[:, n % 4:n % 4 + 1],
                                       scale=HD ** -0.5, accum_out=a_sum[:, j % 2, h:h + 1]).then_inc(s_a_p, 1)
                    if n >= 1:
                        m = n - 1
                        w = (m // QH + 1) * P
                        act.wait_ge(s_pt_turned, m + 1)
                        if m >= 2:
                            act.wait_ge(s_pv, m - 1)
                        act.activation(a_pt[:, m % 2, 0:w], ps(2 + m % 2)[:, 0:w], ACT.Copy).then_inc(s_pt_copied, 1)
                def copy_keys(b):
                    for i in range(4):
                        act.wait_ge(s_kt_turned, 4 * b + i + 1)
                        if b >= 2 and i == 0:
                            act.wait_ge(s_s_log, b - 1)
                        act.activation(kTb[b % 2][:, i // 2, 512 * (i % 2):512 * (i % 2) + 512], ps(5 + i % 2), ACT.Copy).then_inc(s_kt_copied, 1)

                def sample_probs(g):
                    act.wait_ge(s_s_neg, g + 1)
                    act.activation(s_prob, s_logit[g], ACT.Exp, bias=s_stat[:, g:g + 1], scale=HD ** -0.5,
                                   accum_out=s_stat[:, 2 + g:3 + g]).then_inc(s_s_exp, 1)
                    act.wait_ge(s_s_pt, g + 1)
                    act.activation(s_pt[g][:, 0:8, :].rearrange("p g c -> p (g c)"), ps(5, 2), ACT.Copy)
                    act.activation(s_pt[g][0:NS, 8, :], ps(2)[0:NS, P:2 * P], ACT.Copy).then_inc(s_s_ptc, 1)

                for b in range(6):
                    copy_keys(b)
                sample_probs(0)
                copy_keys(6)
                copy_keys(7)
                sample_probs(1)

                norm(s_sq2, s_sum2, s_rstd2, rstd_ffn.rearrange("p (h t) -> p h t", h=2))
                for f in range(FT):
                    act.wait_ge(s_out_done, FFN0 + 2 * f + 1)
                    if f >= 2:
                        act.wait_ge(s_up_free, f - 1)
                    act.activation(sig(f), ps(0, 2).rearrange("p (h t) -> p h t", h=2)[:, :, 0:HALF], ACT.Silu).then_inc(s_gate_silu, 1)
                act.wait_ge(s_up_free, FT)
                for f in range(FT):
                    act.activation(hid_low(f), hid[:, f, :], ACT.Copy).then_inc(s_high_copied, 1)
                act.wait_ge(s_low_ready, FT)
                act.wait_ge(s_out_done, DOWN0 + 1)
                for f in range(FT):
                    act.activation(hh[:, f, :], hid[:, f, :], ACT.Copy).then_inc(s_hid_split, 1)
        def tensor_layer(block, l):
            @block.tensor
            def _(pe):
                def slot(n):
                    if n > FFN0 + 1 and n < DOWN0:
                        pe.wait_ge(s_up_free if n % 2 else s_gate_silu, (n - FFN0) // 2)
                    elif n >= DOWN0:
                        pe.wait_ge(s_out_free, n - 1 - 2 * FT)
                    elif n >= 2:
                        pe.wait_ge(s_out_free, n - 1)
                    return ps(2 * (n % 2), 2)

                def token_tile(i, n, t):
                    if t == 0:
                        slab_arrived(pe, i)
                    w = slab_view(i)
                    out = slot(n + t // 2) if t % 2 == 0 else ps(2 * ((n + t // 2) % 2), 2)
                    c, r = TILES[t]
                    for k in range(KT):
                        mm = pe.matmul(out[0:r, 512 * (t % 2):512 * (t % 2) + 512], xnv[:, k, c:c + r], w[:, k, :],
                                       start=(k == 0), stop=(k == KT - 1))
                    if t in (1, 3, 4):
                        mm.then_inc(s_out_done, 1)

                def token_slab(i, n):
                    for t in range(5):
                        token_tile(i, n, t)

                def feature_tile(i, n, c, src):
                    slab_arrived(pe, i)
                    w = slab_view(i)
                    nk = w.shape[1]
                    out = slot(n)
                    for k in range(nk):
                        for hf in range(2):
                            mm = pe.matmul(out[:, 512 * hf:512 * hf + HALF], w[:, k, c:c + P],
                                           src[:, k, HALF * hf:HALF * hf + HALF], start=(k == 0), stop=(k == nk - 1))
                    mm.then_inc(s_out_done, 1)

                def down_tile(m):
                    out = slot(DOWN0 + m)
                    for k in range(FT):
                        if m == 1:
                            pe.wait_ge(s_hid_split, k + 1)
                        c = CHUNKS * (m - 1) + k // 2
                        if k % 2 == 0:
                            pe.wait_ge(s_down_split, c + 1)
                        cols = slice(P * (k % 2), P * (k % 2) + P)
                        for q, (w, v) in enumerate(((0, hh[:, k, :]), (0, hid_low(k)), (1, hh[:, k, :]))):
                            for hf in range(2):
                                mm = pe.matmul(out[:, 512 * hf:512 * hf + HALF], down_part(c, w)[:, cols],
                                               v[:, HALF * hf:HALF * hf + HALF], start=(k == 0 and q == 0), stop=(k == FT - 1 and q == 2))
                        if k == FT - 1:
                            mm.then_inc(s_out_done, 1)
                        elif k % 2 == 1:
                            mm.then_inc(s_down_used, 1)

                def split_tile(f, u):
                    n = FFN0 + 2 * f + u
                    out = slot(n)
                    for k in range(KT):
                        if u == 0:
                            pe.wait_ge(s_w_split, 2 * f + 1 + k // 4)
                        if n == FFN0:
                            pe.wait_ge(s_xn2_split, k + 1)
                        for q, (w, v) in enumerate(((0, xh), (0, xl), (1, xh))):
                            for hf in range(2):
                                mm = pe.matmul(out[:, 512 * hf:512 * hf + HALF], w_part(f, w)[:, k, u, :],
                                               v[:, k, HALF * hf:HALF * hf + HALF],
                                               start=(k == 0 and q == 0), stop=(k == KT - 1 and q == 2))
                    mm.then_inc(s_out_done, 1)

                def sum_squares(squares, k):
                    pe.wait_ge(squares, k + 1)
                    for hf in range(2):
                        mm = pe.matmul(ps(4 + hf)[:, 0:HALF], ones, cqv[:, k, HALF * hf:HALF * hf + HALF],
                                       start=(k == 0), stop=(k == KT - 1))
                    return mm

                for k in range(KT):
                    mm = sum_squares(s_sq1, k)
                mm.then_inc(s_sum1, 1)
                pe.wait_ge(s_vec_in, 16 * 5)
                pe.transpose(ps(6)[:, 0:80], vec[0:80, :], ident[0:80, 0:80])
                for m in range(8):
                    mm = pe.transpose(ps(7)[:, 24 * m:24 * m + 24], R4[0:24, 3072 + P * m:3072 + P * m + P], ident[0:24, 0:24])
                mm.then_inc(s_conv_state_turned, 1)

                slab_arrived(pe, 0)
                out = slot(0)
                for t, (c, r) in enumerate(TILES):
                    for k in range(KT):
                        if t == 0:
                            pe.wait_ge(s_xn_ready, k + 1)
                        mm = pe.matmul(out[0:r, 80 * t:80 * t + 80], xnv[:, k, c:c + r], slab_view(0)[:, k, :],
                                       start=(k == 0), stop=(k == KT - 1))
                mm.then_inc(s_out_done, 1)
                token_slab(1, 1)
                pe.wait_ge(s_out_free, 1)
                pe.wait_ge(s_rstd1, 1)
                pe.wait_ge(s_vec_copied, 1)
                for q in range(2):
                    for c, r, t in [(c, r, t) for t, (c, r) in enumerate(TILES)]:
                        mm = pe.transpose(ps(4 + 2 * q, 2)[0:MH, c:c + r], g80[0:r, t, MH * q:MH * q + MH], ident[0:r, 0:r])
                mm.then_inc(s_gate_turned, 1)
                token_slab(2, 4)

                pe.wait_ge(s_qi_roped, 1)
                pe.wait_ge(s_gate_read, 1)
                for g in range(5):
                    if g >= 2:
                        pe.wait_ge(s_idx_copied, g - 1)
                    for t in range(4):
                        mm = pe.transpose(ps(4 + g % 2)[:, P * t:P * t + P], qi[:, t, 2 * g:2 * g + 2, :].rearrange("p h d -> p (h d)"), ident)
                    mm.then_inc(s_idx_turned, 1)
                for h in range(IH + 1):
                    pe.transpose(ps(6)[0:HD, NS * h:NS * h + NS], qi[0:NS, 4, h, :], ident[0:NS, 0:NS])
                pe.wait_ge(s_w_spread, 1)
                for g in range(2):
                    mm = pe.transpose(ps(7)[:, NS * g:NS * g + NS], wx[:, P * g:P * g + P], ident[0:NS, 0:NS])
                mm.then_inc(s_idx_turned, 1)
                token_slab(3, 7)

                pe.wait_ge(s_gate_exps, 1)
                pe.wait_ge(s_idx_copied, 6)
                for t, (c, r) in enumerate(TILES):
                    for q, row in enumerate((0, 4, 5)):
                        pe.transpose(ps(6)[0:r, 12 * t + MH * q:12 * t + MH * q + MH], gr[:, row, c:c + r], ident[0:MH, 0:MH])
                pe.transpose(ps(6)[0:NS, 60:64], winter, ident[0:MH, 0:MH])
                pe.transpose(ps(6)[0:DB, 64:68], winter.rearrange("p (b t) -> p b t", b=DB)[:, :, 3], ident[0:MH, 0:MH])\
                  .then_inc(s_gate_cols_turned, 1)

                for n in range(3 * IH):
                    j, h = n // IH + 1, n % IH
                    if n >= 2:
                        pe.wait_ge(s_relu_done, n - 1)
                    q0 = HD * (h % 2)
                    pe.matmul(ps(4 + n % 2)[:, 0:(j + 1) * P], qiT[q0:q0 + HD, h // 2, j * P:(j + 1) * P],
                              kiT[q0:q0 + HD, 0:(j + 1) * P], start=True, stop=True).then_inc(s_dots, 1)

                pe.wait_ge(s_gate_cols_ready, 1)
                pe.wait_ge(s_relu_done, 3 * IH)
                for u in range(10):
                    b = u
                    if b < DB:
                        pe.wait_ge(s_kipage_in0 if b % 2 == 0 else s_kipage_in1, 16 * PAGES * (b // 2 + 1))
                        for hf in range(2):
                            if b >= 1:
                                pe.wait_ge(s_kicopy, 2 * (b - 1) + hf + 1)
                            for g in range(4):
                                mm = pe.transpose(ps(6 + hf)[0:HD, PAGE * g:PAGE * g + PAGE], ki_pages[:, b % 2, 4 * hf + g, :], ident)
                            mm.then_inc(s_kiturn, 1)
                    token_tile(4 + u // 5, 10 + 3 * (u // 5), u % 5)
                    if b < DB:
                        r0 = NS * (b % 4)
                        if b == 4:
                            pe.wait_ge(s_srelu, 1)
                        for hf in range(2):
                            pe.wait_ge(s_kicopy, 2 * b + hf + 1)
                            pe.matmul(ps(4 + hf)[r0:r0 + NS, :], qiTs[:, b, :], kiTb[:, b % 2, 512 * hf:512 * hf + 512],
                                      start=True, stop=True).then_inc(s_sdots, 1)
                    if b == DB:
                        for b in range(DB):
                            r0 = NS * (b % 4)
                            mm = pe.matmul(ps(6)[r0:r0 + NS, NS * (b // 4):NS * (b // 4) + NS], qiTs[:, b, :], kiTs, start=True, stop=True)
                        mm.then_inc(s_snew, 1)

                for m in range(8):
                    feature_tile(6 + m // 4, CONV0 + m, P * (m % 4), xnv)
                    if m == 0:
                        for c, n, dst in ((0, 512, ps(4)), (512, 512, ps(5)), (PAST, NS, ps(7))):
                            pe.wait_ge(s_srelu, 3)
                            for g in range(2):
                                mm = pe.matmul(dst[0:NS, 0:n], wS[:, g, :], relu_s[:, g, c:c + n], start=(g == 0), stop=(g == 1))
                        mm.then_inc(s_sscore, 1)

                pe.wait_ge(s_out_free, OUT0)
                pe.wait_ge(s_conv_done, 8)
                for m in range(8):
                    mm = pe.transpose(ps(0, 2)[0:27, P * m:P * m + P], tails[:, 27 * m:27 * m + 27], ident)
                mm.then_inc(s_tail_turned, 1)
                pe.wait_ge(s_conv_silu, 8)
                pe.wait_ge(s_k_scaled, MH)
                for t, (c, r) in enumerate(TILES):
                    if t >= 2:
                        pe.wait_ge(s_ktok_copied, t - 1)
                    for h in range(MH):
                        mm = pe.transpose(ps(2 + t % 2)[0:r, P * h:P * h + P], cqv[:, MH + h, c:c + r], ident)
                    mm.then_inc(s_ktok_turned, 1)
                pe.wait_ge(s_c0_in, 16 * DB)
                pe.wait_ge(s_sscore_copied, 1)
                pe.wait_ge(s_tail_copied, 1)
                s0 = SEQ
                for g in range(9):
                    if g < 8:
                        h, b0 = g // 2, 4 * (g % 2)
                        if g >= 2:
                            pe.wait_ge(s_c0_copied, g - 1)
                        for i in range(4):
                            mm = pe.transpose(ps(g % 2)[:, P * i:P * i + P], c0[:, b0 + i, h, :], ident)
                        mm.then_inc(s_c0_turned, 1)
                    if g >= 1:
                        h, b0 = (g - 1) // 2, 4 * ((g - 1) % 2)
                        pe.wait_ge(s_c0_copied, g)
                        for i in range(4):
                            b = b0 + i
                            mm = pe.matmul(ps(6)[:, NS * h + DT * b:NS * h + DT * b + DT], ct[:, (g - 1) % 2, P * i:P * i + P],
                                           cqv[:, h, s0 + DT * b:s0 + DT * b + DT], start=True, stop=True)
                        mm.then_inc(s_cq_done, 1)
                for h in range(MH):
                    q, k = cqv[:, h, s0:T], cqv[:, MH + h, s0:T]
                    pe.matmul(ps(7)[0:NS, DB * h:DB * h + DB], q, vT[:, 48 + h:80:MH], start=True, stop=True)
                    pe.matmul(ps(4)[0:NS, NS * h:NS * h + NS], k, q, start=True, stop=True)
                    sel = const("sel", MH)[:, P * h:P * h + P]
                    pe.matmul(ps(4)[0:NS, P + NS * h:P + NS * h + NS], sel[:, 0:NS], negM[:, s0:T], start=True, stop=True)
                    mm = pe.matmul(ps(4)[:, 2 * P + DB * h:2 * P + DB * h + DB], sel,
                                   winter.rearrange("p (b t) -> p b t", b=DB)[:, :, 3], start=True, stop=True)
                mm.then_inc(s_s_small, 1)
                pe.wait_ge(s_cq_copied, 1)
                for h in range(MH):
                    mm = pe.transpose(ps(5)[0:NS, P * h:P * h + P], cqs[:, NS * h:NS * h + NS], ident)
                mm.then_inc(s_cq_turned, 1)
                pe.wait_ge(s_s_sd, 1)
                pe.wait_ge(s_ktok_copied, 5)
                pe.wait_ge(s_ones_set, 1)
                for h in range(MH):
                    mm = pe.matmul(ps(2, 2)[0:NS, 256 * h:256 * h + P + 1], sds[:, h, :], mv[0:NS, 4, h, :], start=True, stop=True)
                mm.then_inc(s_s_num, 1)
                pe.wait_ge(s_s_num_read, 1)
                pe.matmul(ps(5)[0:DB, :], const("blk", NS), kw[0:NS, 4, :, :].rearrange("p h d -> p (h d)"), start=True, stop=True)\
                  .then_inc(s_n_sum, 1)

                def update_memories(h):
                    pe.wait_ge(s_kmask_ready, h + 1)
                    if h >= 1:
                        pe.wait_ge(s_c_new, h)
                    for hf in range(2):
                        mm = pe.matmul(ps(6 + hf), mv[0:NS, 4, h, 0:P], kmask[:, 512 * hf:512 * hf + 512], start=True, stop=True)
                    mm.then_inc(s_u_sum, 1)

                def mem_score(n):
                    h, s = n // 4, n % 4
                    if s == 0:
                        if h >= 2:
                            pe.wait_ge(s_dtmp_ready, 4 * (h - 1))
                        pe.matmul(ps(h % 2), const("sel", MH)[:, P * h:P * h + P], negM[:, 0:SEQ], start=True, stop=True).then_inc(s_negm_bc, 1)
                    if n >= 2:
                        pe.wait_ge(s_sd, n - 1)
                    pe.matmul(ps(2 + n % 2)[:, 0:SEQ - P * s], cqv[:, MH + h, P * s:P * s + P], cqv[:, h, P * s:SEQ],
                              start=True, stop=True).then_inc(s_mem_s, 1)

                mem_score(0)
                mem_score(1)
                for h in range(MH):
                    for n in range(4 * h + 2, min(4 * h + 6, 4 * MH)):
                        mem_score(n)
                    update_memories(h)
                    pe.wait_ge(s_sd_masked, 4 * (h + 1))
                    if h == 0:
                        pe.wait_ge(s_n_new, 1)
                    else:
                        pe.wait_ge(s_num_read, h)
                    for t in range(4):
                        for s in range(t + 1):
                            mm = pe.matmul(ps(4, 2)[:, 256 * t:256 * t + P + 1], sd[h % 2][:, s, P * t:P * t + P],
                                           mv[:, s, h, :], start=(s == 0), stop=(s == t))
                    mm.then_inc(s_num, 1)
                pe.wait_ge(s_sd, 4 * MH)
                for h in range(MH):
                    for s in range(4):
                        pe.matmul(ps(2)[:, P * h:P * h + P], mv[:, s, h, 0:P], kw[:, s, h, :], start=(s == 0), stop=(s == 3))
                for s in range(4):
                    mm = pe.matmul(ps(3)[0:1, :], ones[:, 0:1], kw[:, s, :, :].rearrange("p h d -> p (h d)"), start=(s == 0), stop=(s == 3))
                mm.then_inc(s_c_sum, 1)

                def turn_pair(g):
                    if g >= 2:
                        pe.wait_ge(s_qt_copied, g - 1)
                    for t in range(4):
                        src = qk[:, t, 2 * g:2 * g + 2, :] if g < 4 else k_twice[:, t, g - 4, :, :]
                        mm = pe.transpose(ps(4 + g % 2)[:, P * t:P * t + P], src.rearrange("p h d -> p (h d)"), ident)
                    mm.then_inc(s_qt_turned, 1)

                pe.wait_ge(s_num_read, MH)
                pe.wait_ge(s_c_new, MH)
                for i in range(4):
                    pe.transpose(ps(6)[:, NS * i:NS * i + NS], qk[0:NS, 4, 2 * i:2 * i + 2, :].rearrange("p h d -> p (h d)"), ident[0:NS, 0:NS])
                for p in range(2):
                    mm = pe.transpose(ps(7)[:, NS * p:NS * p + NS], qk[0:NS, 4, 8 + 2 * p:10 + 2 * p, :].rearrange("p h d -> p (h d)"), ident[0:NS, 0:NS])
                mm.then_inc(s_s_turned, 1)
                for g in range(4):
                    turn_pair(g)
                pe.wait_ge(s_c_copied, 1)
                for h in range(MH):
                    pe.wait_ge(s_hn_ready, h + 1)
                    if h >= 2:
                        pe.wait_ge(s_mix_copied, h - 1)
                    for t, (c, r) in enumerate(TILES):
                        mm = pe.transpose(ps(2 * (h % 2), 2)[:, c:c + r], htok[0:r, t, h, :], ident[0:r, 0:r])
                    mm.then_inc(s_mix_turned, 1)
                pe.wait_ge(s_k_twice_ready, 1)
                for g in range(4, 8):
                    turn_pair(g)
                pe.wait_ge(s_qt_copied, 8)
                pe.wait_ge(s_mix_copied, MH)
                pe.wait_ge(s_s_q_ready, 1)

                def turn_out(j):
                    pe.wait_ge(s_a_tok, j + 1)
                    if j >= 1:
                        pe.wait_ge(s_a_copied, j)
                    for f in range(4):
                        mm = pe.transpose(ps(6)[:, P * f:P * f + P], atok[:, P * f:P * f + P], ident)
                    mm.then_inc(s_a_turned, 1)

                for n in range(4 * QH + 2):
                    if n < 4 * QH:
                        j, h = n // QH, n % QH
                        q0 = HD * (h % 2)
                        if n >= 2:
                            pe.wait_ge(s_a_max, n - 1)
                        pe.matmul(ps(n % 2)[:, 0:(j + 1) * P], qT[q0:q0 + HD, h // 2, P * j:P * j + P],
                                  kT2[q0:q0 + HD, h // 2, 0:(j + 1) * P], start=True, stop=True).then_inc(s_a_s, 1)
                    if 1 <= n <= 4 * QH:
                        m = n - 1
                        pe.wait_ge(s_a_p, m + 1)
                        if m >= 2:
                            pe.wait_ge(s_pt_copied, m - 1)
                        for s in range(m // QH + 1):
                            mm = pe.transpose(ps(2 + m % 2)[:, P * s:P * s + P], a_score[:, m % 3, P * s:P * s + P], ident)
                        mm.then_inc(s_pt_turned, 1)
                    if n >= 2:
                        m = n - 2
                        j, h = m // QH, m % QH
                        pe.wait_ge(s_pt_copied, m + 1)
                        if h == 0 and j >= 2:
                            pe.wait_ge(s_a_tok, j - 1)
                        for s in range(j + 1):
                            mm = pe.matmul(ps(4 + j % 2)[:, HD * h:HD * h + HD], a_pt[:, m % 2, P * s:P * s + P],
                                           va[:, s, HD * (h // 2):HD * (h // 2) + HD], start=(s == 0), stop=(s == j))
                        mm.then_inc(s_pv, 1)
                        if h == 4 and j >= 1:
                            turn_out(j - 1)
                turn_out(3)

                def turn_keys(b):
                    pe.wait_ge(k_in[b], 16 * PAGES)
                    if b == 6:
                        pe.wait_ge(s_s_ptc, 1)
                    for i in range(4):
                        if 4 * b + i >= 2:
                            pe.wait_ge(s_kt_copied, 4 * b + i - 1)
                        for q in range(4):
                            pg = 4 * (i % 2) + q
                            mm = pe.transpose(ps(5 + i % 2)[:, P * q:P * q + P], k_pages(b)[:, pg, P * (i // 2):P * (i // 2) + P], ident)
                        mm.then_inc(s_kt_turned, 1)

                def sample_logits(b):
                    pe.wait_ge(s_kt_copied, 4 * b + 4)
                    g, r0 = b // 4, NS * (b % 4)
                    for dst, keys in logit_parts(g, kTb[b % 2])[0:2]:
                        for p in range(2):
                            mm = pe.matmul(dst[r0:r0 + NS, :], s_q[:, p, b, :], keys[:, p, :], start=(p == 0), stop=False,
                                           skip_group_check=True)
                    mm.then_inc(s_s_log, 1)

                def finish_logits(g):
                    new = logit_parts(g, kTb[0])[2][0]
                    for b in range(4 * g, 4 * g + 4):
                        for p in range(2):
                            pe.matmul(new[NS * (b % 4):NS * (b % 4) + NS, :], s_q[:, p, b, :], kTnew[:, p, :], start=(p == 0), stop=False,
                                      skip_group_check=True)
                    pe.wait_ge(s_sample_mask, 1)
                    for (dst, _), (c, w) in zip(logit_parts(g, kTb[0]), ((0, 512), (512, 512), (PAST, NS))):
                        mm = pe.matmul(dst, const("rep", NS)[:, P * g:P * g + P], pen_s[:, c:c + w], start=False, stop=True,
                                       skip_group_check=True)
                    mm.then_inc(s_s_logits, 1)

                def turn_probs(g):
                    pe.wait_ge(s_s_exp, g + 1)
                    pe.wait_ge(s_kt_copied, 24 if g == 0 else 32)
                    for i in range(8):
                        pe.transpose(ps(5, 2)[:, P * i:P * i + P], s_prob[:, NS * g + P * i:NS * g + P * i + P], ident)
                    new = PAST * (1 - g)
                    pe.transpose(ps(2)[0:NS, P:2 * P], s_prob[:, new:new + NS], ident).then_inc(s_s_pt, 1)

                def sample_values(b):
                    g, r0 = b // 4, NS * (b % 4)
                    pe.wait_ge(s_s_ptc, g + 1)
                    pe.wait_ge(v_in[b], 16 * PAGES)
                    out = s_value[g][r0:r0 + NS, :]
                    for pg in range(PAGES):
                        pe.matmul(out, s_pt[g][:, pg, r0:r0 + NS], v_pages(b)[:, pg, :], start=(pg == 0), stop=False)
                    pe.matmul(out, s_pt[g][0:NS, 8, r0:r0 + NS], va[0:NS, 4, :], start=False, stop=True).then_inc(s_s_pv, 1)

                pe.wait_ge(s_a_copied, 4)
                turn_keys(0)
                for b in range(5):
                    turn_keys(b + 1)
                    sample_logits(b)
                    if b == 3:
                        finish_logits(0)
                turn_probs(0)
                sample_logits(5)
                turn_keys(6)
                turn_keys(7)
                sample_logits(6)
                sample_logits(7)
                finish_logits(1)
                for b in range(DB):
                    if b == 4:
                        turn_probs(1)
                    sample_values(b)
                for g in range(2):
                    pe.wait_ge(s_s_rows_ready, g + 1)
                    for p in range(2):
                        mm = pe.transpose(ps(1)[:, P * (2 * g + p):P * (2 * g + p) + P], s_rows[g][:, P * p:P * p + P], ident)
                mm.then_inc(s_s_rows_turned, 1)

                pe.wait_ge(s_mix_ready, 1)
                for m in range(8):
                    feature_tile(8 + m // 4, OUT0 + m, P * (m % 4), mixv)
                    if m >= 2:
                        sum_squares(s_sq2, m - 2)
                sum_squares(s_sq2, KT - 2)
                sum_squares(s_sq2, KT - 1).then_inc(s_sum2, 1)
                for f in range(FT):
                    split_tile(f, 0)
                    split_tile(f, 1)
                pe.wait_ge(s_up_free, FT)
                feature_tile(10 + FT // 2, DOWN0, 0, hid)
                for m in range(1, KT):
                    down_tile(m)
        def vector_layer(block, l):
            @block.vector
            def _(dve):
                chain = [0]

                def step(ins):
                    chain[0] += 1
                    ins.then_inc(s_dve_chain, 1)
                    dve.wait_ge(s_dve_chain, chain[0])

                def spread(ap, shape, at):
                    return ap.unsqueeze(at).broadcast_to(shape)

                dve.wait_ge(s_conv_state_turned, 1)
                dve.tensor_copy(convst[:, :], ps(7)[:, 0:192])
                dve.tensor_copy(vT[:, :], ps(6)[:, 0:80]).then_inc(s_vec_copied, 1)
                dve.wait_ge(s_vec_copied, 1)

                def apply_norm(rstd, g0, ready):
                    for k in range(KT):
                        ins = dve.scalar_tensor_tensor(out=xnv[:, k, :], in0=xv[:, k, :], scalar=vT[:, g0 + k:g0 + k + 1],
                                                       in1=rstd, op0=ALU.mult, op1=ALU.mult)
                        ins.then_inc(ready, 1)

                rstd = R4[:, 0:T]
                dve.wait_ge(s_rstd1, 1)
                apply_norm(rstd, 32, s_xn_ready)

                dve.wait_ge(s_out_free, 1)
                dve.tensor_copy(qi[:, 0:4, 8, :], g80[:, 0:4, 8:72])
                dve.tensor_copy(qi[0:NS, 4, 8, :], g80[0:NS, 4, 8:72])
                dve.tensor_scalar(wP, g80[:, 0:4, 72:80], IH ** -0.5, None, ALU.mult)
                step(dve.tensor_scalar(g80[0:NS, 4, 72:80], g80[0:NS, 4, 72:80], IH ** -0.5, None, ALU.mult))
                dve.tensor_tensor(wx.rearrange("p (b h t) -> p b h t", b=DB, h=IH),
                                  const("rep", NS).rearrange("p (b h t) -> p b h t", b=DB, h=IH),
                                  g80[0:NS, 4, 72:80].unsqueeze(1).unsqueeze(3).broadcast_to([NS, DB, IH, DT]),
                                  ALU.mult).then_inc(s_w_spread, 1)

                def rope(buf, h0, nh, tmp):
                    for tiles, r in ((slice(0, 4), P), (slice(4, 5), NS)):
                        nt = 4 if r == P else 1
                        a = buf[0:r, tiles, h0:h0 + nh, 0:32]
                        b = buf[0:r, tiles, h0:h0 + nh, 32:64]
                        cos, sin = (const(n, r).rearrange("p (t d) -> p t d", t=5)[:, tiles, :].unsqueeze(2).broadcast_to([r, nt, nh, 32])
                                    for n in ("cos", "sin"))
                        n = nt * nh * 32
                        as_, bs = (tmp[0:r, i * n:(i + 1) * n].rearrange("p (t h d) -> p t h d", t=nt, h=nh) for i in range(2))
                        dve.tensor_tensor(as_, a, sin, ALU.mult)
                        step(dve.tensor_tensor(bs, b, sin, ALU.mult))
                        dve.tensor_tensor(a, a, cos, ALU.mult)
                        step(dve.tensor_tensor(b, b, cos, ALU.mult))
                        dve.tensor_tensor(a, a, bs, ALU.subtract)
                        ins = dve.tensor_tensor(b, b, as_, ALU.add)
                        if r == P:
                            step(ins)
                    return ins

                dve.wait_ge(s_out_free, 4)
                step(rope(qi, 0, 9, R4))
                dve.tensor_copy(qi[:, 0:4, 9, :], qi[:, 0:4, 8, :]).then_inc(s_qi_roped, 1)

                dve.wait_ge(s_gate_turned, 1)
                dve.wait_ge(s_gate_in, 16 * 4)
                dve.tensor_scalar(gr[:, 0, :], ps(4, 2)[0:MH, 0:T], bgate[:, 0:1], None, ALU.add)
                dve.tensor_scalar(gr[:, 1, :], ps(6, 2)[0:MH, 0:T], bgate[:, 1:2], None, ALU.add).then_inc(s_gate_read, 1)
                dve.wait_ge(s_gate_read, 1)
                dve.wait_ge(s_gate_log, 1)
                step(dve.scalar_tensor_tensor(out=gr[:, 1, :], in0=gr[:, 1, :], scalar=0.0, in1=gr[:, 2, :],
                                              op0=ALU.min, op1=ALU.subtract))
                step(dve.tensor_tensor_scan(gr[:, 2, :], rm, gr[:, 1, :], 0.0, ALU.mult, ALU.add))
                step(dve.tensor_tensor(gr[:, 0, :], gr[:, 0, :], gr[:, 2, :], ALU.subtract))
                step(dve.tensor_copy(gr[:, 1, :], gr[:, 0, :]))

                def seqs(row):
                    return row[:, SEQ:T].rearrange("p (b t) -> p b t", b=DB)

                first = seqs(gr[:, 1, :])[:, :, 0]
                step(dve.tensor_tensor(first, first, m0T, ALU.max))
                step(dve.tensor_tensor_scan(gr[:, 3, :], ra, gr[:, 1, :], 0.0, ALU.add, ALU.max))
                dve.tensor_tensor(gr[:, 6, :], gr[:, 2, :], gr[:, 3, :], ALU.add)
                step(dve.tensor_scalar(negM[:, :], gr[:, 3, :], -1.0, None, ALU.mult))
                dve.tensor_copy(mrow[:, 0:1], gr[:, 6, SEQ - 1:SEQ])
                dve.tensor_copy(mrow[:, 1:9], seqs(gr[:, 6, :])[:, :, 3])
                dve.tensor_tensor(winter.rearrange("p (b t) -> p b t", b=DB), seqs(negM[:, :]),
                                  m0T.unsqueeze(2).broadcast_to([MH, DB, DT]), ALU.add)
                dve.tensor_tensor(seqs(gr[:, 5, :]), seqs(gr[:, 0, :]),
                                  seqs(negM[:, :])[:, :, 3].unsqueeze(2).broadcast_to([MH, DB, DT]), ALU.add).then_inc(s_gate_rows_ready, 1)
                dve.wait_ge(s_gate_cols_turned, 1)
                dve.tensor_copy(gcols[:, 0:48], ps(6)[:, 0:48])
                dve.tensor_copy(gcols[0:NS, 48:64], ps(6)[0:NS, 48:64])
                dve.tensor_copy(decT, ps(6)[0:DB, 64:68]).then_inc(s_gate_cols_ready, 1)

                for n in range(3 * IH):
                    j, h = n // IH + 1, n % IH
                    dve.wait_ge(s_relu_done, n + 1)
                    acc = penv[:, j - 1, 0:(j + 1) * P]
                    part = relu_p[:, n % 2, 0:(j + 1) * P]
                    if h == 0:
                        ins = dve.tensor_scalar(acc, part, wP[:, j, h:h + 1], None, ALU.mult)
                    else:
                        ins = dve.scalar_tensor_tensor(out=acc, in0=part, scalar=wP[:, j, h:h + 1], in1=acc, op0=ALU.mult, op1=ALU.add)
                    ins.then_inc(s_relu_free, 1)
                    dve.wait_ge(s_relu_free, n + 1)

                def pick(scores, rows, topk):
                    for _ in range(topk // 8):
                        step(dve.max(m8[0:rows, :], scores))
                        step(dve.match_replace(scores, m8[0:rows, :], scores, GONE))
                    step(dve.tensor_scalar(scores, scores, GONE / 2, NEG, ALU.is_gt, ALU.mult))

                for j in (1, 2, 3):
                    dve.wait_ge(s_masked, j)
                    pick(penv[:, j - 1, 0:(j + 1) * P], P, TOPK_P)

                dve.wait_ge(s_out_free, 10)
                dve.wait_ge(s_g_in, 16 * 3)
                for t, (_, r) in enumerate(TILES):
                    sq = rawr[0:r, 0:768].rearrange("p (h d) -> p h d", h=12)
                    step(dve.tensor_tensor(sq, qk[0:r, t, :, :], qk[0:r, t, :, :], ALU.mult))
                    ins = dve.tensor_reduce(small_ss[0:r, t, :], sq, AX.X, ALU.add)
                    if r == P:
                        step(ins)
                ins.then_inc(s_qk_sums, 1)
                dve.wait_ge(s_qk_rstd, 1)
                for t, (_, r) in enumerate(TILES):
                    step(dve.tensor_tensor(qk[0:r, t, :, :], qk[0:r, t, :, :],
                                           small_ss[0:r, t, :].unsqueeze(2).broadcast_to([r, 12, HD]), ALU.mult))
                    dve.tensor_tensor(qk[0:r, t, 0:8, :], qk[0:r, t, 0:8, :],
                                      gqk[0:r, 0:HD].unsqueeze(1).broadcast_to([r, 8, HD]), ALU.mult)
                    step(dve.tensor_tensor(qk[0:r, t, 8:12, :], qk[0:r, t, 8:12, :],
                                           gqk[0:r, HD:2 * HD].unsqueeze(1).broadcast_to([r, 4, HD]), ALU.mult))
                for h0 in (0, 4):
                    step(rope(qk, h0, 4, rawr))
                rope(qk, 8, 4, rawr).then_inc(s_qk_ready, 1)

                dve.wait_ge(s_sscore, 1)
                dve.tensor_copy(pen_s[:, 0:PAST], ps(4, 2)[0:NS, :])
                dve.tensor_tensor(pen_s[:, PAST:KEYS], ps(7)[0:NS, 0:NS], const("newpen", NS), ALU.add).then_inc(s_sscore_copied, 1)
                dve.wait_ge(s_sscore_copied, 1)

                def pick_sample():
                    step(dve.max(m8[0:NS, :], pen_s[:, :]))
                    step(dve.match_replace(pen_s[:, :], m8[0:NS, :], pen_s[:, :], GONE))

                for m in range(8):
                    r_ = raw[m]
                    hist = r_[:, 3 + SEQ:571].rearrange("p (b c) -> p b c", b=DB)
                    step(dve.tensor_copy(hist[:, :, 0:3], convst[:, 24 * m:24 * m + 24].rearrange("p (b j) -> p b j", b=DB)))
                    dve.wait_ge(s_out_free, CONV0 + m + 1)
                    if m == 0:
                        dve.wait_ge(s_raw_zeroed, 1)
                    for j in range(4):
                        w = vT[:, 8 * j + m:8 * j + m + 1]
                        for out, src in ((cqv[:, m, 0:SEQ], r_[:, j:j + SEQ]), (seqs(cqv[:, m, :]), hist[:, :, j:j + DT])):
                            if j == 0:
                                ins = dve.tensor_scalar(out, src, w, None, ALU.mult)
                            else:
                                ins = dve.scalar_tensor_tensor(out=out, in0=src, scalar=w, in1=out, op0=ALU.mult, op1=ALU.add)
                        if j < 3:
                            step(ins)
                    ins.then_inc(s_conv_z, 1)
                    dve.tensor_copy(tails[:, 27 * m:27 * m + 3], r_[:, SEQ:SEQ + 3])
                    dve.tensor_copy(tails[:, 27 * m + 3:27 * m + 27].rearrange("p (b j) -> p b j", b=DB), hist[:, :, 4:7]).then_inc(s_conv_done, 1)
                    if m < PICKS_CONV:
                        pick_sample()

                def columns(t, rows, q):
                    return acol[0:rows, t, q, :]

                for t, (_, r) in enumerate(TILES):
                    dve.wait_ge(s_ktok_turned, t + 1)
                    if t == 0:
                        dve.wait_ge(s_out_done, OUT0)
                    dve.tensor_tensor(kw[0:r, t, :, :], ps(2 + t % 2)[0:r, :].rearrange("p (h d) -> p h d", h=MH),
                                      columns(t, r, 2).unsqueeze(2).broadcast_to([r, MH, P]), ALU.mult).then_inc(s_ktok_copied, 1)
                dve.wait_ge(s_s_small, 1)
                for h in range(MH):
                    ins = dve.tensor_scalar(sds[:, h, :], ps(4)[0:NS, P + NS * h:P + NS * h + NS], acol[0:NS, 4, 0, h:h + 1], 0.0, ALU.add, ALU.min)
                ins.then_inc(s_s_dt, 1)
                dve.tensor_copy(dec_bc, ps(4)[:, 2 * P:2 * P + NS]).then_inc(s_dec_copied, 1)
                dve.wait_ge(s_cq_done, 8)
                dve.tensor_copy(cqs, ps(6)[:, 0:P]).then_inc(s_cq_copied, 1)
                dve.wait_ge(s_s_de, 1)
                step(dve.tensor_tensor(sds, sds, ps(4)[0:NS, 0:P].rearrange("p (h t) -> p h t", h=MH), ALU.mult))
                dve.tensor_tensor(sds, sds, const("bcm", NS).unsqueeze(1).broadcast_to([NS, MH, NS]), ALU.mult).then_inc(s_s_sd, 1)
                wi = gcols[0:NS, 60:64]
                nqm = R4[0:NS, 0:NS].rearrange("p (h b) -> p h b", h=MH)
                step(dve.tensor_tensor(nqm, ps(7)[0:NS, 0:NS].rearrange("p (h b) -> p h b", h=MH),
                                       const("blk", NS).unsqueeze(1).broadcast_to([NS, MH, DB]), ALU.mult))
                step(dve.tensor_reduce(den[0:NS, 4, :], nqm, AX.X, ALU.add))
                step(dve.tensor_tensor(den[0:NS, 4, :], den[0:NS, 4, :], wi, ALU.mult))
                dve.wait_ge(s_cq_turned, 1)
                dve.wait_ge(s_kv_stored, 16 * 8)
                step(dve.tensor_tensor(htok[0:NS, 4, :, :], ps(5)[0:NS, :].rearrange("p (h d) -> p h d", h=MH),
                                       wi.unsqueeze(2).broadcast_to([NS, MH, P]), ALU.mult))
                dve.wait_ge(s_s_num, 1)
                num_s = ps(2, 2)[0:NS, :].rearrange("p (h c) -> p h c", h=MH)
                step(dve.tensor_tensor(den[0:NS, 4, :], den[0:NS, 4, :], num_s[:, :, P], ALU.add))
                dve.tensor_tensor(htok[0:NS, 4, :, :], htok[0:NS, 4, :, :], num_s[:, :, 0:P], ALU.add).then_inc(s_s_num_read, 1)
                dve.wait_ge(s_n0_in, 16)
                nr = nrow.rearrange("p (h d) -> p h d", h=MH)
                step(dve.tensor_tensor(nr, nr, decT.unsqueeze(2).broadcast_to([DB, MH, P]), ALU.mult))
                dve.wait_ge(s_n_sum, 1)
                dve.tensor_tensor(nr, nr, ps(5)[0:DB, :].rearrange("p (h d) -> p h d", h=MH), ALU.add).then_inc(s_n_new, 1)

                def add_memories(h):
                    dve.wait_ge(s_c_decayed, h + 1)
                    dve.wait_ge(s_u_sum, h + 1)
                    dve.tensor_tensor(c0[:, :, h, :], c0[:, :, h, :], ps(6, 2).rearrange("p (b d) -> p b d", b=DB), ALU.add).then_inc(s_c_new, 1)

                def decays(n):
                    h, s = n // 4, n % 4
                    dve.wait_ge(s_negm_bc, h + 1)
                    if n >= 2:
                        dve.wait_ge(s_sd, n - 1)
                    dve.tensor_scalar(dtmp[:, n % 2, P * s:SEQ], ps(h % 2)[:, P * s:SEQ], acol[:, s, 0, h:h + 1], 0.0,
                                      ALU.add, ALU.min).then_inc(s_dtmp_ready, 1)

                def values(h):
                    dve.wait_ge(s_num, h + 1)
                    out = ps(4, 2).rearrange("p (t c) -> p t c", t=4)
                    d, nq = den[:, 0:4, h], out[:, :, P]
                    step(dve.tensor_copy(d, nq))
                    step(dve.scalar_tensor_tensor(out=d, in0=d, scalar=-1.0, in1=nq, op0=ALU.mult, op1=ALU.max))
                    step(dve.tensor_tensor(d, d, acol[:, 0:4, 1, h], ALU.max))
                    step(dve.reciprocal(d, d))
                    dve.tensor_tensor(htok[:, 0:4, h, :], out[:, :, 0:P], d.unsqueeze(2).broadcast_to([P, 4, P]), ALU.mult).then_inc(s_num_read, 1)

                decays(0)
                for n in range(4 * MH):
                    h, s = n // 4, n % 4
                    if n + 1 < 4 * MH:
                        decays(n + 1)
                    dve.wait_ge(s_dexp, n + 1)
                    dve.wait_ge(s_mem_s, n + 1)
                    if s == 0 and h >= 2:
                        dve.wait_ge(s_num, h - 1)
                    dve.tensor_tensor(sd[h % 2][:, s, P * s:SEQ], dtmp[:, n % 2, P * s:SEQ], ps(2 + n % 2)[:, 0:SEQ - P * s], ALU.mult).then_inc(s_sd, 1)
                    if s == 1 and h >= 1:
                        values(h - 1)
                    if s == 2 and h >= 1:
                        add_memories(h - 1)
                values(MH - 1)
                add_memories(MH - 1)
                d = den[0:NS, 4, :]
                neg = small[0:NS, 356:360]
                step(dve.tensor_scalar(neg, d, -1.0, None, ALU.mult))
                step(dve.tensor_tensor(d, d, neg, ALU.max))
                step(dve.tensor_tensor(d, d, columns(4, NS, 1), ALU.max))
                step(dve.reciprocal(d, d))
                dve.tensor_tensor(htok[0:NS, 4, :, :], htok[0:NS, 4, :, :], d.unsqueeze(2).broadcast_to([NS, MH, P]), ALU.mult).then_inc(s_num_read, 1)
                dve.wait_ge(s_s_turned, 1)
                dve.wait_ge(s_s_q_zeroed, 1)
                for h in range(QH):
                    r0, src, p = HD * (h // 2 % 2), HD * (h % 2), h // 4
                    dve.tensor_copy(s_q[r0:r0 + HD, p, :, DT * h:DT * h + DT],
                                    ps(6)[src:src + HD, NS * (h // 2):NS * (h // 2) + NS].rearrange("p (b t) -> p b t", b=DB))
                dve.tensor_copy(kTnew.rearrange("p g s -> p (g s)"), ps(7)[:, 0:2 * NS]).then_inc(s_s_q_ready, 1)
                dve.wait_ge(s_mo_scaled, 1)
                dve.wait_ge(s_hrstd, 1)
                step(dve.tensor_tensor(htok[0:NS, 4, :, :], htok[0:NS, 4, :, :], hss[0:NS, 4, :].unsqueeze(2).broadcast_to([NS, MH, P]), ALU.mult))
                dve.tensor_tensor(htok[0:NS, 4, :, :], htok[0:NS, 4, :, :], mo[0:NS, 4, :].rearrange("p (h d) -> p h d", h=MH), ALU.mult)
                for h in range(MH):
                    v = htok[:, 0:4, h, :]
                    step(dve.tensor_tensor(v, v, hss[:, 0:4, h].unsqueeze(2).broadcast_to([P, 4, P]), ALU.mult))
                    dve.tensor_tensor(v, v, mo[:, 0:4, P * h:P * h + P], ALU.mult).then_inc(s_hn_ready, 1)

                dve.wait_ge(s_c_copied, 1)
                dve.wait_ge(s_stored, 16 * STORES)
                for i in range(2):
                    ins = dve.tensor_copy(k_twice[:, :, :, i, :], qk[:, 0:4, 8:12, :])
                ins.then_inc(s_k_twice_ready, 1)
                dve.wait_ge(s_mix_turned, MH)

                def copy_out(j):
                    dve.wait_ge(s_a_turned, j + 1)
                    dve.tensor_copy(mixv[:, 4:8, P * j:P * j + P], ps(6).rearrange("p (f t) -> p f t", f=4)).then_inc(s_a_copied, 1)

                for n in range(4 * QH + 1):
                    if n < 4 * QH:
                        j, h = n // QH, n % QH
                        w = (j + 1) * P
                        dve.wait_ge(s_a_s, n + 1)
                        if n >= 3:
                            dve.wait_ge(s_pt_turned, n - 2)
                        mask = const("pen0") if j == 0 else penv[:, j - 1, 0:w]
                        step(dve.tensor_tensor_reduce(a_score[:, n % 3, 0:w], ps(n % 2)[:, 0:w], mask, 1.0, GONE, ALU.add, ALU.max,
                                                      a_neg[:, 4 + n % 4:5 + n % 4]))
                        dve.tensor_scalar(a_neg[:, n % 4:n % 4 + 1], a_neg[:, 4 + n % 4:5 + n % 4], -HD ** -0.5, None, ALU.mult)\
                           .then_inc(s_a_max, 1)
                    if 4 * QH - PICKS_PROMPT <= n < 4 * QH:
                        pick_sample()
                    if n >= QH and n % QH == 2 or n == 4 * QH:
                        j = n // QH - 1
                        dve.wait_ge(s_pv, QH * (j + 1))
                        dve.wait_ge(s_a_p, QH * (j + 1))
                        step(dve.reciprocal(a_sum[:, j % 2, :], a_sum[:, j % 2, :]))
                        if j >= 1:
                            dve.wait_ge(s_a_turned, j)
                        dve.tensor_tensor(atok.rearrange("p (h d) -> p h d", h=QH), ps(4 + j % 2).rearrange("p (h d) -> p h d", h=QH),
                                          a_sum[:, j % 2, :].unsqueeze(2).broadcast_to([P, QH, HD]), ALU.mult).then_inc(s_a_tok, 1)
                        if j >= 1:
                            copy_out(j - 1)
                copy_out(3)
                for _ in range(TOPK_S // 8 - PICKS_CONV - PICKS_PROMPT):
                    pick_sample()
                dve.tensor_scalar(pen_s[:, :], pen_s[:, :], GONE / 2, NEG, ALU.is_gt, ALU.mult).then_inc(s_sample_mask, 1)
                for g in range(2):
                    dve.wait_ge(s_s_logits, g + 1)
                    step(dve.tensor_reduce(s_stat[:, 4:5], s_logit[g], AX.X, ALU.max))
                    dve.tensor_scalar(s_stat[:, g:g + 1], s_stat[:, 4:5], -HD ** -0.5, None, ALU.mult).then_inc(s_s_neg, 1)
                for g in range(2):
                    dve.wait_ge(s_s_exp, g + 1)
                    step(dve.reciprocal(s_stat[:, 2 + g:3 + g], s_stat[:, 2 + g:3 + g]))
                    dve.wait_ge(s_s_pv, 4 * g + 4)
                    dve.tensor_scalar(s_rows[g], s_value[g], s_stat[:, 2 + g:3 + g], None, ALU.mult).then_inc(s_s_rows_ready, 1)
                dve.wait_ge(s_s_rows_turned, 1)
                for h in range(QH):
                    p, src, dst = h // 4, HD * (h // 2 % 2), HD * (h % 2)
                    ins = dve.tensor_copy(mixv[dst:dst + HD, 4 + h // 2, SEQ:T].rearrange("p (g b t) -> p g b t", g=2, b=4),
                                          ps(1)[src:src + HD, :].rearrange("p (g q b c) -> p g q b c", g=2, q=2, b=4)[:, :, p, :, DT * h:DT * h + DT])
                ins.then_inc(s_mix_ready, 1)

                def halves(n):
                    dve.wait_ge(s_out_done, n + 1)
                    return ps(2 * (n % 2), 2).rearrange("p (h t) -> p h t", h=2)[:, :, 0:HALF]

                def split(whole, high, low):
                    step(dve.tensor_copy(high, whole))
                    return dve.tensor_tensor(low, whole, high.bitcast(F32), ALU.subtract)

                def split_weights(f):
                    i = 10 + f // 2
                    if f % 2 == 0:
                        slab_arrived(dve, i)
                    whole = slab_view(i).rearrange("p k (u c) -> p k u c", u=2)[:, :, :, P * (f % 2):P * (f % 2) + P]
                    for k in (slice(0, 4), slice(4, 8)):
                        split(whole[:, k], w_part(f, 0)[:, k], w_part(f, 1)[:, k]).then_inc(s_w_split, 1)

                for m in range(KT):
                    v = xv[:, m, :].rearrange("p (h t) -> p h t", h=2)
                    dve.tensor_tensor(v, v, halves(OUT0 + m), ALU.add).then_inc(s_out_free, 1)
                split_weights(0)
                dve.wait_ge(s_out_free, OUT0 + KT)
                dve.wait_ge(s_rstd2, 1)
                for k in range(KT):
                    step(dve.scalar_tensor_tensor(out=cqv[:, k, :], in0=xv[:, k, :], scalar=vT[:, 40 + k:41 + k], in1=rstd_ffn,
                                                  op0=ALU.mult, op1=ALU.mult))
                    split(cqv[:, k, :], xh[:, k, :], xl[:, k, :]).then_inc(s_xn2_split, 1)
                for f in range(FT):
                    if f + 1 < FT:
                        split_weights(f + 1)
                    dve.wait_ge(s_gate_silu, f + 1)
                    dve.tensor_tensor(hid[:, f, :].rearrange("p (h t) -> p h t", h=2), sig(f), halves(FFN0 + 2 * f + 1), ALU.mult).then_inc(s_up_free, 1)
                dve.wait_ge(s_up_free, FT)

                def split_down(c):
                    i = 11 + FT // 2 + c // CHUNKS
                    if c % CHUNKS == 0:
                        slab_arrived(dve, i)
                    if c >= 8:
                        m, k = (c - 8) // CHUNKS, (c - 8) % CHUNKS
                        if k == CHUNKS - 1:
                            dve.wait_ge(s_out_done, DOWN0 + m + 2)
                        else:
                            dve.wait_ge(s_down_used, (CHUNKS - 1) * m + k + 1)
                    whole = slab_view(i)[:, 2 * (c % CHUNKS):2 * (c % CHUNKS) + 2, :].rearrange("p k n -> p (k n)")
                    split(whole, down_part(c, 0), down_part(c, 1)).then_inc(s_down_split, 1)

                def add_down(m):
                    v = xv[:, m, :].rearrange("p (h t) -> p h t", h=2)
                    dve.tensor_tensor(v, v, halves(DOWN0 + m), ALU.add).then_inc(s_out_free, 1)

                for f in range(FT):
                    dve.wait_ge(s_high_copied, f + 1)
                    dve.tensor_tensor(hid_low(f), hid[:, f, :], hid_low(f).bitcast(F32), ALU.subtract).then_inc(s_low_ready, 1)
                for c in range(8):
                    split_down(c)
                for c in range(8, CHUNKS * (KT - 1)):
                    if c % CHUNKS == 9:
                        add_down(c // CHUNKS)
                    split_down(c)
                add_down(KT - 1)
                dve.wait_ge(s_out_free, FFN0 + KT)
        xtok = proj[:, 0:5 * D].rearrange("p (t d) -> p t d", t=5)
        with nc.Block() as block:

            @block.sync
            def _(sp):
                sp.dma_start(con[:, :], A["consts"][:, :]).then_inc(s_const_in, 16)
                sp.dma_start(xtok[:, 0:4, :], A["x_prompt"][0, :, :].rearrange("(t p) d -> p t d", p=P)).then_inc(s_x_in, 16)
                sp.dma_start(xtok[0:NS, 4, :], A["x_sample"][:, :, :].rearrange("b t d -> (b t) d")).then_inc(s_x_in, 16)
                sp.dma_start(pages[:, :], A["page_table"][:, :].rearrange("(a b) g -> a (b g)", a=1)).then_inc(s_x_in, 16)

            @block.tensor
            def _(pe):
                pe.wait_ge(s_const_in, 16)
                pe.wait_ge(s_x_in, 48)
                for k in range(KT):
                    if k >= 4:
                        pe.wait_ge(s_x_copied, k - 3)
                    for t, (c, r) in enumerate(TILES):
                        mm = pe.transpose(ps(2 * (k % 4), 2)[:, c:c + r], xtok[0:r, t, P * k:P * k + P], ident[0:r, 0:r])
                    mm.then_inc(s_x_turned, 1)

            @block.vector
            def _(dve):
                dve.memset(eps[:, :], EPS)
                for k in range(KT):
                    dve.wait_ge(s_x_turned, k + 1)
                    dve.tensor_copy(xv[:, k, :], ps(2 * (k % 4), 2)[:, 0:T]).then_inc(s_x_copied, 1)
                dve.wait_ge(s_x_copied, KT)

        with nc.Fori(0, DEPTH) as l:
            with nc.Block() as layer:
                sync_layer(layer, l)
                pool_layer(layer, l)
                act_layer(layer, l)
                tensor_layer(layer, l)
                vector_layer(layer, l)
            nc.all_engine_barrier()
            clearers = (nc.sync, nc.scalar, nc.vector, nc.tensor, nc.gpsimd)
            for i, s in enumerate(layer_semaphores):
                clearers[i % len(clearers)].sem_clear(s)
            nc.all_engine_barrier()

        with nc.Block() as block:
            @block.tensor
            def _(pe):
                for t, (c, r) in enumerate(TILES):
                    if t >= 4:
                        pe.wait_ge(s_y_copied, t - 3)
                    for k in range(KT):
                        mm = pe.transpose(ps(2 * (t % 4), 2)[0:r, P * k:P * k + P], xv[:, k, c:c + r], ident)
                    mm.then_inc(s_y_turned, 1)

            @block.vector
            def _(dve):
                for t, (c, r) in enumerate(TILES):
                    dve.wait_ge(s_y_turned, t + 1)
                    dve.tensor_copy(xtok[0:r, t, :], ps(2 * (t % 4), 2)[0:r, :]).then_inc(s_y_copied, 1)

            @block.sync
            def _(sp):
                for t, (c, r) in enumerate(TILES):
                    sp.wait_ge(s_y_copied, t + 1)
                    dst = O["y_p"][0, c:c + r, :] if t < 4 else O["y_s"][:, :, :].rearrange("b t d -> (b t) d")
                    sp.dma_start(dst, xtok[0:r, t, :]).then_inc(s_y_stored, 16)
                sp.wait_ge(s_y_stored, 16 * 5)

_OUTS = [("y_p", (1, SEQ, D)), ("y_s", (DB, DT, D)),
         ("k_p", (DEPTH, 1, SEQ, KVH, HD)), ("v_p", (DEPTH, 1, SEQ, KVH, HD)), ("kidx_p", (DEPTH, 1, SEQ, HD)),
         ("C_p", (DEPTH, 1, MH, P, P)), ("n_p", (DEPTH, 1, MH, P)), ("m_p", (DEPTH, 1, MH)), ("conv_p", (DEPTH, 1, 3, 1024)),
         ("k_s", (DEPTH, DB, DT, KVH, HD)), ("v_s", (DEPTH, DB, DT, KVH, HD)), ("kidx_s", (DEPTH, DB, DT, HD)),
         ("C_s", (DEPTH, DB, MH, P, P)), ("n_s", (DEPTH, DB, MH, P)), ("m_s", (DEPTH, DB, MH)), ("conv_s", (DEPTH, DB, 3, 1024))]
_INS = ["x_prompt", "x_sample", "cache_k", "cache_v", "cache_kidx", "page_table", "state_C", "state_n", "state_m", "state_conv",
        "g_mix", "w_in", "conv_w", "b_gate", "g_mout", "g_q", "g_k", "w_out", "g_ffn", "w_gate_up", "w_down"]


def _constants():
    import numpy as np
    c = np.zeros((P, NCONST), np.float32)

    def put(name, value):
        a, n = CAT[name]
        c[:value.shape[0], a:a + n] = value.reshape(value.shape[0], n)

    put("ident", np.eye(P))
    put("ones", np.ones((P, P)))
    half = HD // 2
    inv = np.float32(10000.0) ** (-np.arange(half, dtype=np.float32) / np.float32(half))
    pos = np.concatenate([np.arange(SEQ), np.tile(PAST + np.arange(DT), DB), np.zeros(P - NS)]).astype(np.float32)
    ang = (pos[:, None] * inv[None, :]).astype(np.float32)
    tiles = ang.reshape(5, P, half).transpose(1, 0, 2)
    put("cos", np.cos(tiles))
    put("sin", np.sin(tiles))
    row = np.arange(NS)
    same = row[:, None] // DT == row[None, :] // DT
    put("bcm", (same & (row[:, None] <= row[None, :])).astype(np.float32))
    put("newpen", np.where(same & (row[None, :] <= row[:, None]), 0.0, NEG))
    put("blk", (row[:, None] // DT == np.arange(DB)[None, :]).astype(np.float32))
    wide = np.arange(2 * P)
    put("rep", ((wide[None, :] // NS == row[:, None] // DT) & (wide[None, :] % DT == row[:, None] % DT)).astype(np.float32))
    put("sel", (np.arange(MH)[:, None] == np.arange(MH * P)[None, :] // P).astype(np.float32))
    put("pen0", np.where(np.arange(P)[None, :] <= np.arange(P)[:, None], 0.0, NEG))
    rows = np.zeros((MH, 2 * T), np.float32)
    rows[:, 0:T] = 1.0
    rows[:, SEQ:T:DT] = 0.0
    rows[:, T + SEQ::DT] = GONE
    return c, rows


def kernel(**inputs):
    import numpy as np
    import concourse.bacc as bacc
    from concourse.bass_utils import run_bass_kernel_spmd

    nc = bacc.Bacc("TRN2", target_bir_lowering=False, num_devices=1)
    data = {n: np.ascontiguousarray(inputs[n]) for n in _INS}
    for n in ("cache_k", "cache_v"):
        data[n] = data[n].reshape(DEPTH * POOL, PAGE, KVH * HD)
    data["cache_kidx"] = data["cache_kidx"].reshape(DEPTH * POOL, PAGE, HD)
    data["consts"], data["gate_rows"] = _constants()
    arrays, A, O = {}, {}, {}
    for n, a in data.items():
        arrays[f"in_{n}_dram"] = a
        A[n] = nc.dram_tensor(f"in_{n}_dram", a.shape, mybir.dt.from_np(a.dtype), kind="ExternalInput").ap()
    for n, shape in _OUTS:
        O[n] = nc.dram_tensor(f"out_{n}_dram", shape, F32, kind="ExternalOutput").ap()
    build(nc, A, O)
    r = run_bass_kernel_spmd(nc, [arrays], core_ids=[0])
    return tuple(r.results[0][f"out_{n}_dram"] for n, _ in _OUTS)
```
